# Optimizing a Trainium2 kernel written in Bass

```python
import jax
import jax.numpy as jnp
from jax import lax
import numpy as np
import jax, jax.numpy as jnp

D_MODEL = 1024
BATCH = 1
SEQ = 512
DEPTH = 2

MLSTM_HEADS = 4
MLSTM_DH = 64
MLSTM_CHUNK = 64
CONV_K = 4
HGRN_HEADS = 4
HGRN_DK = 64
HGRN_DV = 64
HGRN_CHUNK = 32
SWA_Q_HEADS = 8
SWA_KV_HEADS = 2
SWA_DH = 64
WINDOW = 128
ROPE_THETA = 500000.0
ROT_DIM = SWA_DH // 4
D_FF = 4 * D_MODEL
PLE_DIM = 256
EPS = 1e-6

MLSTM_W = MLSTM_HEADS * MLSTM_DH
HGRN_KW = HGRN_HEADS * HGRN_DK
HGRN_VW = HGRN_HEADS * HGRN_DV
SWA_QW = SWA_Q_HEADS * SWA_DH
SWA_KVW = SWA_KV_HEADS * SWA_DH
MIX_W = MLSTM_W + HGRN_VW + SWA_QW
IN_SPLITS = (MLSTM_W, MLSTM_W, MLSTM_W, MLSTM_W, MLSTM_HEADS, MLSTM_HEADS,
             HGRN_KW, HGRN_KW, HGRN_VW, HGRN_VW, SWA_QW, SWA_KVW, SWA_KVW)
IN_W = 4 * MLSTM_W + 2 * MLSTM_HEADS + 2 * HGRN_KW + 2 * HGRN_VW + SWA_QW + 2 * SWA_KVW


def _rms_norm(x, g):
    xf = x.astype(jnp.float32)
    y = xf * lax.rsqrt(jnp.mean(xf * xf, axis=-1, keepdims=True) + EPS) * g.astype(jnp.float32)
    return y.astype(x.dtype)

def _head_rms_norm(x, g, n_heads):
    B, S, W = x.shape
    d = W // n_heads
    y = _rms_norm(x.reshape(B, S, n_heads, d), g.reshape(n_heads, d))
    return y.reshape(B, S, W)

def _split_cols(y, sizes):
    out = []
    o = 0
    for s in sizes:
        out.append(y[..., o:o + s])
        o += s
    return out

def _heads(t, n_heads):
    B, S, W = t.shape
    return t.reshape(B, S, n_heads, W // n_heads)

def _to_chunks(t, L):
    B, S, H = t.shape[:3]
    t = t.reshape((B, S // L, L, H) + t.shape[3:])
    return jnp.moveaxis(t, (1, 3), (0, 2))

def _from_chunks(t):
    nc, B, H, L, d = t.shape
    return jnp.moveaxis(t, (0, 2), (1, 3)).reshape(B, nc * L, H * d)

def _causal_conv(u, w, b):
    K = w.shape[0]
    y = lax.conv_general_dilated(u, w[:, None, :].astype(u.dtype), window_strides=(1,),
                                 padding=[(K - 1, 0)], dimension_numbers=('NWC', 'WIO', 'NWC'),
                                 feature_group_count=u.shape[-1])
    return y + b.astype(u.dtype)

def _rope_tables(positions):
    inv_freq = ROPE_THETA ** (-jnp.arange(0, ROT_DIM, 2, dtype=jnp.float32) / ROT_DIM)
    ang = positions.astype(jnp.float32)[..., None] * inv_freq
    return jnp.cos(ang)[:, :, None, :], jnp.sin(ang)[:, :, None, :]

def _partial_rope(x, cos, sin):
    xf = x.astype(jnp.float32)
    half = ROT_DIM // 2
    x1, x2, rest = xf[..., :half], xf[..., half:ROT_DIM], xf[..., ROT_DIM:]
    y = jnp.concatenate([x1 * cos - x2 * sin, x2 * cos + x1 * sin, rest], axis=-1)
    return y.astype(x.dtype)

def mlstm_chunkwise(q, k, v, i_pre, f_pre):
    f32 = jnp.float32
    B, S, H, dk = q.shape
    dv = v.shape[-1]
    L = MLSTM_CHUNK
    xs = (_to_chunks(q.astype(f32), L), _to_chunks(k.astype(f32), L), _to_chunks(v.astype(f32), L),
          _to_chunks(i_pre.astype(f32), L), _to_chunks(jax.nn.log_sigmoid(f_pre.astype(f32)), L))
    causal = jnp.tril(jnp.ones((L, L), dtype=bool))

    def step(carry, inp):
        C, n, m = carry
        q_, k_, v_, i_, lf = inp
        b = jnp.cumsum(lf, axis=-1)
        dmat = jnp.where(causal, b[..., :, None] - b[..., None, :] + i_[..., None, :], -jnp.inf)
        inter = b + m[..., None]
        m_j = jnp.maximum(inter, jnp.max(dmat, axis=-1))
        w_intra = jnp.exp(dmat - m_j[..., None])
        w_inter = jnp.exp(inter - m_j)
        s = jnp.einsum('bhld,bhsd->bhls', q_, k_) * w_intra
        num = jnp.einsum('bhls,bhse->bhle', s, v_) + w_inter[..., None] * jnp.einsum('bhld,bhde->bhle', q_, C)
        den = jnp.sum(s, axis=-1) + w_inter * jnp.einsum('bhld,bhd->bhl', q_, n)
        h = num / jnp.maximum(jnp.abs(den), jnp.exp(-m_j))[..., None]
        m_new = m_j[..., -1]
        w_s = jnp.exp(b[..., -1:] - b + i_ - m_new[..., None])
        decay = jnp.exp(b[..., -1] + m - m_new)
        C_new = decay[..., None, None] * C + jnp.einsum('bhs,bhsd,bhse->bhde', w_s, k_, v_)
        n_new = decay[..., None] * n + jnp.einsum('bhs,bhsd->bhd', w_s, k_)
        return (C_new, n_new, m_new), h

    init = (jnp.zeros((B, H, dk, dv), f32), jnp.zeros((B, H, dk), f32), jnp.zeros((B, H), f32))
    _, h = lax.scan(step, init, xs)
    return _from_chunks(h)

def hgrn2_chunkwise(q, f_pre, inp, lb):
    f32 = jnp.float32
    B, S, H, dk = q.shape
    dv = inp.shape[-1]
    L = HGRN_CHUNK
    fp = f_pre.astype(f32)
    lb = lb.astype(f32)
    log_f = jnp.logaddexp(jnp.log(lb), jnp.log1p(-lb) + jax.nn.log_sigmoid(fp))
    key = (1.0 - lb) * jax.nn.sigmoid(-fp)
    qf = jax.nn.silu(q.astype(f32))
    xs = (_to_chunks(qf, L), _to_chunks(key, L), _to_chunks(inp.astype(f32), L), _to_chunks(log_f, L))
    causal = jnp.tril(jnp.ones((L, L), dtype=bool))[:, :, None]

    def step(S_state, chunk):
        q_, k_, v_, lf = chunk
        G = jnp.cumsum(lf, axis=2)
        inter = jnp.einsum('bhld,bhde->bhle', q_ * jnp.exp(G), S_state)
        diff = G[:, :, :, None, :] - G[:, :, None, :, :]
        decay = jnp.exp(jnp.where(causal, diff, -jnp.inf))
        A = jnp.einsum('bhld,bhlsd,bhsd->bhls', q_, decay, k_)
        o = inter + jnp.einsum('bhls,bhse->bhle', A, v_)
        G_last = G[:, :, -1]
        S_new = jnp.exp(G_last)[..., None] * S_state + jnp.einsum(
            'bhsd,bhse->bhde', k_ * jnp.exp(G_last[:, :, None] - G), v_)
        return S_new, o

    _, o = lax.scan(step, jnp.zeros((B, H, dk, dv), f32), xs)
    return _from_chunks(o)

def swa_sink_attention(q, k, v, sinks):
    B, S, HQ, d = q.shape
    HKV = k.shape[2]
    G = HQ // HKV
    W = WINDOW
    nb = S // W
    qb = q.reshape(B, nb, W, HKV, G, d)
    kb = k.reshape(B, nb, W, HKV, d)
    vb = v.reshape(B, nb, W, HKV, d)
    kk = jnp.concatenate([jnp.concatenate([jnp.zeros_like(kb[:, :1]), kb[:, :-1]], axis=1), kb], axis=2)
    vv = jnp.concatenate([jnp.concatenate([jnp.zeros_like(vb[:, :1]), vb[:, :-1]], axis=1), vb], axis=2)
    s = jnp.einsum('bnqhgd,bnkhd->bnhgqk', qb, kk).astype(jnp.float32) * (d ** -0.5)
    qi = jnp.arange(W)[:, None]
    ki = jnp.arange(2 * W)[None, :]
    blk = jnp.arange(nb)[:, None, None]
    mask = (ki > qi) & (ki <= qi + W) & ((blk > 0) | (ki >= W))
    s = jnp.where(mask[None, :, None, None], s, -jnp.inf)
    sink = sinks.astype(jnp.float32).reshape(HKV, G)[None, None, :, :, None, None]
    m = jnp.maximum(jnp.max(s, axis=-1, keepdims=True), sink)
    pexp = jnp.exp(s - m)
    probs = pexp / (jnp.sum(pexp, axis=-1, keepdims=True) + jnp.exp(sink - m))
    o = jnp.einsum('bnhgqk,bnkhd->bnqhgd', probs.astype(v.dtype), vv)
    return o.reshape(B, S, HQ * d)

def first_inputs(seed: int = 0) -> dict:
    key = jax.random.key(seed)
    ks = jax.random.split(key, 24)
    f32 = jnp.float32
    nrm = lambda k, shape, scale: jax.random.normal(k, shape, f32) * scale
    x = nrm(ks[0], (BATCH, SEQ, D_MODEL), 1.0)
    p = nrm(ks[1], (DEPTH, BATCH, SEQ, PLE_DIM), 1.0)
    start = jax.random.randint(ks[2], (BATCH, 1), 0, 4096, dtype=jnp.int32)
    positions = (start + jnp.arange(SEQ, dtype=jnp.int32)[None, :]).astype(jnp.int32)
    return {
        "x": x,
        "p": p,
        "positions": positions,
        "in_norm_g": 1.0 + nrm(ks[3], (DEPTH, D_MODEL), 0.05),
        "w_in": nrm(ks[4], (DEPTH, D_MODEL, IN_W), D_MODEL ** -0.5),
        "b_in": nrm(ks[5], (DEPTH, IN_W), 0.02),
        "mlstm_f_bias": jnp.linspace(3.0, 6.0, MLSTM_HEADS, dtype=f32)[None, :] + nrm(ks[6], (DEPTH, MLSTM_HEADS), 0.1),
        "mlstm_conv_w": nrm(ks[7], (DEPTH, CONV_K, 2 * MLSTM_W), CONV_K ** -0.5),
        "mlstm_conv_b": nrm(ks[8], (DEPTH, 2 * MLSTM_W), 0.02),
        "mlstm_norm_g": 1.0 + nrm(ks[9], (DEPTH, MLSTM_W), 0.05),
        "hgrn_lb_logits": nrm(ks[10], (DEPTH, HGRN_KW), 0.1),
        "hgrn_norm_g": 1.0 + nrm(ks[11], (DEPTH, HGRN_VW), 0.05),
        "swa_q_norm_g": 1.0 + nrm(ks[12], (DEPTH, SWA_DH), 0.05),
        "swa_k_norm_g": 1.0 + nrm(ks[13], (DEPTH, SWA_DH), 0.05),
        "swa_sinks": nrm(ks[14], (DEPTH, SWA_Q_HEADS), 0.5),
        "w_out": nrm(ks[15], (DEPTH, MIX_W, D_MODEL), MIX_W ** -0.5),
        "mlp_norm_g": 1.0 + nrm(ks[16], (DEPTH, D_MODEL), 0.05),
        "w_up": nrm(ks[17], (DEPTH, D_MODEL, D_FF), D_MODEL ** -0.5),
        "w_down": nrm(ks[18], (DEPTH, D_FF, D_MODEL), D_FF ** -0.5),
        "ple_norm_g": 1.0 + nrm(ks[19], (DEPTH, D_MODEL), 0.05),
        "w_ple_gate": nrm(ks[20], (DEPTH, D_MODEL, D_MODEL), D_MODEL ** -0.5),
        "w_ple_proj": nrm(ks[21], (DEPTH, PLE_DIM, D_MODEL), PLE_DIM ** -0.5),
        "ple_post_norm_g": 1.0 + nrm(ks[22], (DEPTH, D_MODEL), 0.05),
    }

def first_block(x, p, positions, in_norm_g, w_in, b_in, mlstm_f_bias, mlstm_conv_w, mlstm_conv_b,
              mlstm_norm_g, hgrn_lb_logits, hgrn_norm_g, swa_q_norm_g, swa_k_norm_g, swa_sinks,
              w_out, mlp_norm_g, w_up, w_down, ple_norm_g, w_ple_gate, w_ple_proj, ple_post_norm_g):
    cos, sin = _rope_tables(positions)
    lb_all = jnp.cumsum(jax.nn.softmax(hgrn_lb_logits.astype(jnp.float32), axis=0), axis=0)
    lb_all = lb_all - lb_all[0:1]
    B, S, _ = x.shape
    for l in range(DEPTH):
        h = _rms_norm(x, in_norm_g[l])
        y = h @ w_in[l] + b_in[l]
        (mq, mk, mv, mo, mi, mf, hq, hf, hi, hg, sq, sk, sv) = _split_cols(y, IN_SPLITS)

        qk = jax.nn.silu(_causal_conv(jnp.concatenate([mq, mk], axis=-1), mlstm_conv_w[l], mlstm_conv_b[l]))
        mq_c, mk_c = qk[..., :MLSTM_W], qk[..., MLSTM_W:]
        m_h = mlstm_chunkwise(_heads(mq_c, MLSTM_HEADS), _heads(mk_c, MLSTM_HEADS) * (MLSTM_DH ** -0.5),
                              _heads(mv, MLSTM_HEADS), mi, mf + mlstm_f_bias[l])
        m_out = (_head_rms_norm(m_h, mlstm_norm_g[l], MLSTM_HEADS)
                 * jax.nn.sigmoid(mo.astype(jnp.float32))).astype(x.dtype)

        h_h = hgrn2_chunkwise(_heads(hq, HGRN_HEADS), _heads(hf, HGRN_HEADS), _heads(hi, HGRN_HEADS),
                              lb_all[l].reshape(HGRN_HEADS, HGRN_DK))
        h_out = (_head_rms_norm(h_h, hgrn_norm_g[l], HGRN_HEADS)
                 * jax.nn.silu(hg.astype(jnp.float32))).astype(x.dtype)

        q_s = _partial_rope(_rms_norm(_heads(sq, SWA_Q_HEADS), swa_q_norm_g[l]), cos, sin)
        k_s = _partial_rope(_rms_norm(_heads(sk, SWA_KV_HEADS), swa_k_norm_g[l]), cos, sin)
        s_out = swa_sink_attention(q_s, k_s, _heads(sv, SWA_KV_HEADS), swa_sinks[l]).astype(x.dtype)

        x = x + jnp.concatenate([m_out, h_out, s_out], axis=-1) @ w_out[l]

        u = _rms_norm(x, mlp_norm_g[l]) @ w_up[l]
        x = x + jnp.square(jax.nn.relu(u)) @ w_down[l]

        gate = jax.nn.sigmoid((_rms_norm(x, ple_norm_g[l]) @ w_ple_gate[l]).astype(jnp.float32))
        e = _rms_norm(p[l] @ w_ple_proj[l], ple_post_norm_g[l]).astype(jnp.float32)
        x = x + (gate * e).astype(x.dtype)
    return x


N_MIXERS = 3
NORM_EPS = 1e-6
BLOCK = 128
NEG_INF = -1e30
SWA_HEADS = 16
SWA_KV_HEADS_2 = 4
SWA_HEAD_DIM = D_MODEL // SWA_HEADS
SWA_GROUP = SWA_HEADS // SWA_KV_HEADS_2
SWA_WINDOW = 128
SWA_ROT = SWA_HEAD_DIM // 4
RWKV_HEAD_DIM = 64
RWKV_HEADS = D_MODEL // RWKV_HEAD_DIM
RWKV_DECAY_LORA = 64
RWKV_A_LORA = 64
RWKV_GATE_LORA = 160
RWKV_GN_EPS = 64e-5
MLA_HEADS = 16
MLA_NOPE = 64
MLA_ROPE = 32
MLA_V = 64
MLA_Q_LORA = 384
MLA_KV_LORA = 256
FFN_DIM = 2816
CONV_WIDTH = 3


F32 = jnp.float32

def rms_norm(x, g):
    xf = x.astype(F32)
    y = xf * lax.rsqrt(jnp.mean(xf * xf, axis=-1, keepdims=True) + NORM_EPS)
    return (y * g.astype(F32)).astype(x.dtype)

def rope_tables(seq, rot_dim):
    inv = ROPE_THETA ** (-jnp.arange(0, rot_dim, 2, dtype=F32) / rot_dim)
    ang = jnp.arange(seq, dtype=F32)[:, None] * inv[None, :]
    return jnp.cos(ang), jnp.sin(ang)

def rope_slice(x, cos, sin, start):
    rot = 2 * cos.shape[-1]
    half = rot // 2
    x1 = x[..., start:start + half]
    x2 = x[..., start + half:start + rot]
    c = cos[None, :, None, :].astype(x.dtype)
    s = sin[None, :, None, :].astype(x.dtype)
    return jnp.concatenate([x[..., :start], x1 * c - x2 * s, x2 * c + x1 * s, x[..., start + rot:]], axis=-1)

def swa_mixer(h, w_qkv, q_gain, k_gain, sinks, w_o, cos, sin):
    b, s, _ = h.shape
    nb = s // BLOCK
    qd = SWA_HEADS * SWA_HEAD_DIM
    kd = SWA_KV_HEADS_2 * SWA_HEAD_DIM
    qkv = h @ w_qkv
    q = qkv[..., :qd].reshape(b, s, SWA_HEADS, SWA_HEAD_DIM)
    k = qkv[..., qd:qd + kd].reshape(b, s, SWA_KV_HEADS_2, SWA_HEAD_DIM)
    v = qkv[..., qd + kd:].reshape(b, s, SWA_KV_HEADS_2, SWA_HEAD_DIM)
    q = rope_slice(rms_norm(q, q_gain), cos, sin, 0)
    k = rope_slice(rms_norm(k, k_gain), cos, sin, 0)
    q = q.reshape(b, nb, BLOCK, SWA_KV_HEADS_2, SWA_GROUP, SWA_HEAD_DIM)

    def band(t):
        tp = jnp.pad(t, ((0, 0), (BLOCK, BLOCK), (0, 0), (0, 0)))
        tp = tp.reshape(b, nb + 2, BLOCK, SWA_KV_HEADS_2, SWA_HEAD_DIM)
        return jnp.concatenate([tp[:, :-2], tp[:, 1:-1], tp[:, 2:]], axis=2)

    kb, vb = band(k), band(v)
    blk = jnp.arange(nb)[:, None]
    qpos = blk * BLOCK + jnp.arange(BLOCK)[None, :]
    kpos = (blk - 1) * BLOCK + jnp.arange(3 * BLOCK)[None, :]
    valid = ((kpos >= 0) & (kpos < s))[:, None, :]
    mask = (jnp.abs(qpos[:, :, None] - kpos[:, None, :]) <= SWA_WINDOW) & valid
    sink = sinks.astype(F32).reshape(SWA_KV_HEADS_2, SWA_GROUP)[None, :, :, None, None]
    scale = SWA_HEAD_DIM ** -0.5

    def attend(args):
        qb, kbb, vbb, mb = args
        sc = jnp.einsum('bqhgd,bkhd->bhgqk', qb, kbb).astype(F32) * scale
        sc = jnp.where(mb, sc, NEG_INF)
        m = jnp.maximum(jnp.max(sc, axis=-1, keepdims=True), sink)
        p = jnp.exp(sc - m)
        p = p / (jnp.sum(p, axis=-1, keepdims=True) + jnp.exp(sink - m))
        return jnp.einsum('bhgqk,bkhd->bqhgd', p.astype(vbb.dtype), vbb)

    o = lax.map(attend, (jnp.moveaxis(q, 1, 0), jnp.moveaxis(kb, 1, 0), jnp.moveaxis(vb, 1, 0), mask))
    o = jnp.moveaxis(o, 0, 1).reshape(b, s, qd)
    return o @ w_o

def wkv7_scan(r, w, k, v, a, bb, reverse):
    b, s, nh, n = r.shape
    seq = tuple(jnp.moveaxis(t, 1, 0) for t in (r, w, k, v, a, bb))

    def step(state, inp):
        r_t, w_t, k_t, v_t, a_t, b_t = inp
        sa = jnp.einsum('bhvk,bhk->bhv', state, a_t)
        state = state * w_t[:, :, None, :] + sa[..., None] * b_t[:, :, None, :] + v_t[..., None] * k_t[:, :, None, :]
        y = jnp.einsum('bhvk,bhk->bhv', state, r_t)
        return state, y

    s0 = jnp.zeros((b, nh, n, n), F32)
    _, y = lax.scan(step, s0, seq, reverse=reverse)
    return jnp.moveaxis(y, 0, 1)

def rwkv7_mixer(h, mu, w_r, w_k, w_v, w0, w1, w2, a0, a1, a2, g1, g2, k_k, k_a, r_k, lnx_w, lnx_b, w_o):
    b, s, d = h.shape
    hp = jnp.pad(h, ((0, 0), (1, 1), (0, 0)))
    xx = 0.5 * (hp[:, :-2] + hp[:, 2:]) - h
    xr = h + xx * mu[0]
    xw = h + xx * mu[1]
    xk = h + xx * mu[2]
    xv = h + xx * mu[3]
    xa = h + xx * mu[4]
    xg = h + xx * mu[5]
    r = xr @ w_r
    k = xk @ w_k
    v = xv @ w_v
    g = jax.nn.sigmoid(xg @ g1) @ g2

    def heads(t):
        return t.reshape(b, s, RWKV_HEADS, RWKV_HEAD_DIM)

    kk = heads(k * k_k).astype(F32)
    kk = kk / jnp.maximum(jnp.sqrt(jnp.sum(kk * kk, axis=-1, keepdims=True)), 1e-12)
    rf = heads(r).astype(F32)
    vf = heads(v).astype(F32)
    kf = k.astype(F32)
    rkf = r_k.astype(F32)

    def direction(dirn):
        wl = (w0[dirn] + jnp.tanh(xw @ w1[dirn]) @ w2[dirn]).astype(F32)
        decay = jnp.exp(-jnp.exp(-jax.nn.softplus(-wl) - 0.5))
        a = jax.nn.sigmoid((a0[dirn] + (xa @ a1[dirn]) @ a2[dirn]).astype(F32))
        kd = kf * (1.0 + (a - 1.0) * k_a.astype(F32))
        a, kd, decay = heads(a), heads(kd), heads(decay)
        y = wkv7_scan(rf, decay, kd, vf, -kk, kk * a, reverse=(dirn == 1))
        bonus = jnp.sum(rf * kd * rkf, axis=-1, keepdims=True) * vf
        return y, bonus

    y_f, bonus_f = direction(0)
    y_b, bonus_b = direction(1)
    y = y_f + y_b
    mean = jnp.mean(y, axis=-1, keepdims=True)
    var = jnp.mean(jnp.square(y - mean), axis=-1, keepdims=True)
    yn = ((y - mean) * lax.rsqrt(var + RWKV_GN_EPS)).reshape(b, s, d) * lnx_w.astype(F32) + lnx_b.astype(F32)
    out = (yn + (bonus_f + bonus_b).reshape(b, s, d)) * g.astype(F32)
    return out.astype(h.dtype) @ w_o

def mla_mixer(h, w_down, cq_gain, ckv_gain, w_uq, w_ukv, q_gain, k_gain, w_o, cos, sin):
    b, s, _ = h.shape
    nb = s // BLOCK
    down = h @ w_down
    cq = rms_norm(down[..., :MLA_Q_LORA], cq_gain)
    ckv = rms_norm(down[..., MLA_Q_LORA:MLA_Q_LORA + MLA_KV_LORA], ckv_gain)
    k_rope = down[..., MLA_Q_LORA + MLA_KV_LORA:]
    q = (cq @ w_uq).reshape(b, s, MLA_HEADS, MLA_NOPE + MLA_ROPE)
    kv = (ckv @ w_ukv).reshape(b, s, MLA_HEADS, MLA_NOPE + MLA_V)
    k = jnp.concatenate([kv[..., :MLA_NOPE], jnp.broadcast_to(k_rope[:, :, None, :], (b, s, MLA_HEADS, MLA_ROPE))], axis=-1)
    v = kv[..., MLA_NOPE:]
    q = rope_slice(rms_norm(q, q_gain), cos, sin, MLA_NOPE)
    k = rope_slice(rms_norm(k, k_gain), cos, sin, MLA_NOPE)
    scale = (MLA_NOPE + MLA_ROPE) ** -0.5
    qb = jnp.moveaxis(q.reshape(b, nb, BLOCK, MLA_HEADS, MLA_NOPE + MLA_ROPE), 1, 0)

    def attend(qblk):
        sc = jnp.einsum('bqhd,bkhd->bhqk', qblk, k).astype(F32) * scale
        p = jax.nn.softmax(sc, axis=-1)
        return jnp.einsum('bhqk,bkhd->bqhd', p.astype(v.dtype), v)

    o = lax.map(attend, qb)
    o = jnp.moveaxis(o, 0, 1).reshape(b, s, MLA_HEADS * MLA_V)
    return o @ w_o

def conv_ffn(h, w_up, conv_w, conv_b, w_down):
    s = h.shape[1]
    pad = CONV_WIDTH // 2
    u = h @ w_up
    up = jnp.pad(u, ((0, 0), (pad, pad), (0, 0)))
    acc = up[:, :s] * conv_w[0] + conv_b
    for t in range(1, CONV_WIDTH):
        acc = acc + up[:, t:t + s] * conv_w[t]
    gate, val = jnp.split(acc, 2, axis=-1)
    return (jax.nn.silu(gate) * val) @ w_down

def second_inputs(seed: int = 0) -> dict:
    key = jax.random.key(seed)
    ks = iter(jax.random.split(key, 48))
    n_a = len(range(0, DEPTH, N_MIXERS))
    n_b = len(range(1, DEPTH, N_MIXERS))
    n_c = len(range(2, DEPTH, N_MIXERS))
    d = D_MODEL

    def nrm(shape, scale):
        return scale * jax.random.normal(next(ks), shape, F32)

    def unif(shape, lo, hi):
        return jax.random.uniform(next(ks), shape, F32, lo, hi)

    qkv_w = (SWA_HEADS + 2 * SWA_KV_HEADS_2) * SWA_HEAD_DIM
    return {
        'x': nrm((BATCH, SEQ, d), 1.0),
        'norm_tok': 1.0 + nrm((DEPTH, d), 0.05),
        'norm_ch': 1.0 + nrm((DEPTH, d), 0.05),
        'ffn_w_up': nrm((DEPTH, d, 2 * FFN_DIM), d ** -0.5),
        'ffn_conv_w': nrm((DEPTH, CONV_WIDTH, 2 * FFN_DIM), CONV_WIDTH ** -0.5),
        'ffn_conv_b': nrm((DEPTH, 2 * FFN_DIM), 0.02),
        'ffn_w_down': nrm((DEPTH, FFN_DIM, d), FFN_DIM ** -0.5),
        'swa_w_qkv': nrm((n_a, d, qkv_w), d ** -0.5),
        'swa_q_gain': 1.0 + nrm((n_a, SWA_HEAD_DIM), 0.05),
        'swa_k_gain': 1.0 + nrm((n_a, SWA_HEAD_DIM), 0.05),
        'swa_sinks': nrm((n_a, SWA_HEADS), 1.0),
        'swa_w_o': nrm((n_a, SWA_HEADS * SWA_HEAD_DIM, d), d ** -0.5),
        'rwkv_mu': unif((n_b, 6, d), 0.0, 1.0),
        'rwkv_w_r': nrm((n_b, d, d), d ** -0.5),
        'rwkv_w_k': nrm((n_b, d, d), d ** -0.5),
        'rwkv_w_v': nrm((n_b, d, d), d ** -0.5),
        'rwkv_w0': unif((n_b, 2, d), -6.0, -1.0),
        'rwkv_w1': nrm((n_b, 2, d, RWKV_DECAY_LORA), d ** -0.5),
        'rwkv_w2': nrm((n_b, 2, RWKV_DECAY_LORA, d), 0.5 * RWKV_DECAY_LORA ** -0.5),
        'rwkv_a0': nrm((n_b, 2, d), 0.5),
        'rwkv_a1': nrm((n_b, 2, d, RWKV_A_LORA), d ** -0.5),
        'rwkv_a2': nrm((n_b, 2, RWKV_A_LORA, d), 0.5 * RWKV_A_LORA ** -0.5),
        'rwkv_g1': nrm((n_b, d, RWKV_GATE_LORA), d ** -0.5),
        'rwkv_g2': nrm((n_b, RWKV_GATE_LORA, d), RWKV_GATE_LORA ** -0.5),
        'rwkv_k_k': 0.85 + nrm((n_b, d), 0.1),
        'rwkv_k_a': 1.0 + nrm((n_b, d), 0.1),
        'rwkv_r_k': nrm((n_b, RWKV_HEADS, RWKV_HEAD_DIM), 0.1),
        'rwkv_lnx_w': 1.0 + nrm((n_b, d), 0.05),
        'rwkv_lnx_b': nrm((n_b, d), 0.01),
        'rwkv_w_o': nrm((n_b, d, d), d ** -0.5),
        'mla_w_down': nrm((n_c, d, MLA_Q_LORA + MLA_KV_LORA + MLA_ROPE), d ** -0.5),
        'mla_cq_gain': 1.0 + nrm((n_c, MLA_Q_LORA), 0.05),
        'mla_ckv_gain': 1.0 + nrm((n_c, MLA_KV_LORA), 0.05),
        'mla_w_uq': nrm((n_c, MLA_Q_LORA, MLA_HEADS * (MLA_NOPE + MLA_ROPE)), MLA_Q_LORA ** -0.5),
        'mla_w_ukv': nrm((n_c, MLA_KV_LORA, MLA_HEADS * (MLA_NOPE + MLA_V)), MLA_KV_LORA ** -0.5),
        'mla_q_gain': 1.0 + nrm((n_c, MLA_NOPE + MLA_ROPE), 0.05),
        'mla_k_gain': 1.0 + nrm((n_c, MLA_NOPE + MLA_ROPE), 0.05),
        'mla_w_o': nrm((n_c, MLA_HEADS * MLA_V, d), d ** -0.5),
    }

def second_block(x, norm_tok, norm_ch, ffn_w_up, ffn_conv_w, ffn_conv_b, ffn_w_down,
              swa_w_qkv, swa_q_gain, swa_k_gain, swa_sinks, swa_w_o,
              rwkv_mu, rwkv_w_r, rwkv_w_k, rwkv_w_v, rwkv_w0, rwkv_w1, rwkv_w2,
              rwkv_a0, rwkv_a1, rwkv_a2, rwkv_g1, rwkv_g2, rwkv_k_k, rwkv_k_a, rwkv_r_k,
              rwkv_lnx_w, rwkv_lnx_b, rwkv_w_o,
              mla_w_down, mla_cq_gain, mla_ckv_gain, mla_w_uq, mla_w_ukv,
              mla_q_gain, mla_k_gain, mla_w_o):
    s = x.shape[1]
    cos_a, sin_a = rope_tables(s, SWA_ROT)
    cos_c, sin_c = rope_tables(s, MLA_ROPE)
    for i in range(DEPTH):
        kind = i % N_MIXERS
        j = i // N_MIXERS
        h = rms_norm(x, norm_tok[i])
        if kind == 0:
            y = swa_mixer(h, swa_w_qkv[j], swa_q_gain[j], swa_k_gain[j], swa_sinks[j], swa_w_o[j], cos_a, sin_a)
        elif kind == 1:
            y = rwkv7_mixer(h, rwkv_mu[j], rwkv_w_r[j], rwkv_w_k[j], rwkv_w_v[j], rwkv_w0[j], rwkv_w1[j], rwkv_w2[j],
                            rwkv_a0[j], rwkv_a1[j], rwkv_a2[j], rwkv_g1[j], rwkv_g2[j], rwkv_k_k[j], rwkv_k_a[j],
                            rwkv_r_k[j], rwkv_lnx_w[j], rwkv_lnx_b[j], rwkv_w_o[j])
        else:
            y = mla_mixer(h, mla_w_down[j], mla_cq_gain[j], mla_ckv_gain[j], mla_w_uq[j], mla_w_ukv[j],
                          mla_q_gain[j], mla_k_gain[j], mla_w_o[j], cos_c, sin_c)
        x = x + y
        x = x + conv_ffn(rms_norm(x, norm_ch[i]), ffn_w_up[i], ffn_conv_w[i], ffn_conv_b[i], ffn_w_down[i])
    return x


def setup_inputs(seed=0):
    out = dict(first_inputs(seed))
    for name, value in second_inputs(seed + 1).items():
        if name != "x":
            out[name + "_2"] = value
    return out


def reference(
    x, p, positions, in_norm_g, w_in, b_in, mlstm_f_bias, mlstm_conv_w, mlstm_conv_b,
    mlstm_norm_g, hgrn_lb_logits, hgrn_norm_g, swa_q_norm_g, swa_k_norm_g, swa_sinks, w_out,
    mlp_norm_g, w_up, w_down, ple_norm_g, w_ple_gate, w_ple_proj, ple_post_norm_g, norm_tok_2,
    norm_ch_2, ffn_w_up_2, ffn_conv_w_2, ffn_conv_b_2, ffn_w_down_2, swa_w_qkv_2, swa_q_gain_2,
    swa_k_gain_2, swa_sinks_2, swa_w_o_2, rwkv_mu_2, rwkv_w_r_2, rwkv_w_k_2, rwkv_w_v_2,
    rwkv_w0_2, rwkv_w1_2, rwkv_w2_2, rwkv_a0_2, rwkv_a1_2, rwkv_a2_2, rwkv_g1_2, rwkv_g2_2,
    rwkv_k_k_2, rwkv_k_a_2, rwkv_r_k_2, rwkv_lnx_w_2, rwkv_lnx_b_2, rwkv_w_o_2, mla_w_down_2,
    mla_cq_gain_2, mla_ckv_gain_2, mla_w_uq_2, mla_w_ukv_2, mla_q_gain_2, mla_k_gain_2,
    mla_w_o_2,
):
    x = first_block(
        x, p, positions, in_norm_g, w_in, b_in, mlstm_f_bias, mlstm_conv_w, mlstm_conv_b,
        mlstm_norm_g, hgrn_lb_logits, hgrn_norm_g, swa_q_norm_g, swa_k_norm_g, swa_sinks, w_out,
        mlp_norm_g, w_up, w_down, ple_norm_g, w_ple_gate, w_ple_proj, ple_post_norm_g,
    )
    return second_block(
        x, norm_tok_2, norm_ch_2, ffn_w_up_2, ffn_conv_w_2, ffn_conv_b_2, ffn_w_down_2,
        swa_w_qkv_2, swa_q_gain_2, swa_k_gain_2, swa_sinks_2, swa_w_o_2, rwkv_mu_2, rwkv_w_r_2,
        rwkv_w_k_2, rwkv_w_v_2, rwkv_w0_2, rwkv_w1_2, rwkv_w2_2, rwkv_a0_2, rwkv_a1_2,
        rwkv_a2_2, rwkv_g1_2, rwkv_g2_2, rwkv_k_k_2, rwkv_k_a_2, rwkv_r_k_2, rwkv_lnx_w_2,
        rwkv_lnx_b_2, rwkv_w_o_2, mla_w_down_2, mla_cq_gain_2, mla_ckv_gain_2, mla_w_uq_2,
        mla_w_ukv_2, mla_q_gain_2, mla_k_gain_2, mla_w_o_2,
    )


_drawn_inputs = setup_inputs


def setup_inputs(seed=0):
    import zlib

    import numpy as np

    out = dict(_drawn_inputs(seed))
    spreads = {}
    factors = {'mlstm_conv_b': 6.212,
     'mlstm_norm_g': 3.077,
     'hgrn_lb_logits': 8.0,
     'hgrn_norm_g': 2.853,
     'swa_q_norm_g': 8.0,
     'swa_k_norm_g': 8.0,
     'swa_sinks': 43.776,
     'ple_norm_g': 6.588,
     'ffn_conv_b_2': 5.32,
     'swa_q_gain_2': 8.0,
     'swa_k_gain_2': 8.0,
     'swa_sinks_2': 8.0,
     'rwkv_w1_2': 4.353,
     'rwkv_w2_2': 4.658,
     'rwkv_lnx_w_2': 4.765,
     'rwkv_lnx_b_2': 44.607}
    for name, (base, spread) in spreads.items():
        noise = np.random.default_rng([zlib.crc32(name.encode()), seed]).standard_normal(out[name].shape)
        drawn = base * np.exp(spread * noise) if base else spread * noise
        out[name] = jnp.asarray(drawn.astype(out[name].dtype))
    for name, factor in factors.items():
        out[name] = (out[name] * factor).astype(out[name].dtype)
    return out
```

```python
from contextlib import ExitStack, contextmanager

import numpy as np
import concourse.bass as bass
from concourse import mybir

F32 = mybir.dt.float32
I32 = mybir.dt.int32
ALU = mybir.AluOpType
ACT = mybir.ActivationFunctionType
AX_X = mybir.AxisListType.X

P = 128
S = 512
NT = S // P
D = 1024
DT = D // P
DEPTH = 2
EPS = 1e-6
HD = 64
CONV_K = 4
D_FF = 4 * D
FFT = D_FF // P
PLE = 256
FFN = 2816
GT = FFN // P
ROPE_THETA = 500000.0
ROT = HD // 4
NEG = -1e30
RW_CHUNK = 64
RING = 4
FIRST_SEMAPHORE = 150
DECAY_SCALE = float(np.exp(-0.5))

IN_TILES = ["mq", "mq", "mk", "mk", "mv", "mv", "mo", "mo", "hq", "hq", "hf", "hf", "hi", "hi", "hg", "hg",
            "sq", "sq", "sq", "sq", "sk", "sv"]
MQ, MK, MV, MO, HQ, HF, HI, HG, SQ, SK, SV = 0, 2, 4, 6, 8, 10, 12, 14, 16, 20, 21
NIN = len(IN_TILES)


def columns(*named):
    at, places = 0, {}
    for name, width in named:
        places[name] = at
        at += width
    return places, at


V1, V1_W = columns(("in_g", DT), ("b_in", NIN), ("m_g", 2), ("h_g", 2), ("q_g", 1), ("k_g", 1),
                   ("conv_w", CONV_K * 4), ("conv_b", 4), ("mlp_g", DT), ("ple_g", DT), ("post_g", DT),
                   ("sinks", 8), ("b_i", 1), ("b_f", 1), ("f_bias", 1), ("lb", 2 * DEPTH), ("is_first", 1))
V2, V2_W = columns(("tok_g", DT), ("ch_g", DT), ("conv_w", 3 * 2 * GT), ("conv_b", 2 * GT))
VS, VS_W = columns(("q_g", 1), ("k_g", 1), ("sinks", 16))
VR, VR_W = columns(("mu", 6 * DT), ("w0", 2 * DT), ("a0", 2 * DT), ("k_k", DT), ("k_a", DT), ("r_k", DT),
                   ("ln_w", DT), ("ln_b", DT))

HG_LEVELS = 7
RW_LEVELS = 5
CONSTS, CONSTS_W = columns(("ident", P), ("ones", P), ("head_ones", P), ("rot", P), ("inv_freq", 1),
                           ("pick", 4 * P), ("pick_pair", 2 * P))
MASKS, MASKS_W = columns(("causal", P), ("levels", HG_LEVELS * P))
BANDS1_W = 2 * P
BANDS2_W = 3 * P
RMASKS, RMASKS_W = columns(("before", P), ("upto", P), ("pair", P), ("pair_t", P), ("merge", RW_LEVELS * P))


def constants():
    i, j = np.arange(P)[:, None], np.arange(P)[None, :]
    c = np.zeros((P, CONSTS_W), np.float32)
    c[:, CONSTS["ident"]:CONSTS["ident"] + P] = i == j
    c[:, CONSTS["ones"]:CONSTS["ones"] + P] = 1.0
    c[:, CONSTS["head_ones"]:CONSTS["head_ones"] + P] = i // HD == j // HD
    half = ROT // 2
    for base in (0, HD):
        for d in range(half):
            c[base + half + d, CONSTS["rot"] + base + d] = -1.0
            c[base + d, CONSTS["rot"] + base + half + d] = 1.0
            f = np.float32(ROPE_THETA) ** np.float32(-2.0 * d / ROT)
            c[base + d, CONSTS["inv_freq"]] = f
            c[base + half + d, CONSTS["inv_freq"]] = f
    for h in range(4):
        c[h, CONSTS["pick"] + h * P:CONSTS["pick"] + (h + 1) * P] = 1.0
        at = CONSTS["pick_pair"] + (h // 2) * P + (h % 2) * HD
        c[h, at:at + HD] = 1.0
    m = np.zeros((P, MASKS_W), np.float32)
    m[:, 0:P] = i <= j
    for level in range(HG_LEVELS):
        w = 1 << level
        same = i // (2 * w) == j // (2 * w)
        m[:, MASKS["levels"] + level * P:MASKS["levels"] + (level + 1) * P] = same & (i % (2 * w) < w) & (j % (2 * w) >= w)
    b1 = np.concatenate([np.where(j > i, 0, NEG), np.where(j <= i, 0, NEG)], 1).astype(np.float32)
    b2 = np.concatenate([np.where(j >= i, 0, NEG), np.zeros((P, P)), np.where(j <= i, 0, NEG)], 1).astype(np.float32)
    r = np.zeros((P, RMASKS_W), np.float32)
    chunk = i // RW_CHUNK == j // RW_CHUNK
    r[:, RMASKS["before"]:RMASKS["before"] + P] = chunk & (i < j)
    r[:, RMASKS["upto"]:RMASKS["upto"] + P] = chunk & (i <= j)
    r[:, RMASKS["pair"]:RMASKS["pair"] + P] = (i // 2 == j // 2) & (i > j)
    r[:, RMASKS["pair_t"]:RMASKS["pair_t"] + P] = (i // 2 == j // 2) & (i < j)
    for level in range(RW_LEVELS):
        w = 2 << level
        same = i // (2 * w) == j // (2 * w)
        r[:, RMASKS["merge"] + level * P:RMASKS["merge"] + (level + 1) * P] = same & (i % (2 * w) < w) & (j % (2 * w) >= w)
    return {"consts": c, "masks": m, "bands1": b1, "bands2": b2, "rmasks": r}


@contextmanager
def stage(nc, name, *signals):
    with ExitStack() as held:
        sems, numbers = {}, []
        for signal in signals:
            word, _, count = signal.partition("*")
            made = [held.enter_context(nc.semaphore(f"{name}_{word}{j}", num=FIRST_SEMAPHORE + len(numbers) + j)) for j in range(int(count or 1))]
            numbers += [s.num for s in made]
            sems[word] = made if count else made[0]
        block = held.enter_context(ExitStack())
        yield block.enter_context(nc.Block(no_gpsimd_drain=True)), sems
        block.close()
        nc.all_engine_barrier(sems_to_clear=range(min(numbers), max(numbers) + 1))


def tile_of(ap, index):
    return ap[:, bass.ds(index, 1), :].rearrange("p a n -> p (a n)")


def row_of(dram, index):
    return dram[bass.ds(index, 1)].rearrange("a p n -> p (a n)")


def spread(ap, n):
    return ap.unsqueeze(1).broadcast_to([ap.shape[0], n, ap.shape[1]])


def load(nc, name, pairs):
    with stage(nc, name, "loaded") as (block, s):
        @block.sync
        def _(sp):
            for dst, src in pairs:
                sp.dma_start(dst, src).then_inc(s["loaded"], 16)
            sp.wait_ge(s["loaded"], 16 * len(pairs))


def norm(nc, name, m, src, gain, dst, width=D):
    tiles = width // P
    with stage(nc, name, "squares_ready", "sums_ready", "root_ready", "rstd_ready", "normed") as (block, s):
        @block.scalar
        def _(act):
            for k in range(tiles):
                nc.scalar.activation(m.sq[:, k, :], src[:, k, :], ACT.Square).then_inc(s["squares_ready"], 1)
            act.wait_ge(s["sums_ready"], 1)
            nc.scalar.activation(m.rstd[:], m.ps[:, 0, :], ACT.Sqrt, scale=1.0 / width, bias=m.eps[:, 0:1]).then_inc(s["root_ready"], 1)

        @block.tensor
        def _(pe):
            for k in range(tiles):
                pe.wait_ge(s["squares_ready"], k + 1)
                mm = nc.tensor.matmul(m.ps[:, 0, :], m.ones, m.sq[:, k, :], start=(k == 0), stop=(k == tiles - 1))
            mm.then_inc(s["sums_ready"], 1)

        @block.vector
        def _(dve):
            dve.wait_ge(s["root_ready"], 1)
            nc.vector.reciprocal(m.rstd[:], m.rstd[:]).then_inc(s["rstd_ready"], 1)
            dve.wait_ge(s["rstd_ready"], 1)
            for k in range(tiles):
                nc.vector.scalar_tensor_tensor(out=dst[:, k, :], in0=src[:, k, :], scalar=gain[:, k:k + 1],
                                               in1=m.rstd[:], op0=ALU.mult, op1=ALU.mult).then_inc(s["normed"], 1)


def linear(nc, name, m, weights, first, rhs, n_tiles, parts, ks, unroll, signals=(), on_act=None, on_dve=None, at_start=None):
    ring = unroll * parts
    assert n_tiles % unroll == 0 and ks * P <= m.ring.shape[2] and ring <= RING
    with stage(nc, name, f"loaded*{ring}", "slots_used", "banks_free", *signals) as (block, s):
        @block.sync
        def _(sp):
            with sp.Fori(0, n_tiles // unroll) as i:
                for j in range(ring):
                    sp.wait_ge(s["slots_used"], i * ring + (j + 1))
                    sp.dma_start(m.ring[:, j, 0:ks * P], row_of(weights, i * ring + (first + j))).then_inc(s["loaded"][j], 16)

        @block.tensor
        def _(pe):
            pe.sem_inc(s["slots_used"], ring)
            pe.sem_inc(s["banks_free"], unroll)
            if at_start:
                at_start(pe, s)
            with pe.Fori(0, n_tiles // unroll) as i:
                for u in range(unroll):
                    pe.wait_ge(s["banks_free"], i * unroll + (u + 1))
                    for part in range(parts):
                        j = u * parts + part
                        pe.wait_ge(s["loaded"][j], i * 16 + 16)
                        for k in range(ks):
                            mm = nc.tensor.matmul(m.ps[:, u, :], m.ring[:, j, k * P:(k + 1) * P], rhs(part * ks + k),
                                                  start=(part == 0 and k == 0), stop=(part == parts - 1 and k == ks - 1))
                        mm.then_inc(s["slots_used"], 1)

        def products(i):
            return lambda u: i * ring + (ring + (u + 1) * parts)

        if on_act:
            @block.scalar
            def _(act):
                with act.Fori(0, n_tiles // unroll) as i:
                    on_act(act, i, s, products(i))
        if on_dve:
            @block.vector
            def _(dve):
                with dve.Fori(0, n_tiles // unroll) as i:
                    on_dve(dve, i, s, products(i))


def add_to_x(nc, m, unroll):
    def on_dve(dve, i, s, products):
        for u in range(unroll):
            dve.wait_ge(s["slots_used"], products(u))
            x = tile_of(m.x, i * unroll + u)
            nc.vector.tensor_tensor(x, x, m.ps[:, u, :], ALU.add).then_inc(s["banks_free"], 1)
    return on_dve


def to_tiles(nc, m, dst, unroll, func=ACT.Copy, bias=None):
    def on_act(act, i, s, products):
        for u in range(unroll):
            act.wait_ge(s["slots_used"], products(u))
            if bias is None:
                ins = nc.scalar.activation(tile_of(dst, i * unroll + u), m.ps[:, u, :], func)
            else:
                ins = nc.scalar.activation(tile_of(dst, i * unroll + u), m.ps[:, u, :], func, bias=bias[:, bass.ds(i * unroll + u, 1)])
            ins.then_inc(s["banks_free"], 1)
    return on_act


def rope_table(nc, name, m, positions):
    two_pi = 2.0 * np.pi
    high = float(np.float32(6.28125))
    mid = float(np.float32(0.0019340515))
    mid = float(np.frombuffer((np.frombuffer(np.float32(mid).tobytes(), np.uint32) & np.uint32(0xFFFFF000)).tobytes(), np.float32)[0])
    low = float(two_pi - high - mid)
    magic = 12582912.0
    with ExitStack() as tmp, stage(nc, name, "steps", "angles_ready", "positions_loaded", "tables_ready") as (block, s):
        pos = tmp.enter_context(nc.sbuf_tensor(f"{name}_pos", [P, S], I32))
        turns = tmp.enter_context(nc.sbuf_tensor(f"{name}_turns", [P, S], F32))

        @block.sync
        def _(sp):
            sp.dma_start(pos[:], positions).then_inc(s["positions_loaded"], 16)

        @block.vector
        def _(dve):
            done = [0]

            def step(ins):
                done[0] += 1
                ins.then_inc(s["steps"], 1)
                dve.wait_ge(s["steps"], done[0])

            dve.wait_ge(s["positions_loaded"], 16)
            step(nc.vector.tensor_copy(m.sin[:], pos[:]))
            step(nc.vector.tensor_scalar(m.sin[:], m.sin[:], m.c[:, CONSTS["inv_freq"]:CONSTS["inv_freq"] + 1], None, ALU.mult))
            step(nc.vector.tensor_scalar(turns[:], m.sin[:], 1.0 / two_pi, None, ALU.mult))
            step(nc.vector.tensor_scalar(turns[:], turns[:], magic, None, ALU.add))
            step(nc.vector.tensor_scalar(turns[:], turns[:], -magic, None, ALU.add))
            for part in (high, mid, low):
                step(nc.vector.scalar_tensor_tensor(out=m.sin[:], in0=turns[:], scalar=-part, in1=m.sin[:], op0=ALU.mult, op1=ALU.add))
            step(nc.vector.tensor_scalar(turns[:], m.sin[:], np.pi / 2, -two_pi, ALU.is_gt, ALU.mult))
            step(nc.vector.scalar_tensor_tensor(out=m.cos[:], in0=m.sin[:], scalar=np.pi / 2, in1=turns[:], op0=ALU.add, op1=ALU.add))
            for t in (m.sin, m.cos):
                step(nc.vector.tensor_scalar(t[:], t[:], 3.1415925, -3.1415925, ALU.min, ALU.max))
            dve.sem_inc(s["angles_ready"], 1)

        @block.scalar
        def _(act):
            act.wait_ge(s["angles_ready"], 1)
            for t in (m.sin, m.cos):
                nc.scalar.activation(t[:], t[:], ACT.Sin).then_inc(s["tables_ready"], 1)


def heads_norm_rope(nc, name, m, tiles, gain):
    n = tiles.shape[1]
    with ExitStack() as tmp, stage(nc, name, "squares_ready", "sums_ready", "root_ready", "rstd_ready", "normed",
                                   "rotated", "turned", "scaled") as (block, s):
        sq, rstd = m.sq[:, 0:n, :], m.sq[:, 4:4 + n, :]
        other = tmp.enter_context(nc.sbuf_tensor(f"{name}_other", [P, n, S], F32))

        @block.scalar
        def _(act):
            nc.scalar.activation(sq, tiles, ACT.Square).then_inc(s["squares_ready"], 1)
            act.wait_ge(s["sums_ready"], n)
            nc.scalar.activation(rstd, m.ps[:, 0:n, :], ACT.Sqrt, scale=1.0 / HD, bias=m.eps[:, 0:1]).then_inc(s["root_ready"], 1)

        @block.tensor
        def _(pe):
            pe.wait_ge(s["squares_ready"], 1)
            for k in range(n):
                nc.tensor.matmul(m.ps[:, k, :], m.head_ones, sq[:, k, :], start=True, stop=True).then_inc(s["sums_ready"], 1)
            pe.wait_ge(s["normed"], 1)
            for k in range(n):
                nc.tensor.matmul(m.ps[:, 4 + k, :], m.rot, tiles[:, k, :], start=True, stop=True).then_inc(s["rotated"], 1)

        @block.vector
        def _(dve):
            dve.wait_ge(s["root_ready"], 1)
            nc.vector.reciprocal(rstd, rstd).then_inc(s["rstd_ready"], 1)
            dve.wait_ge(s["rstd_ready"], 1)
            nc.vector.scalar_tensor_tensor(out=tiles, in0=tiles, scalar=gain, in1=rstd, op0=ALU.mult, op1=ALU.mult).then_inc(s["normed"], 1)
            dve.wait_ge(s["rotated"], n)
            nc.vector.tensor_tensor(other[:], m.ps[:, 4:4 + n, :], spread(m.sin[:], n), ALU.mult).then_inc(s["turned"], 1)
            nc.vector.tensor_tensor(tiles, tiles, spread(m.cos[:], n), ALU.mult).then_inc(s["scaled"], 1)
            dve.wait_ge(s["turned"], 1)
            dve.wait_ge(s["scaled"], 1)
            nc.vector.tensor_tensor(tiles, tiles, other[:], ALU.add).then_inc(s["scaled"], 1)


def heads_norm_gate(nc, name, m, src, gain, gate, func, dst):
    with stage(nc, name, "squares_ready", "sums_ready", "root_ready", "rstd_ready", "gate_ready", "normed", "done") as (block, s):
        sq, rstd, g = m.sq[:, 0:2, :], m.sq[:, 2:4, :], m.sq[:, 4:6, :]

        @block.scalar
        def _(act):
            nc.scalar.activation(sq, src, ACT.Square).then_inc(s["squares_ready"], 1)
            nc.scalar.activation(g, gate, func).then_inc(s["gate_ready"], 1)
            act.wait_ge(s["sums_ready"], 2)
            nc.scalar.activation(rstd, m.ps[:, 0:2, :], ACT.Sqrt, scale=1.0 / HD, bias=m.eps[:, 0:1]).then_inc(s["root_ready"], 1)

        @block.tensor
        def _(pe):
            pe.wait_ge(s["squares_ready"], 1)
            for k in range(2):
                nc.tensor.matmul(m.ps[:, k, :], m.head_ones, sq[:, k, :], start=True, stop=True).then_inc(s["sums_ready"], 1)

        @block.vector
        def _(dve):
            dve.wait_ge(s["root_ready"], 1)
            nc.vector.reciprocal(rstd, rstd).then_inc(s["rstd_ready"], 1)
            dve.wait_ge(s["rstd_ready"], 1)
            for k in range(2):
                nc.vector.scalar_tensor_tensor(out=rstd[:, k, :], in0=src[:, k, :], scalar=gain[:, k:k + 1], in1=rstd[:, k, :],
                                               op0=ALU.mult, op1=ALU.mult).then_inc(s["normed"], 1)
            dve.wait_ge(s["normed"], 2)
            dve.wait_ge(s["gate_ready"], 1)
            nc.vector.tensor_tensor(dst, rstd, g, ALU.mult).then_inc(s["done"], 1)


def transpose_tiles(nc, name, m, src, dst):
    n = src.shape[1]
    with stage(nc, name, "turned", "copied") as (block, s):
        @block.tensor
        def _(pe):
            for j in range(NT):
                for k in range(n):
                    nc.tensor.transpose(m.ps[:, j, k * P:(k + 1) * P], src[:, k, j * P:(j + 1) * P], m.ident).then_inc(s["turned"], 1)

        @block.vector
        def _(dve):
            for j in range(NT):
                dve.wait_ge(s["turned"], n * (j + 1))
                nc.vector.tensor_copy(dst[:, j, 0:n * P], m.ps[:, j, 0:n * P]).then_inc(s["copied"], 1)


def conv_silu(nc, m, tiles, vec):
    with ExitStack() as tmp, stage(nc, "conv", "taps", "silu_done") as (block, s):
        acc = tmp.enter_context(nc.sbuf_tensor("conv_acc", [P, 4, S], F32))

        @block.vector
        def _(dve):
            for tap in range(CONV_K):
                back = tap
                for k in range(4):
                    w = vec[:, V1["conv_w"] + (CONV_K - 1 - tap) * 4 + k:V1["conv_w"] + (CONV_K - 1 - tap) * 4 + k + 1]
                    if tap == 0:
                        ins = nc.vector.tensor_scalar(acc[:, k, :], tiles[:, k, :], w, vec[:, V1["conv_b"] + k:V1["conv_b"] + k + 1], ALU.mult, ALU.add)
                    else:
                        dve.wait_ge(s["taps"], tap * 4 - 3 + k)
                        ins = nc.vector.scalar_tensor_tensor(out=acc[:, k, back:], in0=tiles[:, k, 0:S - back], scalar=w,
                                                             in1=acc[:, k, back:], op0=ALU.mult, op1=ALU.add)
                    ins.then_inc(s["taps"], 1)

        @block.scalar
        def _(act):
            act.wait_ge(s["taps"], 4 * CONV_K)
            nc.scalar.activation(tiles, acc[:], ACT.Silu).then_inc(s["silu_done"], 1)


def mlstm(nc, m, vec, y, gates, dst):
    with ExitStack() as tmp:
        def sb(name, shape):
            return tmp.enter_context(nc.sbuf_tensor(f"mlstm_{name}", shape, F32))

        F, ABS, LN, LF, B, M, C, A = range(8)
        rows = sb("rows", [4, 8, S])
        neg_m = sb("neg_m", [4, S])
        zeros = sb("zeros", [4, S])
        v_tok = sb("v_tok", [P, NT, 2 * P])
        a_col = sb("a_col", [P, NT, 4])
        w = sb("w", [P, 4, S])
        den = sb("den", [P, 2, S])
        em = sb("em", [P, 2, S])

        with stage(nc, "mlstm_gates", "steps", "abs_ready", "exp_ready", "ln_ready") as (block, s):
            @block.vector
            def _(dve):
                done = [0]

                def step(ins):
                    done[0] += 1
                    ins.then_inc(s["steps"], 1)
                    dve.wait_ge(s["steps"], done[0])

                step(nc.vector.memset(zeros[:], 0.0))
                step(nc.vector.tensor_scalar(rows[:, F, :], gates[32:36, :], vec[32:36, V1["f_bias"]:V1["f_bias"] + 1], None, ALU.add))
                step(nc.vector.scalar_tensor_tensor(out=rows[:, ABS, :], in0=rows[:, F, :], scalar=-1.0, in1=rows[:, F, :], op0=ALU.mult, op1=ALU.max))
                dve.sem_inc(s["abs_ready"], 1)
                step(nc.vector.tensor_scalar(rows[:, F, :], rows[:, F, :], 0.0, None, ALU.min))
                dve.wait_ge(s["ln_ready"], 1)
                step(nc.vector.tensor_tensor(rows[:, LF, :], rows[:, F, :], rows[:, LN, :], ALU.subtract))
                step(nc.vector.tensor_tensor_scan(rows[:, B, :], rows[:, LF, :], zeros[:], 0.0, ALU.add, ALU.add))
                step(nc.vector.tensor_tensor_scan(rows[:, M, :], rows[:, LF, :], gates[0:4, :], 0.0, ALU.add, ALU.max))
                step(nc.vector.tensor_tensor(rows[:, C, :], rows[:, B, :], rows[:, M, :], ALU.subtract))
                step(nc.vector.tensor_tensor(rows[:, A, :], gates[0:4, :], rows[:, B, :], ALU.subtract))
                step(nc.vector.tensor_scalar(neg_m[:], rows[:, M, :], -1.0, None, ALU.mult))

            @block.scalar
            def _(act):
                act.wait_ge(s["abs_ready"], 1)
                nc.scalar.activation(rows[:, LN, :], rows[:, ABS, :], ACT.Exp, scale=-1.0).then_inc(s["exp_ready"], 1)
                act.wait_ge(s["exp_ready"], 1)
                nc.scalar.activation(rows[:, LN, :], rows[:, LN, :], ACT.Ln, bias=m.one[:, 0:1][0:4]).then_inc(s["ln_ready"], 1)

        transpose_tiles(nc, "mlstm_v", m, y[:, MV:MV + 2, :], v_tok)

        with stage(nc, "mlstm_a", "turned", "copied") as (block, s):
            @block.tensor
            def _(pe):
                for j in range(NT):
                    nc.tensor.transpose(m.ps[:, 0, 4 * j:4 * j + 4], rows[:, A, j * P:(j + 1) * P], m.ident[0:4, 0:4]).then_inc(s["turned"], 1)

            @block.vector
            def _(dve):
                dve.wait_ge(s["turned"], NT)
                nc.vector.tensor_copy(a_col[:].rearrange("p a b -> p (a b)"), m.ps[:, 0, 0:4 * NT]).then_inc(s["copied"], 1)

        units = [(h, j) for h in range(4) for j in range(NT)]
        with stage(nc, "mlstm", "rows_spread", "scores_ready", "args_ready", "exp_ready", "weighted", "masked", "summed") as (block, s):
            @block.tensor
            def _(pe):
                def outputs(n):
                    h, j = units[n]
                    pe.wait_ge(s["masked"], n + 1)
                    for bank, lhsT in ((4, v_tok[:, j, h * HD:(h + 1) * HD]), (6, m.ones[:, 0:HD])):
                        mm = nc.tensor.matmul(m.ps[(h % 2) * HD:(h % 2 + 1) * HD, bank + h // 2, j * P:], lhsT, w[:, n % 4, j * P:],
                                              start=(j == 0), stop=(j == NT - 1))
                    mm.then_inc(s["summed"], 1)

                for n, (h, j) in enumerate(units):
                    lo = (h % 2) * HD
                    if j == 0:
                        if h >= 2:
                            pe.wait_ge(s["args_ready"], (h - 1) * NT)
                        nc.tensor.matmul(m.ps[:, h % 2, :], m.pick[0:4, h * P:(h + 1) * P], rows[:, C, :], start=True, stop=True).then_inc(s["rows_spread"], 1)
                    if n >= 2:
                        pe.wait_ge(s["weighted"], n - 1)
                    nc.tensor.matmul(m.ps[:, 2 + n % 2, j * P:], y[lo:lo + HD, MK + h // 2, j * P:(j + 1) * P],
                                     y[lo:lo + HD, MQ + h // 2, j * P:], start=True, stop=True).then_inc(s["scores_ready"], 1)
                    if n >= 1:
                        outputs(n - 1)
                outputs(len(units) - 1)

            @block.vector
            def _(dve):
                def args(n):
                    h, j = units[n]
                    dve.wait_ge(s["rows_spread"], h + 1)
                    if n >= 4:
                        dve.wait_ge(s["summed"], n - 3)
                    nc.vector.tensor_scalar(w[:, n % 4, j * P:], m.ps[:, h % 2, j * P:], a_col[:, j, h:h + 1], 0.0, ALU.add, ALU.min).then_inc(s["args_ready"], 1)

                args(0)
                for n, (h, j) in enumerate(units):
                    if n + 1 < len(units):
                        args(n + 1)
                    dve.wait_ge(s["exp_ready"], n + 1)
                    dve.wait_ge(s["scores_ready"], n + 1)
                    nc.vector.scalar_tensor_tensor(out=w[:, n % 4, j * P:], in0=m.ps[:, 2 + n % 2, j * P:], scalar=HD ** -0.5,
                                                   in1=w[:, n % 4, j * P:], op0=ALU.mult, op1=ALU.mult).then_inc(s["weighted"], 1)
                    dve.wait_ge(s["weighted"], n + 1)
                    nc.vector.tensor_tensor(w[:, n % 4, j * P:(j + 1) * P], w[:, n % 4, j * P:(j + 1) * P], m.masks[:, 0:P], ALU.mult).then_inc(s["masked"], 1)

            @block.scalar
            def _(act):
                for n, (h, j) in enumerate(units):
                    act.wait_ge(s["args_ready"], n + 1)
                    nc.scalar.activation(w[:, n % 4, j * P:], w[:, n % 4, j * P:], ACT.Exp).then_inc(s["exp_ready"], 1)

        with stage(nc, "mlstm_out", "floor_spread", "floor_ready", "abs_ready", "steps") as (block, s):
            @block.tensor
            def _(pe):
                for k in range(2):
                    nc.tensor.matmul(m.ps[:, k, :], m.pick_pair[0:4, k * P:(k + 1) * P], neg_m[:], start=True, stop=True).then_inc(s["floor_spread"], 1)

            @block.scalar
            def _(act):
                nc.scalar.activation(den[:], m.ps[:, 6:8, :], ACT.Abs).then_inc(s["abs_ready"], 1)
                act.wait_ge(s["floor_spread"], 2)
                nc.scalar.activation(em[:], m.ps[:, 0:2, :], ACT.Exp).then_inc(s["floor_ready"], 1)

            @block.vector
            def _(dve):
                dve.wait_ge(s["abs_ready"], 1)
                dve.wait_ge(s["floor_ready"], 1)
                nc.vector.tensor_tensor(den[:], den[:], em[:], ALU.max).then_inc(s["steps"], 1)
                dve.wait_ge(s["steps"], 1)
                nc.vector.reciprocal(den[:], den[:]).then_inc(s["steps"], 1)
                dve.wait_ge(s["steps"], 2)
                nc.vector.tensor_tensor(den[:], den[:], m.ps[:, 4:6, :], ALU.mult).then_inc(s["steps"], 1)

        heads_norm_gate(nc, "mlstm_norm", m, den[:], vec[:, V1["m_g"]:V1["m_g"] + 2], y[:, MO:MO + 2, :], ACT.Sigmoid, dst)


def hgrn(nc, m, vec, y, dst):
    with ExitStack() as tmp:
        def sb(name, shape):
            return tmp.enter_context(nc.sbuf_tensor(f"hgrn_{name}", shape, F32))

        lb = sb("lb", [P, 8, 2])
        zeros = sb("zeros", [P, S])
        G = sb("G", [P, 2, S])
        a = sb("a", [P, 2, S])
        b = sb("b", [P, 2, S])
        q_dec = sb("q_dec", [P, 2, S])
        k_dec = sb("k_dec", [P, 2, S])
        v_tok = sb("v_tok", [P, NT, 2 * P])
        A = sb("A", [P, 10, 2, 2, P])
        part = sb("part", [P, 2, 2, 2, P])
        q, f, key = y[:, HQ:HQ + 2, :], y[:, HF:HF + 2, :], y[:, HF:HF + 2, :]
        D_, ABS, LN, MIN, LP1, LP0, LOG_LB, LOG_1M = range(8)
        z0, z1 = vec[:, V1["lb"]:V1["lb"] + 2], vec[:, V1["lb"] + 2:V1["lb"] + 4]
        first = vec[:, V1["is_first"]:V1["is_first"] + 1]

        with stage(nc, "hgrn_gates", "steps", "acts", "to_act") as (block, s):
            @block.vector
            def _(dve):
                done = [0]

                def step(ins):
                    done[0] += 1
                    ins.then_inc(s["steps"], 1)
                    dve.wait_ge(s["steps"], done[0])

                step(nc.vector.tensor_tensor(lb[:, D_, :], z1, z0, ALU.subtract))
                step(nc.vector.scalar_tensor_tensor(out=lb[:, ABS, :], in0=lb[:, D_, :], scalar=-1.0, in1=lb[:, D_, :], op0=ALU.mult, op1=ALU.max))
                step(nc.vector.scalar_tensor_tensor(out=a[:], in0=f, scalar=-1.0, in1=f, op0=ALU.mult, op1=ALU.max))
                dve.sem_inc(s["to_act"], 1)
                step(nc.vector.memset(zeros[:], 0.0))
                dve.wait_ge(s["acts"], 4)
                step(nc.vector.tensor_scalar(lb[:, MIN, :], lb[:, D_, :], 0.0, None, ALU.min))
                step(nc.vector.tensor_tensor(lb[:, LP1, :], lb[:, MIN, :], lb[:, LN, :], ALU.subtract))
                step(nc.vector.tensor_tensor(lb[:, LP0, :], lb[:, LP1, :], lb[:, D_, :], ALU.subtract))
                step(nc.vector.tensor_scalar(lb[:, MIN, :], first.broadcast_to([P, 2]), -1.0, 1.0, ALU.mult, ALU.add))
                step(nc.vector.tensor_tensor(lb[:, LOG_1M, :], lb[:, LP0, :], lb[:, MIN, :], ALU.mult))
                step(nc.vector.tensor_tensor(lb[:, LP1, :], lb[:, LP1, :], lb[:, MIN, :], ALU.mult))
                step(nc.vector.scalar_tensor_tensor(out=lb[:, LOG_LB, :], in0=first.broadcast_to([P, 2]), scalar=NEG, in1=lb[:, LP1, :], op0=ALU.mult, op1=ALU.add))
                step(nc.vector.scalar_tensor_tensor(out=b[:], in0=f, scalar=0.0, in1=a[:], op0=ALU.min, op1=ALU.subtract))
                for k in range(2):
                    step(nc.vector.tensor_scalar(b[:, k, :], b[:, k, :], lb[:, LOG_1M, k:k + 1], None, ALU.add))
                for k in range(2):
                    step(nc.vector.tensor_scalar(a[:, k, :], b[:, k, :], lb[:, LOG_LB, k:k + 1], None, ALU.min))
                    step(nc.vector.tensor_scalar(G[:, k, :], b[:, k, :], lb[:, LOG_LB, k:k + 1], None, ALU.max))
                step(nc.vector.tensor_tensor(a[:], a[:], G[:], ALU.subtract))
                dve.sem_inc(s["to_act"], 1)
                dve.wait_ge(s["acts"], 9)
                step(nc.vector.tensor_tensor(b[:], G[:], a[:], ALU.add))
                for k in range(2):
                    step(nc.vector.tensor_tensor_scan(G[:, k, :], b[:, k, :], zeros[:], 0.0, ALU.add, ALU.add))
                    step(nc.vector.tensor_scalar(key[:, k, :], key[:, k, :], lb[:, MIN, k:k + 1], None, ALU.mult))

            @block.scalar
            def _(act):
                done = [0]

                def step(ins):
                    done[0] += 1
                    ins.then_inc(s["acts"], 1)
                    act.wait_ge(s["acts"], done[0])

                act.wait_ge(s["to_act"], 1)
                step(nc.scalar.activation(lb[:, LN, :], lb[:, ABS, :], ACT.Exp, scale=-1.0))
                step(nc.scalar.activation(a[:], a[:], ACT.Exp, scale=-1.0))
                step(nc.scalar.activation(lb[:, LN, :], lb[:, LN, :], ACT.Ln, bias=m.one[:, 0:1]))
                step(nc.scalar.activation(a[:], a[:], ACT.Ln, bias=m.one[:, 0:1]))
                act.wait_ge(s["to_act"], 2)
                step(nc.scalar.activation(a[:], a[:], ACT.Exp))
                step(nc.scalar.activation(lb[:, MIN, :], lb[:, LOG_1M, :], ACT.Exp))
                step(nc.scalar.activation(a[:], a[:], ACT.Ln, bias=m.one[:, 0:1]))
                step(nc.scalar.activation(key, f, ACT.Sigmoid, scale=-1.0))
                step(nc.scalar.activation(q, q, ACT.Silu))

        transpose_tiles(nc, "hgrn_v", m, y[:, HI:HI + 2, :], v_tok)

        diagonal = [(j, j) for j in range(NT)]
        across = [[(0, 1), (2, 3)], [(0, 2), (0, 3), (1, 2), (1, 3)]]
        place = {pair: n for n, pair in enumerate(diagonal + across[0] + across[1])}
        levels = [(0, diagonal)] + [(1 << n, diagonal) for n in range(HG_LEVELS)] + [(P, across[0]), (2 * P, across[1])]
        with stage(nc, "hgrn", "diffs_ready", "exp_ready", "q_ready", "k_ready", "scored", "level_scored", "masked", "added") as (block, s):
            def halves(ap, w, which):
                return ap.rearrange("p t (n two w) -> p (t n) two w", two=2, w=w)[:, :, which, :]

            def bank_of(block, parity):
                return block // 2 % 4 * 2 + parity

            def scores_of(block):
                at = bank_of(block, 0)
                return m.ps[:, at:at + 2, block % 2 * 2 * P:(block % 2 + 1) * 2 * P].rearrange("p a (b t) -> p a b t", b=2)

            def spread4(mask):
                return mask.unsqueeze(1).unsqueeze(1).broadcast_to([P, 2, 2, P])

            def middle(w):
                g = halves(G[:], w, 0)[:, :, w - 1:w]
                return g.broadcast_to([P, S // w, w])

            @block.vector
            def _(dve):
                blocks = 0
                for n, (w, pairs) in enumerate(levels):
                    if n >= 1:
                        if n >= 2:
                            dve.wait_ge(s["k_ready"], n - 1)
                            dve.wait_ge(s["q_ready"], n - 1)
                        nc.vector.tensor_tensor(halves(b[:], w, 0), middle(w), halves(G[:], w, 0), ALU.subtract).then_inc(s["diffs_ready"], 1)
                        nc.vector.tensor_tensor(halves(b[:], w, 1), halves(G[:], w, 1), middle(w), ALU.subtract).then_inc(s["diffs_ready"], 1)
                        dve.wait_ge(s["exp_ready"], n)
                        if n >= 2:
                            dve.wait_ge(s["level_scored"], n)
                        nc.vector.tensor_tensor(q_dec[:], q, b[:], ALU.mult).then_inc(s["q_ready"], 1)
                    for x, pair in enumerate(pairs):
                        dve.wait_ge(s["scored"], blocks // 2 * 2 + 2)
                        scores = scores_of(blocks)
                        into = A[:, place[pair], :, :, :]
                        if w == 0:
                            ins = nc.vector.tensor_tensor(into, scores, spread4(m.ident), ALU.mult)
                        elif w >= P:
                            ins = nc.vector.tensor_copy(into, scores)
                        else:
                            if blocks >= 6:
                                dve.wait_ge(s["added"], blocks - 5)
                            mask = m.masks[:, MASKS["levels"] + (n - 1) * P:MASKS["levels"] + n * P]
                            ins = nc.vector.tensor_tensor(part[:, blocks % 2, :, :, :], scores, spread4(mask), ALU.mult)
                        ins.then_inc(s["masked"], 1)
                        blocks += 1

            @block.gpsimd
            def _(pool):
                blocks = 4
                for n, (w, pairs) in enumerate(levels):
                    if n >= 1:
                        pool.wait_ge(s["exp_ready"], n)
                        if n >= 2:
                            pool.wait_ge(s["level_scored"], n)
                        nc.gpsimd.tensor_tensor(k_dec[:], key, b[:], ALU.mult).then_inc(s["k_ready"], 1)
                    if 1 <= n <= HG_LEVELS:
                        for x, pair in enumerate(pairs):
                            pool.wait_ge(s["masked"], blocks + 1)
                            if blocks >= 8:
                                pool.wait_ge(s["added"], blocks - 7)
                            into = A[:, place[pair], :, :, :].rearrange("p a b t -> p (a b t)")
                            more = part[:, blocks % 2, :, :, :].rearrange("p a b t -> p (a b t)")
                            nc.gpsimd.tensor_tensor(into, into, more, ALU.add).then_inc(s["added"], 1)
                            blocks += 1

            @block.scalar
            def _(act):
                for n in range(1, len(levels)):
                    act.wait_ge(s["diffs_ready"], 2 * n)
                    nc.scalar.activation(b[:], b[:], ACT.Exp).then_inc(s["exp_ready"], 1)

            @block.tensor
            def _(pe):
                blocks = 0
                for n, (w, pairs) in enumerate(levels):
                    kk, qq = (k_dec, q_dec) if n else (key, q)
                    if n >= 1:
                        pe.wait_ge(s["q_ready"], n)
                        pe.wait_ge(s["k_ready"], n)
                    for sT, lT in pairs:
                        if blocks >= 8 and blocks % 2 == 0:
                            pe.wait_ge(s["masked"], blocks - 6)
                        for h in range(4):
                            lo = (h % 2) * HD
                            at = (blocks % 2 * 2 + h // 2) * P
                            mm = nc.tensor.matmul(m.ps[:, bank_of(blocks, h % 2), at:at + P], kk[lo:lo + HD, h // 2, sT * P:(sT + 1) * P],
                                                  qq[lo:lo + HD, h // 2, lT * P:(lT + 1) * P], start=True, stop=True)
                        mm.then_inc(s["scored"], 1)
                        blocks += 1
                    pe.wait_ge(s["scored"], blocks)
                    pe.sem_inc(s["level_scored"], 1)

        with stage(nc, "hgrn_out", "summed", "copied") as (block, s):
            @block.tensor
            def _(pe):
                for h in range(4):
                    for lT in range(NT):
                        for sT in range(lT + 1):
                            mm = nc.tensor.matmul(m.ps[(h % 2) * HD:(h % 2 + 1) * HD, h // 2, lT * P:(lT + 1) * P],
                                                  v_tok[:, sT, h * HD:(h + 1) * HD], A[:, place[sT, lT], h % 2, h // 2, :],
                                                  start=(sT == 0), stop=(sT == lT))
                mm.then_inc(s["summed"], 1)

            @block.vector
            def _(dve):
                dve.wait_ge(s["summed"], 1)
                nc.vector.tensor_copy(a[:], m.ps[:, 0:2, :]).then_inc(s["copied"], 1)

        heads_norm_gate(nc, "hgrn_norm", m, a[:], vec[:, V1["h_g"]:V1["h_g"] + 2], y[:, HG:HG + 2, :], ACT.Silu, dst)


def band_attention(nc, name, m, q, k, v, sinks, bands, reach, dst):
    pairs = k.shape[1]
    nr = len(reach)
    with ExitStack() as tmp:
        def sb(name_, shape):
            return tmp.enter_context(nc.sbuf_tensor(f"{name}_{name_}", shape, F32))

        qs = sb("qs", [P, 4, S])
        k_dup = sb("k_dup", [P, 2, S])
        vs = sb("vs", [P, S])
        v_tok = sb("v_tok", [P, NT, P])
        p = sb("p", [P, 3, nr * P])
        pt = sb("pt", [P, 2, nr * P])
        stat = sb("stat", [P, 8, 8])
        sink = sb("sink", [P, 8])
        MAX, NEG_MAX, SUM, SINK, DEN, REC = range(6)
        units = [(h, b) for h in range(8) for b in range(NT)]
        N = len(units)

        def tiles_of(b):
            return [b + r for r in reach if 0 <= b + r < NT]

        def width(b):
            return len(tiles_of(b)) * P

        def bands_of(b):
            at = next(x for x, r in enumerate(reach) if 0 <= b + r)
            return bands[:, at * P:at * P + width(b)]

        with stage(nc, name, "copied", "v_turned", "v_ready", "scored", "biased", "max_ready", "neg_ready",
                   "exp_ready", "sink_ready", "den_ready", "rec_ready", "normed", "turned", "pt_ready", "summed", "out") as (block, s):
            @block.vector
            def _(dve):
                with dve.Fori(0, pairs) as g:
                    nc.vector.tensor_copy(qs[:], q[:, bass.ds(g * 4, 4), :]).then_inc(s["copied"], 1)
                    for half in range(2):
                        for to in range(2):
                            nc.vector.tensor_copy(k_dup[to * HD:(to + 1) * HD, half:half + 1, :],
                                                  k[half * HD:(half + 1) * HD, bass.ds(g, 1), :]).then_inc(s["copied"], 1)
                    nc.vector.tensor_copy(vs[:], tile_of(v, g)).then_inc(s["copied"], 1)
                    nc.vector.tensor_copy(sink[:], sinks[:, bass.ds(g * 8, 8)]).then_inc(s["copied"], 1)
                    dve.wait_ge(s["v_turned"], g * NT + NT)
                    for b in range(NT):
                        nc.vector.tensor_copy(v_tok[:, b, :], m.ps[:, 7, b * P:(b + 1) * P]).then_inc(s["v_ready"], 1)

                    def finish(n):
                        h, b = units[n]
                        st = stat[:, n % 8, :]
                        dve.wait_ge(s["exp_ready"], g * N + (n + 1))
                        dve.wait_ge(s["sink_ready"], g * N + (n + 1))
                        nc.vector.tensor_tensor(st[:, DEN:DEN + 1], st[:, SUM:SUM + 1], st[:, SINK:SINK + 1], ALU.add).then_inc(s["den_ready"], 1)
                        dve.wait_ge(s["den_ready"], g * N + (n + 1))
                        nc.vector.reciprocal(st[:, REC:REC + 1], st[:, DEN:DEN + 1]).then_inc(s["rec_ready"], 1)
                        dve.wait_ge(s["rec_ready"], g * N + (n + 1))
                        nc.vector.tensor_scalar(p[:, n % 3, 0:width(b)], p[:, n % 3, 0:width(b)], st[:, REC:REC + 1], None, ALU.mult).then_inc(s["normed"], 1)

                    for n, (h, b) in enumerate(units):
                        st = stat[:, n % 8, :]
                        dve.wait_ge(s["scored"], g * N + (n + 1))
                        if n >= 3:
                            dve.wait_ge(s["turned"], g * N + (n - 2))
                        nc.vector.scalar_tensor_tensor(out=p[:, n % 3, 0:width(b)], in0=m.ps[:, n % 2, 0:width(b)], scalar=HD ** -0.5,
                                                       in1=bands_of(b), op0=ALU.mult, op1=ALU.add).then_inc(s["biased"], 1)
                        dve.wait_ge(s["biased"], g * N + (n + 1))
                        nc.vector.tensor_reduce(st[:, MAX:MAX + 1], p[:, n % 3, 0:width(b)], AX_X, ALU.max).then_inc(s["max_ready"], 1)
                        dve.wait_ge(s["max_ready"], g * N + (n + 1))
                        if n == 0:
                            dve.wait_ge(s["copied"], g * 7 + 7)
                        nc.vector.tensor_scalar(st[:, NEG_MAX:NEG_MAX + 1], st[:, MAX:MAX + 1], sink[:, h:h + 1], -1.0, ALU.max, ALU.mult).then_inc(s["neg_ready"], 1)
                        if n >= 1:
                            finish(n - 1)
                    finish(N - 1)
                    dve.wait_ge(s["out"], g * 4 + 4)

            @block.scalar
            def _(act):
                with act.Fori(0, pairs) as g:
                    def take(n):
                        h, b = units[n]
                        act.wait_ge(s["turned"], g * N + (n + 1))
                        if n >= 2:
                            act.wait_ge(s["summed"], g * N + (n - 1))
                        nc.scalar.activation(pt[:, n % 2, 0:width(b)], m.ps[:, 2 + n % 2, 0:width(b)], ACT.Copy).then_inc(s["pt_ready"], 1)
                        if b == NT - 1 and h % 2 == 1 and h >= 3:
                            out(h // 2 - 1)

                    def out(pair):
                        act.wait_ge(s["summed"], g * N + (pair + 1) * 2 * NT)
                        nc.scalar.activation(tile_of(dst, g * 4 + pair), m.ps[:, 4 + pair % 2, :], ACT.Copy).then_inc(s["out"], 1)

                    for n, (h, b) in enumerate(units):
                        st = stat[:, n % 8, :]
                        act.wait_ge(s["neg_ready"], g * N + (n + 1))
                        nc.scalar.activation(p[:, n % 3, 0:width(b)], p[:, n % 3, 0:width(b)], ACT.Exp, bias=st[:, NEG_MAX:NEG_MAX + 1],
                                             accum_out=st[:, SUM:SUM + 1]).then_inc(s["exp_ready"], 1)
                        nc.scalar.activation(st[:, SINK:SINK + 1], sink[:, h:h + 1], ACT.Exp, bias=st[:, NEG_MAX:NEG_MAX + 1]).then_inc(s["sink_ready"], 1)
                        if n >= 2:
                            take(n - 2)
                    take(N - 2)
                    take(N - 1)
                    out(3)

            @block.tensor
            def _(pe):
                with pe.Fori(0, pairs) as g:
                    pe.wait_ge(s["copied"], g * 7 + 7)
                    for b in range(NT):
                        nc.tensor.transpose(m.ps[:, 7, b * P:(b + 1) * P], vs[:, b * P:(b + 1) * P], m.ident).then_inc(s["v_turned"], 1)

                    def turn(n):
                        h, b = units[n]
                        pe.wait_ge(s["normed"], g * N + (n + 1))
                        if n >= 2:
                            pe.wait_ge(s["pt_ready"], g * N + (n - 1))
                        for x in range(len(tiles_of(b))):
                            mm = nc.tensor.transpose(m.ps[:, 2 + n % 2, x * P:(x + 1) * P], p[:, n % 3, x * P:(x + 1) * P], m.ident)
                        mm.then_inc(s["turned"], 1)

                    def outputs(n):
                        h, b = units[n]
                        pe.wait_ge(s["pt_ready"], g * N + (n + 1))
                        if n == 0:
                            pe.wait_ge(s["v_ready"], g * NT + NT)
                        if h % 2 == 0 and b == 0 and h >= 4:
                            pe.wait_ge(s["out"], g * 4 + (h // 2 - 1))
                        head = (h // 4) * HD
                        for x, t in enumerate(tiles_of(b)):
                            mm = nc.tensor.matmul(m.ps[(h % 2) * HD:(h % 2 + 1) * HD, 4 + h // 2 % 2, b * P:(b + 1) * P],
                                                  v_tok[:, t, head:head + HD], pt[:, n % 2, x * P:(x + 1) * P],
                                                  start=(x == 0), stop=(x == len(tiles_of(b)) - 1))
                        mm.then_inc(s["summed"], 1)

                    for n, (h, b) in enumerate(units):
                        lo = (h % 2) * HD
                        if n >= 2:
                            pe.wait_ge(s["biased"], g * N + (n - 1))
                        t = tiles_of(b)
                        nc.tensor.matmul(m.ps[:, n % 2, 0:width(b)], qs[lo:lo + HD, h // 2, b * P:(b + 1) * P],
                                         k_dup[lo:lo + HD, h // 4, t[0] * P:(t[-1] + 1) * P], start=True, stop=True).then_inc(s["scored"], 1)
                        if n >= 2:
                            turn(n - 2)
                        if n >= 3:
                            outputs(n - 3)
                    turn(N - 2)
                    outputs(N - 3)
                    turn(N - 1)
                    outputs(N - 2)
                    outputs(N - 1)


def first_block(nc, m, a, layer_count=DEPTH):
    with ExitStack() as held:
        def sb(name, shape):
            return held.enter_context(nc.sbuf_tensor(f"first_{name}", shape, F32))

        big = sb("big", [P, FFT, S])
        vec = sb("vec", [P, V1_W])
        m.sin = sb("sin", [P, S])
        m.cos = sb("cos", [P, S])
        m.masks = sb("masks", [P, MASKS_W])
        bands = sb("bands", [P, BANDS1_W])
        gates = sb("gates", [P, S])
        y = big[:, 0:NIN, :]
        load(nc, "first_tables", [(m.masks[:], a["masks"]), (bands[:], a["bands1"])])
        rope_table(nc, "rope1", m, a["positions"])
        with nc.Fori(0, layer_count) as layer:
            load(nc, "layer_vec", [(vec[:], row_of(a["vec1"], layer))])
            norm(nc, "in_norm", m, m.x, vec[:, V1["in_g"]:V1["in_g"] + DT], m.h)
            linear(nc, "in_gates", m, a["w_gates"], layer, lambda k: m.h[:, k, :], 1, 1, DT, 1,
                   on_act=to_tiles(nc, m, gates[:].unsqueeze(1), 1, ACT.Identity, vec[:, V1["b_i"]:V1["b_i"] + 1]))
            linear(nc, "in_proj", m, a["w_in"], layer * NIN, lambda k: m.h[:, k, :], NIN, 1, DT, 2,
                   on_act=to_tiles(nc, m, y, 2, ACT.Identity, vec[:, V1["b_in"]:V1["b_in"] + NIN]))
            conv_silu(nc, m, y[:, MQ:MQ + 4, :], vec)
            mlstm(nc, m, vec, y, gates, m.h[:, 0:2, :])
            hgrn(nc, m, vec, y, m.h[:, 2:4, :])
            heads_norm_rope(nc, "q1", m, y[:, SQ:SQ + 4, :], vec[:, V1["q_g"]:V1["q_g"] + 1])
            heads_norm_rope(nc, "k1", m, y[:, SK:SK + 1, :], vec[:, V1["k_g"]:V1["k_g"] + 1])
            band_attention(nc, "swa1", m, y[:, SQ:SQ + 4, :], y[:, SK:SK + 1, :], y[:, SV:SV + 1, :],
                           vec[:, V1["sinks"]:V1["sinks"] + 8], bands, (-1, 0), m.h[:, 4:8, :])
            linear(nc, "out1", m, a["w_out"], layer * DT, lambda k: m.h[:, k, :], DT, 1, DT, 4, on_dve=add_to_x(nc, m, 4))

            norm(nc, "mlp_norm", m, m.x, vec[:, V1["mlp_g"]:V1["mlp_g"] + DT], m.h)

            def squared_relu(dve, i, s, products):
                for u in range(4):
                    dve.wait_ge(s["slots_used"], products(u))
                    t = tile_of(big, i * 4 + u)
                    nc.vector.tensor_scalar(t, m.ps[:, u, :], 0.0, None, ALU.max).then_inc(s["relu_ready"], 1)
                    dve.wait_ge(s["relu_ready"], i * 4 + (u + 1))
                    nc.vector.tensor_tensor(t, t, t, ALU.mult).then_inc(s["banks_free"], 1)

            linear(nc, "up1", m, a["w_up"], layer * FFT, lambda k: m.h[:, k, :], FFT, 1, DT, 4, ("relu_ready",), on_dve=squared_relu)
            linear(nc, "down1", m, a["w_down"], layer * (DT * 4), lambda k: big[:, k, :], DT, 4, DT, 1, on_dve=add_to_x(nc, m, 1))

            norm(nc, "ple_norm", m, m.x, vec[:, V1["ple_g"]:V1["ple_g"] + DT], m.h)
            gate, e, pt = big[:, 0:DT, :], big[:, DT:2 * DT, :], big[:, 2 * DT:2 * DT + PLE // P, :]
            linear(nc, "ple_gate", m, a["w_gate"], layer * DT, lambda k: m.h[:, k, :], DT, 1, DT, 4, on_act=to_tiles(nc, m, gate, 4, ACT.Sigmoid))
            load(nc, "ple_in", [(pt, a["p_t"][bass.ds(layer, 1)].rearrange("a p k n -> p (a k) n"))])
            linear(nc, "ple_proj", m, a["w_ple"], layer * DT, lambda k: pt[:, k, :], DT, 1, PLE // P, 4, on_act=to_tiles(nc, m, e, 4))
            norm(nc, "post_norm", m, e, vec[:, V1["post_g"]:V1["post_g"] + DT], e)
            with stage(nc, "ple_add", "gated", "added") as (block, s):
                @block.vector
                def _(dve):
                    nc.vector.tensor_tensor(e, e, gate, ALU.mult).then_inc(s["gated"], 1)
                    dve.wait_ge(s["gated"], 1)
                    nc.vector.tensor_tensor(m.x[:], m.x[:], e, ALU.add).then_inc(s["added"], 1)


def conv_ffn(nc, m, a, vec, layer):
    with ExitStack() as tmp:
        def sb(name, shape):
            return tmp.enter_context(nc.sbuf_tensor(f"ffn{layer}_{name}", shape, F32))

        hidden = sb("hidden", [P, GT, S])
        padded = sb("padded", [P, 4, S + 2])
        acc = sb("acc", [P, 4, S])
        with stage(nc, f"ffn{layer}_pad", "zeroed") as (block, s):
            @block.vector
            def _(dve):
                nc.vector.memset(padded[:, :, 0:1], 0.0).then_inc(s["zeroed"], 1)
                nc.vector.memset(padded[:, :, S + 1:S + 2], 0.0).then_inc(s["zeroed"], 1)

        conv_up(nc, m, a, vec, layer, hidden, padded, acc)
        linear(nc, f"ffn{layer}_down", m, a["w_ffn_down"], layer * (DT * 2), lambda k: hidden[:, k, :], DT, 2, GT // 2, 2, on_dve=add_to_x(nc, m, 2))


def conv_up(nc, m, a, vec, layer, hidden, padded, acc):
    def on_act(act, i, s, products):
        for u in range(4):
            act.wait_ge(s["slots_used"], products(u))
            act.wait_ge(s["buffers_free"], i * 4 + (u + 1))
            nc.scalar.activation(padded[:, u, 1:S + 1], m.ps[:, u, :], ACT.Copy).then_inc(s["banks_free"], 1)
            if u % 2 == 1:
                act.wait_ge(s["gates_convolved"], i * 2 + (u // 2 + 1))
                nc.scalar.activation(acc[:, u - 1, :], acc[:, u - 1, :], ACT.Silu).then_inc(s["gates_ready"], 1)

    def on_dve(dve, i, s, products):
        for u in range(4):
            dve.wait_ge(s["banks_free"], i * 4 + (4 + u + 1))
            last = (s["gates_convolved"], s["values_convolved"])[u % 2]
            for t in range(3):
                col = vec[:, bass.ds(i * 4 + (V2["conv_w"] + t * 2 * GT + u), 1)]
                if t == 0:
                    bias = vec[:, bass.ds(i * 4 + (V2["conv_b"] + u), 1)]
                    ins = nc.vector.tensor_scalar(acc[:, u, :], padded[:, u, 0:S], col, bias, ALU.mult, ALU.add)
                else:
                    dve.wait_ge(s["taps"], i * 8 + (2 * u + t))
                    ins = nc.vector.scalar_tensor_tensor(out=acc[:, u, :], in0=padded[:, u, t:t + S], scalar=col, in1=acc[:, u, :],
                                                         op0=ALU.mult, op1=ALU.add)
                ins.then_inc(s["taps"] if t < 2 else last, 1)
            dve.wait_ge(last, i * 2 + (u // 2 + 1))
            dve.sem_inc(s["buffers_free"], 1)
            if u % 2 == 1:
                dve.wait_ge(s["gates_ready"], i * 2 + (u // 2 + 1))
                nc.vector.tensor_tensor(tile_of(hidden, i * 2 + u // 2), acc[:, u - 1, :], acc[:, u, :], ALU.mult).then_inc(s["multiplied"], 1)
                dve.wait_ge(s["multiplied"], i * 2 + (u // 2 + 1))

    linear(nc, f"ffn{layer}_up", m, a["w_ffn_up"], layer * (2 * GT), lambda k: m.h[:, k, :], 2 * GT, 1, DT, 4,
           ("buffers_free", "gates_convolved", "values_convolved", "taps", "gates_ready", "multiplied"), on_act=on_act, on_dve=on_dve,
           at_start=lambda pe, s: pe.sem_inc(s["buffers_free"], 4))


R_, K_, V_, SW, AA, G_ = 0, 1, 2, 3, 5, 7


def rwkv_inputs(nc, m, a, vec, buf, keep):
    with ExitStack() as tmp:
        def sb(name, shape):
            return tmp.enter_context(nc.sbuf_tensor(f"rwkv_{name}", shape, F32))

        xx = m.sq
        mixed = sb("mixed", [P, DT, S])
        low = sb("low", [P, 2, S])
        wide = sb("wide", [P, D])
        with stage(nc, "rwkv_xx", "steps") as (block, s):
            @block.vector
            def _(dve):
                nc.vector.tensor_tensor(xx[:, :, 1:S - 1], m.h[:, :, 0:S - 2], m.h[:, :, 2:S], ALU.add).then_inc(s["steps"], 1)
                nc.vector.tensor_copy(xx[:, :, 0:1], m.h[:, :, 1:2]).then_inc(s["steps"], 1)
                nc.vector.tensor_copy(xx[:, :, S - 1:S], m.h[:, :, S - 2:S - 1]).then_inc(s["steps"], 1)
                dve.wait_ge(s["steps"], 3)
                nc.vector.scalar_tensor_tensor(out=xx[:], in0=xx[:], scalar=0.5, in1=m.h[:], op0=ALU.mult, op1=ALU.subtract).then_inc(s["steps"], 1)

        def mix(i):
            with stage(nc, f"rwkv_mix{i}", "mixed") as (block, s):
                @block.vector
                def _(dve):
                    for k in range(DT):
                        mu = vec[:, VR["mu"] + i * DT + k:VR["mu"] + i * DT + k + 1]
                        nc.vector.scalar_tensor_tensor(out=mixed[:, k, :], in0=xx[:, k, :], scalar=mu, in1=m.h[:, k, :],
                                                       op0=ALU.mult, op1=ALU.add).then_inc(s["mixed"], 1)

        def store(what):
            with stage(nc, f"rwkv_store{what}", "stored") as (block, s):
                @block.sync
                def _(sp):
                    sp.dma_start(keep[what].rearrange("k p n -> p k n"), buf[:]).then_inc(s["stored"], 16)
                    sp.wait_ge(s["stored"], 16)

        def from_mixed(k):
            return mixed[:, k, :]

        for what, i, w in ((R_, 0, a["w_r"]), (K_, 2, a["w_k"]), (V_, 3, a["w_v"])):
            mix(i)
            linear(nc, f"rwkv_p{what}", m, w, 0, from_mixed, DT, 1, DT, 4, on_act=to_tiles(nc, m, buf, 4))
            store(what)

        for what, i, w1, w2, bias, func in ((SW, 1, a["w_w1"], a["w_w2"], VR["w0"], ACT.Tanh), (AA, 4, a["w_a1"], a["w_a2"], VR["a0"], ACT.Copy)):
            mix(i)
            linear(nc, f"rwkv_low{what}", m, w1, 0, from_mixed, 1, 1, DT, 1, on_act=to_tiles(nc, m, low, 1, func))
            load(nc, f"rwkv_wide{what}", [(wide[:], w2)])
            for d in range(2):
                lo = d * HD
                with stage(nc, f"rwkv_back{what}{d}", "product_ready", "taken") as (block, s):
                    @block.tensor
                    def _(pe):
                        for k in range(DT):
                            nc.tensor.matmul(m.ps[:, k, :], wide[lo:lo + HD, k * P:(k + 1) * P], low[lo:lo + HD, 0, :], start=True, stop=True).then_inc(s["product_ready"], 1)

                    @block.scalar
                    def _(act):
                        for k in range(DT):
                            act.wait_ge(s["product_ready"], k + 1)
                            at = bias + d * DT + k
                            nc.scalar.activation(buf[:, k, :], m.ps[:, k, :], ACT.Sigmoid, bias=vec[:, at:at + 1]).then_inc(s["taken"], 1)
                store(what + d)

        mix(5)
        linear(nc, "rwkv_g1", m, a["w_g1"], 0, from_mixed, 2, 1, DT, 2, on_act=to_tiles(nc, m, low, 2, ACT.Sigmoid))
        linear(nc, "rwkv_g2", m, a["w_g2"], 0, lambda k: low[:, k, :], DT, 1, 2, 4, on_act=to_tiles(nc, m, buf, 4))
        store(G_)


def rwkv_heads(nc, m, a, vec, keep):
    with ExitStack() as tmp:
        def sb(name, shape):
            return tmp.enter_context(nc.sbuf_tensor(f"heads_{name}", shape, F32))

        L = m.sq
        masks = sb("masks", [P, RMASKS_W])
        mask4 = sb("mask4", [P, 4, P])
        restart = sb("restart", [P, S])
        par = sb("par", [P, 5, 1])
        AR = sb("AR", [P, 2, NT, 2, P])
        BK = sb("BK", [P, 2, 2, S])
        V2_ = sb("V2", [P, S])
        bonus = sb("bonus", [P, S])
        tok = sb("tok", [P, 2, NT, 4, P])
        M = sb("M", [P, NT, 4, 4, P])
        X = sb("X", [P, NT, 4, P])
        XT = sb("XT", [P, NT, 4, P])
        T1 = sb("T1", [P, 2, 4, P])
        NM = sb("NM", [P, 2, 4, P])
        p_end = sb("p_end", [P, 2, NT, 2])
        state = sb("state", [P, 2, HD])
        grown = sb("grown", [P, 2, HD])
        gn_eps = sb("gn_eps", [P, 1])
        t16 = M[:].rearrange("p t i k n -> p (t i) (k n)")
        KR, KK, KD, B_, GS, PM, EG, EN, EP = 0, 1, 2, 4, 6, 8, 10, 12, 14
        WT = X
        ZV = T1[:].rearrange("p a i n -> p (a i n)").rearrange("p (t i e) -> p t i e", t=NT, i=4)
        U0 = NM[:].rearrange("p a i n -> p (a i n)").rearrange("p (t i e) -> p t i e", t=NT, i=4)
        U = sb("U", [P, NT, 4, HD])
        KV = sb("KV", [P, 2, NT, 2, HD])

        load(nc, "heads_tables", [(masks[:], a["rmasks"]), (restart[:], a["restart"])])
        with stage(nc, "heads_mask4", "copied") as (block, s):
            @block.vector
            def _(dve):
                for k in range(4):
                    nc.vector.tensor_copy(mask4[:, k, :], masks[:, RMASKS["before"] + (k % 2) * P:RMASKS["before"] + (k % 2 + 1) * P]).then_inc(s["copied"], 1)
                nc.vector.memset(gn_eps[:], 64e-5).then_inc(s["copied"], 1)

        def turned(ap, d):
            return ap if d == 0 else ap[:, ::-1]

        with nc.Fori(0, DT) as c:
            with stage(nc, "heads_in", "loaded") as (block, s):
                @block.sync
                def _(sp):
                    for w in range(8):
                        sp.dma_start(L[:, w, :], row_of(keep[w], c)).then_inc(s["loaded"], 16)
                    sp.wait_ge(s["loaded"], 8 * 16)

            with stage(nc, "heads_scale", "steps", "squares_ready", "kk_sums", "root_ready", "sums_ready", "exps_ready", "bonus_in", "bonus_sums", "to_square") as (block, s):
                @block.vector
                def _(dve):
                    done = [0]

                    def step(ins):
                        done[0] += 1
                        ins.then_inc(s["steps"], 1)
                        dve.wait_ge(s["steps"], done[0])

                    params = vec[:, VR["k_k"]:VR["k_k"] + 5 * DT].rearrange("p (w c) -> p w c", c=DT)
                    step(nc.vector.tensor_copy(par[:], params[:, :, bass.ds(c, 1)]))
                    step(nc.vector.tensor_scalar(t16[:, KR, :], L[:, K_, :], par[:, 0, :], None, ALU.mult))
                    dve.sem_inc(s["to_square"], 1)
                    for d in range(2):
                        sw = turned(L[:, SW + d, :], d)
                        step(nc.vector.tensor_tensor_scan(t16[:, GS + d, :], restart[:], sw, 0.0, ALU.mult, ALU.add))
                        step(nc.vector.tensor_tensor(t16[:, PM + d, :], t16[:, GS + d, :], sw, ALU.subtract))
                        dve.sem_inc(s["sums_ready"], 1)
                        step(nc.vector.tensor_scalar(t16[:, KD + d, :], L[:, AA + d, :], -1.0, par[:, 1, :], ALU.add, ALU.mult))
                        step(nc.vector.scalar_tensor_tensor(out=t16[:, KD + d, :], in0=t16[:, KD + d, :], scalar=1.0, in1=L[:, K_, :], op0=ALU.add, op1=ALU.mult))
                    step(nc.vector.tensor_tensor(bonus[:], t16[:, KD, :], t16[:, KD + 1, :], ALU.add))
                    step(nc.vector.scalar_tensor_tensor(out=bonus[:], in0=bonus[:], scalar=par[:, 2, :], in1=L[:, R_, :], op0=ALU.mult, op1=ALU.mult))
                    dve.sem_inc(s["bonus_in"], 1)
                    dve.wait_ge(s["root_ready"], 1)
                    step(nc.vector.tensor_scalar(t16[:, KK, :], t16[:, KK, :], 1e-12, None, ALU.max))
                    step(nc.vector.reciprocal(t16[:, KK, :], t16[:, KK, :]))
                    step(nc.vector.tensor_tensor(t16[:, KK, :], t16[:, KK, :], t16[:, KR, :], ALU.mult))
                    step(nc.vector.tensor_copy(V2_[:], L[:, V_, ::-1]))
                    for d in range(2):
                        step(nc.vector.tensor_tensor(t16[:, B_ + d, :], t16[:, KK, :], L[:, AA + d, :], ALU.mult))
                        dve.wait_ge(s["exps_ready"], 3 * d + 3)
                        def by_tile(ap):
                            return ap.rearrange("p (t n) -> p t n", n=P)
                        step(nc.vector.tensor_tensor(AR[:, d, :, 1, :], by_tile(turned(L[:, R_, :], d)), by_tile(t16[:, EG + d, :]), ALU.mult))
                        step(nc.vector.scalar_tensor_tensor(out=AR[:, d, :, 0, :], in0=by_tile(turned(t16[:, KK, :], d)), scalar=-1.0,
                                                            in1=by_tile(t16[:, EP + d, :]), op0=ALU.mult, op1=ALU.mult))
                        step(nc.vector.tensor_tensor(BK[:, 0, d, :], turned(t16[:, B_ + d, :], d), t16[:, EN + d, :], ALU.mult))
                        step(nc.vector.tensor_tensor(BK[:, 1, d, :], turned(t16[:, KD + d, :], d), t16[:, EN + d, :], ALU.mult))
                        ends = t16[:, EG + d, RW_CHUNK - 1::RW_CHUNK].rearrange("p (t u) -> p u t", u=2)
                        step(nc.vector.tensor_copy(p_end[:, :, :, d], ends))
                    dve.wait_ge(s["bonus_sums"], 1)
                    step(nc.vector.tensor_tensor(bonus[:], m.ps[:, 1, :], L[:, V_, :], ALU.mult))

                @block.scalar
                def _(act):
                    act.wait_ge(s["to_square"], 1)
                    nc.scalar.activation(t16[:, KK, :], t16[:, KR, :], ACT.Square).then_inc(s["squares_ready"], 1)
                    act.wait_ge(s["kk_sums"], 1)
                    nc.scalar.activation(t16[:, KK, :], m.ps[:, 0, :], ACT.Sqrt).then_inc(s["root_ready"], 1)
                    for d in range(2):
                        act.wait_ge(s["sums_ready"], d + 1)
                        nc.scalar.activation(t16[:, EG + d, :], t16[:, GS + d, :], ACT.Exp, scale=-DECAY_SCALE).then_inc(s["exps_ready"], 1)
                        nc.scalar.activation(t16[:, EN + d, :], t16[:, GS + d, :], ACT.Exp, scale=DECAY_SCALE).then_inc(s["exps_ready"], 1)
                        nc.scalar.activation(t16[:, EP + d, :], t16[:, PM + d, :], ACT.Exp, scale=-DECAY_SCALE).then_inc(s["exps_ready"], 1)

                @block.tensor
                def _(pe):
                    pe.wait_ge(s["squares_ready"], 1)
                    nc.tensor.matmul(m.ps[:, 0, :], m.head_ones, t16[:, KK, :], start=True, stop=True).then_inc(s["kk_sums"], 1)
                    pe.wait_ge(s["bonus_in"], 1)
                    nc.tensor.matmul(m.ps[:, 1, :], m.head_ones, bonus[:], start=True, stop=True).then_inc(s["bonus_sums"], 1)

            with stage(nc, "heads_turn", "turned", "copied_act", "copied_dve") as (block, s):
                @block.tensor
                def _(pe):
                    for n in range(8):
                        d, t = n // NT, n % NT
                        at = slice(t * P, (t + 1) * P)
                        vv = L[:, V_, at] if d == 0 else V2_[:, at]
                        for kind, src in enumerate((AR[:, d, t, 0, :], BK[:, 0, d, at], BK[:, 1, d, at], vv)):
                            mm = nc.tensor.transpose(m.ps[:, n, kind * P:(kind + 1) * P], src, m.ident)
                        mm.then_inc(s["turned"], 1)

                def copies(eng, which):
                    for n in range(which, 8, 2):
                        d, t = n // NT, n % NT
                        eng.wait_ge(s["turned"], n + 1)
                        into = tok[:, d, t, :, :].rearrange("p k n -> p (k n)")
                        if which:
                            nc.scalar.activation(into, m.ps[:, n, :], ACT.Copy).then_inc(s["copied_act"], 1)
                        else:
                            nc.vector.tensor_copy(into, m.ps[:, n, :]).then_inc(s["copied_dve"], 1)

                @block.scalar
                def _(act):
                    copies(act, 1)

                @block.vector
                def _(dve):
                    copies(dve, 0)

            with stage(nc, "heads_grams", "products", "masked", "started", "steps") as (block, s):
                @block.tensor
                def _(pe):
                    for t in range(NT):
                        if t >= 1:
                            pe.wait_ge(s["masked"], 6 * t)
                        at = slice(t * P, (t + 1) * P)
                        for inst in range(4):
                            hh, d = inst // 2, inst % 2
                            lo = slice(hh * HD, (hh + 1) * HD)
                            ar = AR[lo, d, t, :, :].rearrange("p a n -> p (a n)")
                            nc.tensor.matmul(m.ps[:, inst, 0:2 * P], BK[lo, 0, d, at], ar, start=True, stop=True)
                            nc.tensor.matmul(m.ps[:, inst, 2 * P:4 * P], BK[lo, 1, d, at], ar, start=True, stop=True)
                            mm = nc.tensor.matmul(m.ps[:, 4 + hh, d * P:(d + 1) * P], AR[lo, d, t, 0, :], BK[lo, 0, d, at], start=True, stop=True)
                        mm.then_inc(s["products"], 1)

                @block.vector
                def _(dve):
                    for t in range(NT):
                        dve.wait_ge(s["products"], t + 1)
                        for inst in range(4):
                            nc.vector.tensor_tensor(M[:, t, inst, :, :], m.ps[:, inst, :].rearrange("p (k n) -> p k n", k=4), mask4[:], ALU.mult).then_inc(s["masked"], 1)
                        for hh in range(2):
                            nc.vector.tensor_tensor(X[:, t, 2 * hh:2 * hh + 2, :], m.ps[:, 4 + hh, 0:2 * P].rearrange("p (d n) -> p d n", d=2),
                                                    spread(masks[:, RMASKS["pair"]:RMASKS["pair"] + P], 2), ALU.mult).then_inc(s["masked"], 1)
                        dve.wait_ge(s["masked"], 6 * t + 6)
                        nc.vector.tensor_tensor(XT[:, t, :, :], M[:, t, :, 0, :], spread(masks[:, RMASKS["pair_t"]:RMASKS["pair_t"] + P], 4), ALU.mult).then_inc(s["started"], 1)
                        nc.vector.tensor_tensor(X[:, t, :, :], X[:, t, :, :], spread(m.ident, 4), ALU.add).then_inc(s["steps"], 1)
                        dve.wait_ge(s["started"], t + 1)
                        nc.vector.tensor_tensor(XT[:, t, :, :], XT[:, t, :, :], spread(m.ident, 4), ALU.add).then_inc(s["steps"], 1)

            units = [(level, t) for level in range(RW_LEVELS) for t in range(NT)]
            with stage(nc, "heads_merge", "part_ready", "inner_ready", "inner_taken", "outer_ready", "x_added", "added") as (block, s):
                @block.gpsimd
                def _(pool):
                    for n, (level, t) in enumerate(units):
                        if n >= 2:
                            pool.wait_ge(s["inner_ready"], n - 1)
                        mask = masks[:, RMASKS["merge"] + level * P:RMASKS["merge"] + (level + 1) * P]
                        nc.gpsimd.tensor_tensor(NM[:, n % 2, :, :], M[:, t, :, 0, :], spread(mask, 4), ALU.mult).then_inc(s["part_ready"], 1)

                @block.tensor
                def _(pe):
                    def outer(n):
                        level, t = units[n]
                        pe.wait_ge(s["inner_taken"], n + 1)
                        if n >= 2:
                            pe.wait_ge(s["added"], n - 1)
                        for i in range(4):
                            if level < RW_LEVELS - 1:
                                nc.tensor.matmul(m.ps[:, 2 + n % 2, i * P:(i + 1) * P], XT[:, t, i, :], T1[:, n % 2, i, :], start=True, stop=True)
                            mm = nc.tensor.matmul(m.ps[:, 4 + n % 2, i * P:(i + 1) * P], T1[:, n % 2, i, :], XT[:, t, i, :], start=True, stop=True)
                        mm.then_inc(s["outer_ready"], 1)

                    for n, (level, t) in enumerate(units):
                        pe.wait_ge(s["part_ready"], n + 1)
                        if n >= NT:
                            pe.wait_ge(s["added"], n - NT + 1)
                        if n >= 2:
                            pe.wait_ge(s["inner_taken"], n - 1)
                        for i in range(4):
                            mm = nc.tensor.matmul(m.ps[:, n % 2, i * P:(i + 1) * P], NM[:, n % 2, i, :], X[:, t, i, :], start=True, stop=True)
                        mm.then_inc(s["inner_ready"], 1)
                        if n >= 1:
                            outer(n - 1)
                    outer(len(units) - 1)

                @block.scalar
                def _(act):
                    for n, (level, t) in enumerate(units):
                        act.wait_ge(s["inner_ready"], n + 1)
                        if n >= 2:
                            act.wait_ge(s["outer_ready"], n - 1)
                        nc.scalar.activation(T1[:, n % 2, :, :].rearrange("p i n -> p (i n)"), m.ps[:, n % 2, :], ACT.Copy).then_inc(s["inner_taken"], 1)

                @block.vector
                def _(dve):
                    for n, (level, t) in enumerate(units):
                        dve.wait_ge(s["outer_ready"], n + 1)
                        x, xt = (ap[:, t, :, :].rearrange("p i n -> p (i n)") for ap in (X, XT))
                        if level < RW_LEVELS - 1:
                            nc.vector.tensor_tensor(x, x, m.ps[:, 2 + n % 2, :], ALU.add).then_inc(s["x_added"], 1)
                            dve.wait_ge(s["x_added"], n + 1)
                        nc.vector.tensor_tensor(xt, xt, m.ps[:, 4 + n % 2, :], ALU.add).then_inc(s["added"], 1)

            with stage(nc, "heads_apply", "products", "taken_act", "taken_dve") as (block, s):
                @block.tensor
                def _(pe):
                    for t in range(NT):
                        for inst in range(4):
                            hh, d = inst // 2, inst % 2
                            e = slice(hh * HD, (hh + 1) * HD)
                            nc.tensor.matmul(m.ps[e, t, d * P:(d + 1) * P], tok[:, d, t, 0, e], XT[:, t, inst, :], start=True, stop=True)
                            mm = nc.tensor.matmul(m.ps[:, 4 + t, inst * HD:(inst + 1) * HD], M[:, t, inst, 2, :], tok[:, d, t, 3, e], start=True, stop=True)
                    mm.then_inc(s["products"], 1)

                @block.scalar
                def _(act):
                    act.wait_ge(s["products"], 1)
                    nc.scalar.activation(WT[:, :, 0:2, :].rearrange("p t d n -> p t (d n)"), m.ps[:, 0:4, 0:2 * P], ACT.Copy).then_inc(s["taken_act"], 1)

                @block.vector
                def _(dve):
                    dve.wait_ge(s["products"], 1)
                    nc.vector.tensor_copy(ZV.rearrange("p t i e -> p t (i e)"), m.ps[:, 4:8, 0:4 * HD]).then_inc(s["taken_dve"], 1)

            with stage(nc, "heads_apply2", "products", "taken") as (block, s):
                @block.tensor
                def _(pe):
                    for t in range(NT):
                        for inst in range(4):
                            hh, d = inst // 2, inst % 2
                            e = slice(hh * HD, (hh + 1) * HD)
                            mm = nc.tensor.matmul(m.ps[:, t, inst * HD:(inst + 1) * HD], XT[:, t, inst, :], ZV[:, t, inst, :], start=True, stop=True)
                    mm.then_inc(s["products"], 1)
                    for u in range(2):
                        on = slice(u * RW_CHUNK, (u + 1) * RW_CHUNK)
                        for t in range(NT):
                            for inst in range(4):
                                hh, d = inst // 2, inst % 2
                                e = slice(hh * HD, (hh + 1) * HD)
                                at = (t * 2 + d) * HD
                                mm = nc.tensor.matmul(m.ps[e, 4 + u, at:at + HD], tok[on, d, t, 2, e], tok[on, d, t, 3, e], start=True, stop=True)
                    mm.then_inc(s["products"], 1)

                @block.vector
                def _(dve):
                    nc.vector.memset(state[:], 0.0).then_inc(s["taken"], 1)
                    dve.wait_ge(s["products"], 1)
                    nc.vector.tensor_copy(U0.rearrange("p t i e -> p t (i e)"), m.ps[:, 0:4, 0:4 * HD]).then_inc(s["taken"], 1)
                    dve.wait_ge(s["products"], 2)
                    for u in range(2):
                        ends = p_end[:, u, :, :].rearrange("p t d -> p (t d)").unsqueeze(2).broadcast_to([P, 2 * NT, HD])
                        nc.vector.tensor_tensor(KV[:, u, :, :, :].rearrange("p t d e -> p (t d) e"),
                                                m.ps[:, 4 + u, :].rearrange("p (a e) -> p a e", e=HD), ends, ALU.mult).then_inc(s["taken"], 1)

            with stage(nc, "heads_scan", "from_state", "u_ready", "update_ready", "grown", "state_ready", "out_ready", "inter_taken", "steps",
                       "centred", "sums", "squared", "root_ready") as (block, s):
                @block.tensor
                def _(pe):
                    for n in range(2 * NT):
                        t, u = n // 2, n % 2
                        on = slice(u * RW_CHUNK, (u + 1) * RW_CHUNK)
                        if n >= 1:
                            pe.wait_ge(s["state_ready"], 2 * n)
                        for inst in range(4):
                            hh, d = inst // 2, inst % 2
                            e = slice(hh * HD, (hh + 1) * HD)
                            mm = nc.tensor.matmul(m.ps[on, hh, d * HD:(d + 1) * HD], WT[e, t, d, on], state[e, d, :], start=True, stop=True)
                        mm.then_inc(s["from_state"], 1)
                        for inst in range(4):
                            hh, d = inst // 2, inst % 2
                            e = slice(hh * HD, (hh + 1) * HD)
                            nc.tensor.matmul(m.ps[e, 4 + d, n * RW_CHUNK:(n + 1) * RW_CHUNK], state[e, d, :], AR[e, d, t, 1, on], start=True, stop=True)
                        pe.wait_ge(s["u_ready"], n + 1)
                        for inst in range(4):
                            hh, d = inst // 2, inst % 2
                            e = slice(hh * HD, (hh + 1) * HD)
                            mm = nc.tensor.matmul(m.ps[e, 2, d * HD:(d + 1) * HD], tok[on, d, t, 1, e], U[on, t, inst, :], start=True, stop=True)
                        mm.then_inc(s["update_ready"], 1)
                        if u == 1:
                            for inst in range(4):
                                hh, d = inst // 2, inst % 2
                                e = slice(hh * HD, (hh + 1) * HD)
                                into = m.ps[e, 6 + d, t * P:(t + 1) * P]
                                nc.tensor.matmul(into, U[:, t, inst, :], M[:, t, inst, 1, :], start=True, stop=False)
                                mm = nc.tensor.matmul(into, tok[:, d, t, 3, e], M[:, t, inst, 3, :], start=False, stop=True)
                            mm.then_inc(s["out_ready"], 1)
                    pe.wait_ge(s["centred"], 1)
                    nc.tensor.matmul(m.ps[:, 0, :], m.head_ones, XT[:, 0, :, :].rearrange("p i n -> p (i n)"), start=True, stop=True).then_inc(s["sums"], 1)
                    pe.wait_ge(s["squared"], 1)
                    nc.tensor.matmul(m.ps[:, 1, :], m.head_ones, XT[:, 1, :, :].rearrange("p i n -> p (i n)"), start=True, stop=True).then_inc(s["sums"], 1)

                @block.vector
                def _(dve):
                    for n in range(2 * NT):
                        t, u = n // 2, n % 2
                        on = slice(u * RW_CHUNK, (u + 1) * RW_CHUNK)
                        dve.wait_ge(s["from_state"], n + 1)
                        nc.vector.tensor_tensor(U[on, t, :, :].rearrange("p (h d) e -> p h (d e)", h=2), m.ps[on, 0:2, 0:2 * HD],
                                                U0[on, t, :, :].rearrange("p (h d) e -> p h (d e)", h=2), ALU.add).then_inc(s["u_ready"], 1)
                        if n >= 1:
                            dve.wait_ge(s["state_ready"], 2 * n)
                        for d in range(2):
                            nc.vector.scalar_tensor_tensor(out=grown[:, d, :], in0=state[:, d, :], scalar=p_end[:, u, t, d:d + 1],
                                                           in1=KV[:, u, t, d, :], op0=ALU.mult, op1=ALU.add).then_inc(s["grown"], 1)
                        dve.wait_ge(s["grown"], 2 * n + 2)
                        dve.wait_ge(s["update_ready"], n + 1)
                        for d in range(2):
                            nc.vector.scalar_tensor_tensor(out=state[:, d, :], in0=m.ps[:, 2, d * HD:(d + 1) * HD], scalar=p_end[:, u, t, d:d + 1],
                                                           in1=grown[:, d, :], op0=ALU.mult, op1=ALU.add).then_inc(s["state_ready"], 1)
                    done = [0]

                    def step(ins):
                        done[0] += 1
                        ins.then_inc(s["steps"], 1)
                        dve.wait_ge(s["steps"], done[0])

                    y, sq, fw, bw = (XT[:, k, :, :].rearrange("p i n -> p (i n)") for k in range(NT))
                    dve.wait_ge(s["inter_taken"], 2)
                    dve.wait_ge(s["out_ready"], NT)
                    step(nc.vector.tensor_tensor(fw, fw, m.ps[:, 6, :], ALU.add))
                    step(nc.vector.tensor_tensor(bw, bw, m.ps[:, 7, :], ALU.add))
                    step(nc.vector.tensor_tensor(y, fw, bw[:, ::-1], ALU.add))
                    dve.sem_inc(s["centred"], 1)
                    dve.wait_ge(s["sums"], 1)
                    step(nc.vector.scalar_tensor_tensor(out=y, in0=m.ps[:, 0, :], scalar=-1.0 / HD, in1=y, op0=ALU.mult, op1=ALU.add))
                    dve.sem_inc(s["centred"], 1)
                    dve.wait_ge(s["root_ready"], 1)
                    step(nc.vector.reciprocal(fw, fw))
                    step(nc.vector.tensor_tensor(y, y, fw, ALU.mult))
                    step(nc.vector.tensor_scalar(y, y, par[:, 3, :], par[:, 4, :], ALU.mult, ALU.add))
                    step(nc.vector.tensor_tensor(y, y, bonus[:], ALU.add))
                    step(nc.vector.tensor_tensor(tile_of(m.h, c), y, L[:, G_, :], ALU.mult))

                @block.scalar
                def _(act):
                    y, sq, fw, bw = (XT[:, k, :, :].rearrange("p i n -> p (i n)") for k in range(NT))
                    act.wait_ge(s["out_ready"], NT)
                    nc.scalar.activation(fw, m.ps[:, 4, :], ACT.Copy).then_inc(s["inter_taken"], 1)
                    nc.scalar.activation(bw, m.ps[:, 5, :], ACT.Copy).then_inc(s["inter_taken"], 1)
                    act.wait_ge(s["centred"], 2)
                    nc.scalar.activation(sq, y, ACT.Square).then_inc(s["squared"], 1)
                    act.wait_ge(s["sums"], 2)
                    nc.scalar.activation(fw, m.ps[:, 1, :], ACT.Sqrt, scale=1.0 / HD, bias=gn_eps[:, 0:1]).then_inc(s["root_ready"], 1)


def second_block(nc, m, a):
    with ExitStack() as held:
        def sb(name, shape):
            return held.enter_context(nc.sbuf_tensor(f"second_{name}", shape, F32))

        vec = sb("vec", [P, V2_W])
        own = sb("own", [P, VR_W])
        assert VS_W <= VR_W
        load(nc, "vec2_0", [(vec[:], a["vec2"][0]), (own[:, 0:VS_W], a["vec_swa"])])
        norm(nc, "tok_norm0", m, m.x, vec[:, V2["tok_g"]:V2["tok_g"] + DT], m.h)
        with ExitStack() as tmp:
            y = tmp.enter_context(nc.sbuf_tensor("swa2_y", [P, 12, S], F32))
            m.sin = tmp.enter_context(nc.sbuf_tensor("swa2_sin", [P, S], F32))
            m.cos = tmp.enter_context(nc.sbuf_tensor("swa2_cos", [P, S], F32))
            bands = tmp.enter_context(nc.sbuf_tensor("swa2_bands", [P, BANDS2_W], F32))
            load(nc, "bands2", [(bands[:], a["bands2"])])
            rope_table(nc, "rope2", m, a["positions2"])
            linear(nc, "qkv", m, a["w_qkv"], 0, lambda k: m.h[:, k, :], 12, 1, DT, 4, on_act=to_tiles(nc, m, y, 4))
            for half in range(2):
                heads_norm_rope(nc, f"q2_{half}", m, y[:, 4 * half:4 * half + 4, :], own[:, VS["q_g"]:VS["q_g"] + 1])
            heads_norm_rope(nc, "k2", m, y[:, 8:10, :], own[:, VS["k_g"]:VS["k_g"] + 1])
            band_attention(nc, "swa2", m, y[:, 0:8, :], y[:, 8:10, :], y[:, 10:12, :], own[:, VS["sinks"]:VS["sinks"] + 16], bands, (-1, 0, 1), m.h)
        linear(nc, "out2", m, a["w_o_swa"], 0, lambda k: m.h[:, k, :], DT, 1, DT, 4, on_dve=add_to_x(nc, m, 4))
        norm(nc, "ch_norm0", m, m.x, vec[:, V2["ch_g"]:V2["ch_g"] + DT], m.h)
        conv_ffn(nc, m, a, vec, 0)

        load(nc, "vec2_1", [(vec[:], a["vec2"][1]), (own[:], a["vec_rwkv"])])
        norm(nc, "tok_norm1", m, m.x, vec[:, V2["tok_g"]:V2["tok_g"] + DT], m.h)
        keep = [nc.dram_tensor(f"rwkv_keep{w}", (DT, P, S), F32).ap() for w in range(8)]
        with ExitStack() as tmp:
            buf = tmp.enter_context(nc.sbuf_tensor("rwkv_buf", [P, DT, S], F32))
            rwkv_inputs(nc, m, a, own, buf, keep)
        rwkv_heads(nc, m, a, own, keep)
        linear(nc, "out3", m, a["w_o_rwkv"], 0, lambda k: m.h[:, k, :], DT, 1, DT, 4, on_dve=add_to_x(nc, m, 4))
        norm(nc, "ch_norm1", m, m.x, vec[:, V2["ch_g"]:V2["ch_g"] + DT], m.h)
        conv_ffn(nc, m, a, vec, 1)


def lay_out_second(q):
    q = {k[:-2]: np.asarray(v) for k, v in q.items() if k.endswith("_2")}
    a = {}
    up = q["ffn_w_up"].reshape(DEPTH, D, 2, GT, P).transpose(0, 1, 3, 2, 4).reshape(DEPTH, D, 2 * FFN)

    def paired(v):
        return v.reshape(-1, 2, GT, P).transpose(0, 2, 1, 3).reshape(-1, 2 * FFN)

    def each(w, ks):
        return np.concatenate([weight_slots(w[l], ks) for l in range(w.shape[0])])

    a["w_ffn_up"] = each(up, DT)
    a["w_ffn_down"] = each(q["ffn_w_down"], GT // 2)
    a["w_qkv"] = weight_slots(q["swa_w_qkv"][0], DT)
    a["w_o_swa"] = weight_slots(q["swa_w_o"][0], DT)
    for name in ("r", "k", "v"):
        a[f"w_{name}"] = weight_slots(q[f"rwkv_w_{name}"][0], DT)
    a["w_o_rwkv"] = weight_slots(q["rwkv_w_o"][0], DT)
    for name in ("w", "a"):
        a[f"w_{name}1"] = weight_slots(np.concatenate(list(q[f"rwkv_{name}1"][0]), 1), DT)
        a[f"w_{name}2"] = np.concatenate(list(q[f"rwkv_{name}2"][0]), 0)
    g1 = np.zeros((D, 2 * P), np.float32)
    g1[:, :q["rwkv_g1"].shape[2]] = q["rwkv_g1"][0]
    g2 = np.zeros((2 * P, D), np.float32)
    g2[:q["rwkv_g2"].shape[1]] = q["rwkv_g2"][0]
    a["w_g1"] = weight_slots(g1, DT)
    a["w_g2"] = weight_slots(g2, 2)
    vec = np.zeros((DEPTH, P, V2_W), np.float32)
    for l in range(DEPTH):
        for at, what in ((V2["tok_g"], q["norm_tok"][l]), (V2["ch_g"], q["norm_ch"][l]), (V2["conv_w"], paired(q["ffn_conv_w"][l])),
                         (V2["conv_b"], paired(q["ffn_conv_b"][l]))):
            c = as_columns(what)
            vec[l, :, at:at + c.shape[1]] = c
    a["vec2"] = vec
    swa = np.zeros((P, VS_W), np.float32)
    swa[:, VS["q_g"]:VS["q_g"] + 1] = both_heads(q["swa_q_gain"][0])
    swa[:, VS["k_g"]:VS["k_g"] + 1] = both_heads(q["swa_k_gain"][0])
    swa[:, VS["sinks"]:VS["sinks"] + 16] = everywhere(q["swa_sinks"][0])
    a["vec_swa"] = swa
    rwkv = np.zeros((P, VR_W), np.float32)
    for at, what in ((VR["mu"], q["rwkv_mu"][0]), (VR["w0"], q["rwkv_w0"][0]), (VR["a0"], q["rwkv_a0"][0]), (VR["k_k"], q["rwkv_k_k"][0]),
                     (VR["k_a"], q["rwkv_k_a"][0]), (VR["r_k"], q["rwkv_r_k"][0]), (VR["ln_w"], q["rwkv_lnx_w"][0]), (VR["ln_b"], q["rwkv_lnx_b"][0])):
        c = as_columns(what)
        rwkv[:, at:at + c.shape[1]] = c
    a["vec_rwkv"] = rwkv
    a["positions2"] = np.ascontiguousarray(np.broadcast_to(np.arange(S, dtype=np.int32), (P, S)))
    restart = np.ones((P, S), np.float32)
    restart[:, ::RW_CHUNK] = 0.0
    a["restart"] = restart
    return a


class Memory:
    pass


def build(nc, a, out_t):
    with ExitStack() as held:
        def sb(name, shape):
            return held.enter_context(nc.sbuf_tensor(name, shape, F32))

        m = Memory()
        m.x = sb("x", [P, DT, S])
        m.h = sb("h", [P, DT, S])
        m.sq = sb("sq", [P, DT, S])
        m.rstd = sb("rstd", [P, S])
        m.ring = sb("ring", [P, RING, (FFN // P // 2) * P])
        m.c = sb("c", [P, CONSTS_W])
        m.eps = sb("eps", [P, 1])
        m.one = sb("one", [P, 1])
        m.ps = held.enter_context(nc.psum_tensor("ps", [P, 8, S], F32))
        m.ident = m.c[:, CONSTS["ident"]:CONSTS["ident"] + P]
        m.ones = m.c[:, CONSTS["ones"]:CONSTS["ones"] + P]
        m.head_ones = m.c[:, CONSTS["head_ones"]:CONSTS["head_ones"] + P]
        m.rot = m.c[:, CONSTS["rot"]:CONSTS["rot"] + P]
        m.pick = m.c[:, CONSTS["pick"]:CONSTS["pick"] + 4 * P]
        m.pick_pair = m.c[:, CONSTS["pick_pair"]:CONSTS["pick_pair"] + 2 * P]

        with stage(nc, "start", "set") as (block, s):
            @block.vector
            def _(dve):
                nc.vector.memset(m.eps[:], EPS).then_inc(s["set"], 1)
                nc.vector.memset(m.one[:], 1.0).then_inc(s["set"], 1)
        load(nc, "start_load", [(m.x[:], a["x_t"]), (m.c[:], a["consts"])])
        first_block(nc, m, a)
        second_block(nc, m, a)
        with stage(nc, "end", "stored") as (block, s):
            @block.sync
            def _(sp):
                sp.dma_start(out_t, m.x[:]).then_inc(s["stored"], 16)
                sp.wait_ge(s["stored"], 16)


def feature_tiles(a):
    a = np.asarray(a)
    return np.ascontiguousarray(a.T.reshape(a.shape[1] // P, P, a.shape[0]).transpose(1, 0, 2))


def weight_slots(w, ks):
    w = np.asarray(w)
    k, n = w.shape
    w = w.reshape(k // (ks * P), ks, P, n // P, P).transpose(3, 0, 2, 1, 4)
    return np.ascontiguousarray(w).reshape(-1, P, ks * P)


def as_columns(v):
    v = np.asarray(v)
    return v.reshape(-1, P).T


def everywhere(v):
    v = np.asarray(v)
    return np.broadcast_to(v[None, :], (P, v.shape[0]))


def both_heads(v):
    v = np.asarray(v)
    return np.concatenate([v, v])[:, None]


def lay_out(q):
    a = dict(constants())
    a["x_t"] = feature_tiles(q["x"][0])
    a["p_t"] = np.stack([feature_tiles(q["p"][l, 0]) for l in range(DEPTH)])
    a["positions"] = np.ascontiguousarray(np.broadcast_to(np.asarray(q["positions"]), (P, S)))
    w_in = np.asarray(q["w_in"])
    b_in = np.asarray(q["b_in"])
    g0 = 4 * 256
    keep = np.r_[0:g0, g0 + 8:w_in.shape[2]]
    pad = np.zeros((DEPTH, D, P), np.float32)
    pad[:, :, 0:4] = w_in[:, :, g0:g0 + 4]
    pad[:, :, 32:36] = w_in[:, :, g0 + 4:g0 + 8]
    def each(w, ks):
        return np.concatenate([weight_slots(w[l], ks) for l in range(w.shape[0])])
    a["w_gates"] = each(pad, DT)
    a["w_in"] = each(w_in[:, :, keep], DT)
    a["w_out"] = each(np.asarray(q["w_out"]), DT)
    a["w_up"] = each(np.asarray(q["w_up"]), DT)
    a["w_down"] = each(np.asarray(q["w_down"]), DT)
    a["w_gate"] = each(np.asarray(q["w_ple_gate"]), DT)
    a["w_ple"] = each(np.asarray(q["w_ple_proj"]), PLE // P)
    vec = np.zeros((DEPTH, P, V1_W), np.float32)
    for l in range(DEPTH):
        v = vec[l]
        for at, what in ((V1["in_g"], q["in_norm_g"][l]), (V1["b_in"], b_in[l][keep]), (V1["m_g"], q["mlstm_norm_g"][l]),
                         (V1["h_g"], q["hgrn_norm_g"][l]), (V1["conv_w"], q["mlstm_conv_w"][l]), (V1["conv_b"], q["mlstm_conv_b"][l]),
                         (V1["mlp_g"], q["mlp_norm_g"][l]), (V1["ple_g"], q["ple_norm_g"][l]), (V1["post_g"], q["ple_post_norm_g"][l]),
                         (V1["lb"], q["hgrn_lb_logits"])):
            c = as_columns(what)
            v[:, at:at + c.shape[1]] = c
        v[:, V1["q_g"]:V1["q_g"] + 1] = both_heads(q["swa_q_norm_g"][l])
        v[:, V1["k_g"]:V1["k_g"] + 1] = both_heads(q["swa_k_norm_g"][l])
        v[:, V1["sinks"]:V1["sinks"] + 8] = everywhere(q["swa_sinks"][l])
        v[0:4, V1["b_i"]] = b_in[l][g0:g0 + 4]
        v[32:36, V1["b_i"]] = b_in[l][g0 + 4:g0 + 8]
        v[32:36, V1["f_bias"]] = np.asarray(q["mlstm_f_bias"])[l]
        v[:, V1["is_first"]] = 1.0 if l == 0 else 0.0
    a["vec1"] = vec
    a.update(lay_out_second(q))
    return a


def kernel(**inputs):
    import concourse.bacc as _bacc
    from concourse.bass_utils import run_bass_kernel_spmd as _run

    nc = _bacc.Bacc("TRN2", target_bir_lowering=False, num_devices=1)
    arrays, args = {}, {}
    for name, value in lay_out(inputs).items():
        value = np.ascontiguousarray(value)
        arrays[f"in_{name}"] = value
        args[name] = nc.dram_tensor(f"in_{name}", value.shape, mybir.dt.from_np(value.dtype), kind="ExternalInput").ap()
    out_t = nc.dram_tensor("out_t", (P, DT, S), F32, kind="ExternalOutput").ap()
    build(nc, args, out_t)
    r = _run(nc, [arrays], core_ids=[0])
    got = np.asarray(r.results[0]["out_t"])
    return np.ascontiguousarray(got.transpose(1, 0, 2).reshape(D, S).T)[None]
```

```python
from contextlib import ExitStack, contextmanager

import numpy as np
import concourse.bass as bass
from concourse import mybir

F32 = mybir.dt.float32
F32R = mybir.dt.float32r
I32 = mybir.dt.int32
ALU = mybir.AluOpType
ACT = mybir.ActivationFunctionType
AX_X = mybir.AxisListType.X

P = 128
S = 512
NT = S // P
D = 1024
DT = D // P
DEPTH = 2
EPS = 1e-6
HD = 64
CONV_K = 4
D_FF = 4 * D
FFT = D_FF // P
PLE = 256
FFN = 2816
GT = FFN // P
ROPE_THETA = 500000.0
ROT = HD // 4
NEG = -1e30
RW_CHUNK = 64
RING = 4
SPLIT = 2
FIRST_SEMAPHORE = 150
DECAY_SCALE = float(np.exp(-0.5))

IN_TILES = ["mq", "mq", "mk", "mk", "mv", "mv", "mo", "mo", "hq", "hq", "hf", "hf", "hi", "hi", "hg", "hg",
            "sq", "sq", "sq", "sq", "sk", "sv"]
MQ, MK, MV, MO, HQ, HF, HI, HG, SQ, SK, SV = 0, 2, 4, 6, 8, 10, 12, 14, 16, 20, 21
NIN = len(IN_TILES)


def columns(*named):
    at, places = 0, {}
    for name, width in named:
        places[name] = at
        at += width
    return places, at


V1, V1_W = columns(("in_g", DT), ("b_in", NIN), ("m_g", 2), ("h_g", 2), ("q_g", 1), ("k_g", 1),
                   ("conv_w", CONV_K * 4), ("conv_b", 4), ("mlp_g", DT), ("ple_g", DT), ("post_g", DT),
                   ("sinks", 8), ("b_i", 1), ("b_f", 1), ("f_bias", 1), ("lb", 2 * DEPTH), ("is_first", 1))
V2, V2_W = columns(("tok_g", DT), ("ch_g", DT), ("conv_w", 3 * 2 * GT), ("conv_b", 2 * GT))
VS, VS_W = columns(("q_g", 1), ("k_g", 1), ("sinks", 16))
VR, VR_W = columns(("mu", 6 * DT), ("w0", 2 * DT), ("a0", 2 * DT), ("k_k", DT), ("k_a", DT), ("r_k", DT),
                   ("ln_w", DT), ("ln_b", DT))

HG_LEVELS = 7
RW_LEVELS = 5
CONSTS, CONSTS_W = columns(("ident", P), ("ones", P), ("head_ones", P), ("rot", P), ("inv_freq", 1),
                           ("pick", 4 * P), ("pick_pair", 2 * P))
MASKS, MASKS_W = columns(("causal", P), ("levels", HG_LEVELS * P))
BANDS1_W = 2 * P
BANDS2_W = 3 * P
RMASKS, RMASKS_W = columns(("before", P), ("upto", P), ("pair", P), ("pair_t", P), ("merge", RW_LEVELS * P))


def constants():
    i, j = np.arange(P)[:, None], np.arange(P)[None, :]
    c = np.zeros((P, CONSTS_W), np.float32)
    c[:, CONSTS["ident"]:CONSTS["ident"] + P] = i == j
    c[:, CONSTS["ones"]:CONSTS["ones"] + P] = 1.0
    c[:, CONSTS["head_ones"]:CONSTS["head_ones"] + P] = i // HD == j // HD
    half = ROT // 2
    for base in (0, HD):
        for d in range(half):
            c[base + half + d, CONSTS["rot"] + base + d] = -1.0
            c[base + d, CONSTS["rot"] + base + half + d] = 1.0
            f = np.float32(ROPE_THETA) ** np.float32(-2.0 * d / ROT)
            c[base + d, CONSTS["inv_freq"]] = f
            c[base + half + d, CONSTS["inv_freq"]] = f
    for h in range(4):
        c[h, CONSTS["pick"] + h * P:CONSTS["pick"] + (h + 1) * P] = 1.0
        at = CONSTS["pick_pair"] + (h // 2) * P + (h % 2) * HD
        c[h, at:at + HD] = 1.0
    m = np.zeros((P, MASKS_W), np.float32)
    m[:, 0:P] = i <= j
    for level in range(HG_LEVELS):
        w = 1 << level
        same = i // (2 * w) == j // (2 * w)
        m[:, MASKS["levels"] + level * P:MASKS["levels"] + (level + 1) * P] = same & (i % (2 * w) < w) & (j % (2 * w) >= w)
    b1 = np.concatenate([np.where(j > i, 0, NEG), np.where(j <= i, 0, NEG)], 1).astype(np.float32)
    b2 = np.concatenate([np.where(j >= i, 0, NEG), np.zeros((P, P)), np.where(j <= i, 0, NEG)], 1).astype(np.float32)
    r = np.zeros((P, RMASKS_W), np.float32)
    chunk = i // RW_CHUNK == j // RW_CHUNK
    r[:, RMASKS["before"]:RMASKS["before"] + P] = chunk & (i < j)
    r[:, RMASKS["upto"]:RMASKS["upto"] + P] = chunk & (i <= j)
    r[:, RMASKS["pair"]:RMASKS["pair"] + P] = (i // 2 == j // 2) & (i > j)
    r[:, RMASKS["pair_t"]:RMASKS["pair_t"] + P] = (i // 2 == j // 2) & (i < j)
    for level in range(RW_LEVELS):
        w = 2 << level
        same = i // (2 * w) == j // (2 * w)
        r[:, RMASKS["merge"] + level * P:RMASKS["merge"] + (level + 1) * P] = same & (i % (2 * w) < w) & (j % (2 * w) >= w)
    return {"consts": c, "masks": m, "bands1": b1, "bands2": b2, "rmasks": r}


@contextmanager
def stage(nc, name, *signals):
    with ExitStack() as held:
        sems, numbers = {}, []
        for signal in signals:
            word, _, count = signal.partition("*")
            made = [held.enter_context(nc.semaphore(f"{name}_{word}{j}", num=FIRST_SEMAPHORE + len(numbers) + j)) for j in range(int(count or 1))]
            numbers += [s.num for s in made]
            sems[word] = made if count else made[0]
        block = held.enter_context(ExitStack())
        yield block.enter_context(nc.Block(no_gpsimd_drain=True)), sems
        block.close()
        nc.all_engine_barrier(sems_to_clear=range(min(numbers), max(numbers) + 1))


def tile_of(ap, index):
    return ap[:, bass.ds(index, 1), :].rearrange("p a n -> p (a n)")


def row_of(dram, index):
    return dram[bass.ds(index, 1)].rearrange("a p n -> p (a n)")


def spread(ap, n):
    return ap.unsqueeze(1).broadcast_to([ap.shape[0], n, ap.shape[1]])


def load(nc, name, pairs):
    with stage(nc, name, "loaded") as (block, s):
        @block.sync
        def _(sp):
            for dst, src in pairs:
                sp.dma_start(dst, src).then_inc(s["loaded"], 16)
            sp.wait_ge(s["loaded"], 16 * len(pairs))


@contextmanager
def product_memory(nc, m, ks=DT):
    with ExitStack() as held:
        m.count += 1

        def sb(name, shape, dtype):
            return held.enter_context(nc.sbuf_tensor(f"{name}_{m.count}", shape, dtype))

        m.hi = sb("hi", [P, DT, S], F32R)
        m.lo = sb("lo", [P, DT, S], F32R)
        m.ring = sb("ring", [P, RING, ks * P], F32)
        m.w_hi = sb("w_hi", [P, SPLIT, ks * P], F32R)
        m.w_lo = sb("w_lo", [P, SPLIT, ks * P], F32R)
        yield


def norm_first(nc, m, src, gain, width=D):
    tiles = width // P

    def act(eng, s):
        for k in range(tiles):
            nc.scalar.activation(m.sq[:, k, :], src[:, k, :], ACT.Square).then_inc(s["squares_ready"], 1)
        eng.wait_ge(s["sums_ready"], 1)
        nc.scalar.activation(m.rstd[:], m.ps[:, 7, :], ACT.Sqrt, scale=1.0 / width, bias=m.eps[:, 0:1]).then_inc(s["root_ready"], 1)
        for k in range(tiles):
            eng.wait_ge(s["normed"], k + 1)
            nc.scalar.activation(m.hi[:, k, :], m.sq[:, k, :], ACT.Copy).then_inc(s["input_hi"], 1)

    def pe(eng, s):
        for k in range(tiles):
            eng.wait_ge(s["squares_ready"], k + 1)
            mm = nc.tensor.matmul(m.ps[:, 7, :], m.ones, m.sq[:, k, :], start=(k == 0), stop=(k == tiles - 1))
        mm.then_inc(s["sums_ready"], 1)

    def dve(eng, s):
        eng.wait_ge(s["root_ready"], 1)
        nc.vector.reciprocal(m.rstd[:], m.rstd[:]).then_inc(s["rstd_ready"], 1)
        eng.wait_ge(s["rstd_ready"], 1)
        for k in range(tiles):
            nc.vector.scalar_tensor_tensor(out=m.sq[:, k, :], in0=src[:, k, :], scalar=gain[:, k:k + 1],
                                           in1=m.rstd[:], op0=ALU.mult, op1=ALU.mult).then_inc(s["normed"], 1)

    def pool(eng, s):
        for k in range(tiles):
            eng.wait_ge(s["input_hi"], k + 1)
            nc.gpsimd.tensor_tensor(m.lo[:, k, :], m.sq[:, k, :], m.hi[:, k, :].bitcast(F32), ALU.subtract).then_inc(s["input_lo"], 1)

    return {"act": act, "pe": pe, "dve": dve, "pool": pool, "tiles": tiles,
            "signals": ("squares_ready", "sums_ready", "root_ready", "rstd_ready", "normed")}


def split_first(nc, m, src):
    tiles = src.shape[1]

    def act(eng, s):
        for k in range(tiles):
            nc.scalar.activation(m.hi[:, k, :], src[:, k, :], ACT.Copy).then_inc(s["input_hi"], 1)

    def pool(eng, s):
        for k in range(tiles):
            eng.wait_ge(s["input_hi"], k + 1)
            nc.gpsimd.tensor_tensor(m.lo[:, k, :], src[:, k, :], m.hi[:, k, :].bitcast(F32), ALU.subtract).then_inc(s["input_lo"], 1)

    return {"act": act, "pool": pool, "tiles": tiles, "signals": ()}


def mix_first(nc, m, xx, mu, tmp):
    def dve(eng, s):
        for k in range(DT):
            nc.vector.scalar_tensor_tensor(out=tmp[:, k, :], in0=xx[:, k, :], scalar=mu[:, k:k + 1], in1=m.h[:, k, :],
                                           op0=ALU.mult, op1=ALU.add).then_inc(s["mixed"], 1)

    def act(eng, s):
        for k in range(DT):
            eng.wait_ge(s["mixed"], k + 1)
            nc.scalar.activation(m.hi[:, k, :], tmp[:, k, :], ACT.Copy).then_inc(s["input_hi"], 1)

    split = split_first(nc, m, tmp)
    return {"act": act, "dve": dve, "pool": split["pool"], "tiles": DT, "signals": ("mixed",)}


def norm(nc, name, m, src, gain, dst):
    first = norm_first(nc, m, src, gain)
    with stage(nc, name, "copied", "input_hi", *first["signals"]) as (block, s):
        @block.scalar
        def _(act):
            for k in range(DT):
                nc.scalar.activation(m.sq[:, k, :], src[:, k, :], ACT.Square).then_inc(s["squares_ready"], 1)
            act.wait_ge(s["sums_ready"], 1)
            nc.scalar.activation(m.rstd[:], m.ps[:, 7, :], ACT.Sqrt, scale=1.0 / D, bias=m.eps[:, 0:1]).then_inc(s["root_ready"], 1)

        @block.tensor
        def _(pe):
            first["pe"](pe, s)

        @block.vector
        def _(dve):
            dve.wait_ge(s["root_ready"], 1)
            nc.vector.reciprocal(m.rstd[:], m.rstd[:]).then_inc(s["rstd_ready"], 1)
            dve.wait_ge(s["rstd_ready"], 1)
            for k in range(DT):
                nc.vector.scalar_tensor_tensor(out=dst[:, k, :], in0=src[:, k, :], scalar=gain[:, k:k + 1],
                                               in1=m.rstd[:], op0=ALU.mult, op1=ALU.mult).then_inc(s["normed"], 1)


def linear(nc, name, m, weights, base, n_tiles, ks, unroll, rhs=None, parts=1, signals=(), on_act=None, on_dve=None, on_pool=None,
           first=None, at_start=None, at_end=None):
    ring = unroll * parts
    split = min(SPLIT, ring)
    steps = n_tiles // unroll
    assert n_tiles % unroll == 0 and ks * P <= m.ring.shape[2] and ring <= RING and ring % split == 0
    rhs = rhs or (lambda k: (m.hi[:, k, :], m.lo[:, k, :]))
    first = first or {"signals": (), "tiles": 0}
    width = ks * P
    with stage(nc, name, f"loaded*{ring}", "w_hi_ready", "w_lo_ready", "slots_used", "banks_free", "input_hi", "input_lo",
               *first["signals"], *signals) as (block, s):
        @block.sync
        def _(sp):
            with sp.Fori(0, steps) as i:
                for j in range(ring):
                    sp.wait_ge(s["w_lo_ready"], i * ring + (j + 1))
                    sp.dma_start(m.ring[:, j, 0:width], row_of(weights, i * ring + (base + j))).then_inc(s["loaded"][j], 16)
            if at_end:
                at_end(sp, s, split + n_tiles * parts)

        @block.tensor
        def _(pe):
            pe.sem_inc(s["slots_used"], split)
            pe.sem_inc(s["w_lo_ready"], ring)
            pe.sem_inc(s["banks_free"], unroll)
            if at_start:
                at_start(pe, s)
            if "pe" in first:
                first["pe"](pe, s)
            if first["tiles"]:
                pe.wait_ge(s["input_lo"], first["tiles"])
            with pe.Fori(0, steps) as i:
                for u in range(unroll):
                    pe.wait_ge(s["banks_free"], i * unroll + (u + 1))
                    for part in range(parts):
                        j = u * parts + part
                        pe.wait_ge(s["w_lo_ready"], i * ring + (ring + j + 1))
                        for k in range(ks):
                            hi, lo = rhs(part * ks + k)
                            w_hi, w_lo = (w[:, j % split, k * P:(k + 1) * P] for w in (m.w_hi, m.w_lo))
                            ends = part == parts - 1 and k == ks - 1
                            nc.tensor.matmul(m.ps[:, u, :], w_hi, hi, start=(part == 0 and k == 0), stop=False)
                            nc.tensor.matmul(m.ps[:, u, :], w_hi, lo, start=False, stop=False)
                            mm = nc.tensor.matmul(m.ps[:, u, :], w_lo, hi, start=False, stop=ends)
                        mm.then_inc(s["slots_used"], 1)

        lag = min(max(SPLIT // parts, 1), unroll)

        def lagging(eng, split_slot, take):
            def step(i, is_first):
                for u in range(unroll):
                    for part in range(parts):
                        split_slot(i, u * parts + part)
                    if take and not (is_first and u < lag):
                        take(eng, i * unroll + (u - lag), (u - lag) % unroll, s, i * ring + (split + (u - lag + 1) * parts))

            step(0, True)
            if steps > 1:
                with eng.Fori(1, steps) as i:
                    step(i, False)
            if take:
                for t in range(n_tiles - lag, n_tiles):
                    take(eng, t, t % unroll, s, split + (t + 1) * parts)

        @block.scalar
        def _(act):
            if "act" in first:
                first["act"](act, s)

            def split_slot(i, j):
                act.wait_ge(s["loaded"][j], i * 16 + 16)
                act.wait_ge(s["slots_used"], i * ring + (j + 1))
                nc.scalar.activation(m.w_hi[:, j % split, 0:width], m.ring[:, j, 0:width], ACT.Copy).then_inc(s["w_hi_ready"], 1)
            lagging(act, split_slot, on_act)

        @block.vector
        def _(dve):
            if "dve" in first:
                first["dve"](dve, s)

            def split_slot(i, j):
                dve.wait_ge(s["w_hi_ready"], i * ring + (j + 1))
                nc.vector.tensor_tensor(m.w_lo[:, j % split, 0:width], m.ring[:, j, 0:width], m.w_hi[:, j % split, 0:width].bitcast(F32),
                                        ALU.subtract).then_inc(s["w_lo_ready"], 1)
            lagging(dve, split_slot, on_dve)

        if "pool" in first or on_pool:
            @block.gpsimd
            def _(pool):
                if "pool" in first:
                    first["pool"](pool, s)
                if on_pool:
                    with pool.Fori(0, steps) as i:
                        for u in range(unroll):
                            on_pool(pool, i * unroll + u, u, s, i * ring + (split + (u + 1) * parts))


def add_to_x(nc, m):
    def on_dve(dve, t, u, s, used):
        dve.wait_ge(s["slots_used"], used)
        x = tile_of(m.x, t)
        nc.vector.tensor_tensor(x, x, m.ps[:, u, :], ALU.add).then_inc(s["banks_free"], 1)
    return on_dve


def to_tiles(nc, m, dst, func=ACT.Copy, bias=None):
    def on_act(act, t, u, s, used):
        act.wait_ge(s["slots_used"], used)
        more = {} if bias is None else {"bias": bias[:, bass.ds(t, 1)]}
        nc.scalar.activation(tile_of(dst, t), m.ps[:, u, :], func, **more).then_inc(s["banks_free"], 1)
    return on_act


def rope_table(nc, name, m, positions):
    two_pi = 2.0 * np.pi
    high = float(np.float32(6.28125))
    mid = float(np.float32(0.0019340515))
    mid = float(np.frombuffer((np.frombuffer(np.float32(mid).tobytes(), np.uint32) & np.uint32(0xFFFFF000)).tobytes(), np.float32)[0])
    low = float(two_pi - high - mid)
    magic = 12582912.0
    with ExitStack() as tmp, stage(nc, name, "steps", "angles_ready", "positions_loaded", "tables_ready") as (block, s):
        pos = tmp.enter_context(nc.sbuf_tensor(f"{name}_pos", [P, S], I32))
        turns = tmp.enter_context(nc.sbuf_tensor(f"{name}_turns", [P, S], F32))

        @block.sync
        def _(sp):
            sp.dma_start(pos[:], positions).then_inc(s["positions_loaded"], 16)

        @block.vector
        def _(dve):
            done = [0]

            def step(ins):
                done[0] += 1
                ins.then_inc(s["steps"], 1)
                dve.wait_ge(s["steps"], done[0])

            dve.wait_ge(s["positions_loaded"], 16)
            step(nc.vector.tensor_copy(m.sin[:], pos[:]))
            step(nc.vector.tensor_scalar(m.sin[:], m.sin[:], m.c[:, CONSTS["inv_freq"]:CONSTS["inv_freq"] + 1], None, ALU.mult))
            step(nc.vector.tensor_scalar(turns[:], m.sin[:], 1.0 / two_pi, None, ALU.mult))
            step(nc.vector.tensor_scalar(turns[:], turns[:], magic, None, ALU.add))
            step(nc.vector.tensor_scalar(turns[:], turns[:], -magic, None, ALU.add))
            for part in (high, mid, low):
                step(nc.vector.scalar_tensor_tensor(out=m.sin[:], in0=turns[:], scalar=-part, in1=m.sin[:], op0=ALU.mult, op1=ALU.add))
            step(nc.vector.tensor_scalar(turns[:], m.sin[:], np.pi / 2, -two_pi, ALU.is_gt, ALU.mult))
            step(nc.vector.scalar_tensor_tensor(out=m.cos[:], in0=m.sin[:], scalar=np.pi / 2, in1=turns[:], op0=ALU.add, op1=ALU.add))
            for t in (m.sin, m.cos):
                step(nc.vector.tensor_scalar(t[:], t[:], 3.1415925, -3.1415925, ALU.min, ALU.max))
            dve.sem_inc(s["angles_ready"], 1)

        @block.scalar
        def _(act):
            act.wait_ge(s["angles_ready"], 1)
            for t in (m.sin, m.cos):
                nc.scalar.activation(t[:], t[:], ACT.Sin).then_inc(s["tables_ready"], 1)


def heads_norm_rope(nc, name, m, tiles, gain):
    n = tiles.shape[1]
    with ExitStack() as tmp, stage(nc, name, "squares_ready", "sums_ready", "root_ready", "rstd_ready", "normed",
                                   "rotated", "turned", "scaled") as (block, s):
        sq, rstd = m.sq[:, 0:n, :], m.sq[:, 4:4 + n, :]
        other = tmp.enter_context(nc.sbuf_tensor(f"{name}_other", [P, n, S], F32))

        @block.scalar
        def _(act):
            nc.scalar.activation(sq, tiles, ACT.Square).then_inc(s["squares_ready"], 1)
            act.wait_ge(s["sums_ready"], n)
            nc.scalar.activation(rstd, m.ps[:, 0:n, :], ACT.Sqrt, scale=1.0 / HD, bias=m.eps[:, 0:1]).then_inc(s["root_ready"], 1)

        @block.tensor
        def _(pe):
            pe.wait_ge(s["squares_ready"], 1)
            for k in range(n):
                nc.tensor.matmul(m.ps[:, k, :], m.head_ones, sq[:, k, :], start=True, stop=True).then_inc(s["sums_ready"], 1)
            pe.wait_ge(s["normed"], 1)
            for k in range(n):
                nc.tensor.matmul(m.ps[:, 4 + k, :], m.rot, tiles[:, k, :], start=True, stop=True).then_inc(s["rotated"], 1)

        @block.vector
        def _(dve):
            dve.wait_ge(s["root_ready"], 1)
            nc.vector.reciprocal(rstd, rstd).then_inc(s["rstd_ready"], 1)
            dve.wait_ge(s["rstd_ready"], 1)
            nc.vector.scalar_tensor_tensor(out=tiles, in0=tiles, scalar=gain, in1=rstd, op0=ALU.mult, op1=ALU.mult).then_inc(s["normed"], 1)
            dve.wait_ge(s["rotated"], n)
            nc.vector.tensor_tensor(other[:], m.ps[:, 4:4 + n, :], spread(m.sin[:], n), ALU.mult).then_inc(s["turned"], 1)
            nc.vector.tensor_tensor(tiles, tiles, spread(m.cos[:], n), ALU.mult).then_inc(s["scaled"], 1)
            dve.wait_ge(s["turned"], 1)
            dve.wait_ge(s["scaled"], 1)
            nc.vector.tensor_tensor(tiles, tiles, other[:], ALU.add).then_inc(s["scaled"], 1)


def heads_norm_gate(nc, name, m, src, gain, gate, func, dst):
    with stage(nc, name, "squares_ready", "sums_ready", "root_ready", "rstd_ready", "gate_ready", "normed", "done") as (block, s):
        sq, rstd, g = m.sq[:, 0:2, :], m.sq[:, 2:4, :], m.sq[:, 4:6, :]

        @block.scalar
        def _(act):
            nc.scalar.activation(sq, src, ACT.Square).then_inc(s["squares_ready"], 1)
            nc.scalar.activation(g, gate, func).then_inc(s["gate_ready"], 1)
            act.wait_ge(s["sums_ready"], 2)
            nc.scalar.activation(rstd, m.ps[:, 0:2, :], ACT.Sqrt, scale=1.0 / HD, bias=m.eps[:, 0:1]).then_inc(s["root_ready"], 1)

        @block.tensor
        def _(pe):
            pe.wait_ge(s["squares_ready"], 1)
            for k in range(2):
                nc.tensor.matmul(m.ps[:, k, :], m.head_ones, sq[:, k, :], start=True, stop=True).then_inc(s["sums_ready"], 1)

        @block.vector
        def _(dve):
            dve.wait_ge(s["root_ready"], 1)
            nc.vector.reciprocal(rstd, rstd).then_inc(s["rstd_ready"], 1)
            dve.wait_ge(s["rstd_ready"], 1)
            for k in range(2):
                nc.vector.scalar_tensor_tensor(out=rstd[:, k, :], in0=src[:, k, :], scalar=gain[:, k:k + 1], in1=rstd[:, k, :],
                                               op0=ALU.mult, op1=ALU.mult).then_inc(s["normed"], 1)
            dve.wait_ge(s["normed"], 2)
            dve.wait_ge(s["gate_ready"], 1)
            nc.vector.tensor_tensor(dst, rstd, g, ALU.mult).then_inc(s["done"], 1)


def transpose_tiles(nc, name, m, src, dst):
    n = src.shape[1]
    with stage(nc, name, "turned", "copied") as (block, s):
        @block.tensor
        def _(pe):
            for j in range(NT):
                for k in range(n):
                    nc.tensor.transpose(m.ps[:, j, k * P:(k + 1) * P], src[:, k, j * P:(j + 1) * P], m.ident).then_inc(s["turned"], 1)

        @block.vector
        def _(dve):
            for j in range(NT):
                dve.wait_ge(s["turned"], n * (j + 1))
                nc.vector.tensor_copy(dst[:, j, 0:n * P], m.ps[:, j, 0:n * P]).then_inc(s["copied"], 1)


def conv_silu(nc, m, tiles, vec):
    with ExitStack() as tmp, stage(nc, "conv", "taps", "silu_done") as (block, s):
        acc = tmp.enter_context(nc.sbuf_tensor("conv_acc", [P, 4, S], F32))

        @block.vector
        def _(dve):
            for tap in range(CONV_K):
                back = tap
                for k in range(4):
                    w = vec[:, V1["conv_w"] + (CONV_K - 1 - tap) * 4 + k:V1["conv_w"] + (CONV_K - 1 - tap) * 4 + k + 1]
                    if tap == 0:
                        ins = nc.vector.tensor_scalar(acc[:, k, :], tiles[:, k, :], w, vec[:, V1["conv_b"] + k:V1["conv_b"] + k + 1], ALU.mult, ALU.add)
                    else:
                        dve.wait_ge(s["taps"], tap * 4 - 3 + k)
                        ins = nc.vector.scalar_tensor_tensor(out=acc[:, k, back:], in0=tiles[:, k, 0:S - back], scalar=w,
                                                             in1=acc[:, k, back:], op0=ALU.mult, op1=ALU.add)
                    ins.then_inc(s["taps"], 1)

        @block.scalar
        def _(act):
            act.wait_ge(s["taps"], 4 * CONV_K)
            nc.scalar.activation(tiles, acc[:], ACT.Silu).then_inc(s["silu_done"], 1)


def mlstm(nc, m, vec, y, gates, dst):
    with ExitStack() as tmp:
        def sb(name, shape):
            return tmp.enter_context(nc.sbuf_tensor(f"mlstm_{name}", shape, F32))

        F, ABS, LN, LF, B, M, C, A = range(8)
        rows = sb("rows", [4, 8, S])
        neg_m = sb("neg_m", [4, S])
        zeros = sb("zeros", [4, S])
        v_tok = sb("v_tok", [P, NT, 2 * P])
        a_col = sb("a_col", [P, NT, 4])
        w = sb("w", [P, 4, S])
        den = sb("den", [P, 2, S])
        em = sb("em", [P, 2, S])

        with stage(nc, "mlstm_gates", "steps", "abs_ready", "exp_ready", "ln_ready") as (block, s):
            @block.vector
            def _(dve):
                done = [0]

                def step(ins):
                    done[0] += 1
                    ins.then_inc(s["steps"], 1)
                    dve.wait_ge(s["steps"], done[0])

                step(nc.vector.memset(zeros[:], 0.0))
                step(nc.vector.tensor_scalar(rows[:, F, :], gates[32:36, :], vec[32:36, V1["f_bias"]:V1["f_bias"] + 1], None, ALU.add))
                step(nc.vector.scalar_tensor_tensor(out=rows[:, ABS, :], in0=rows[:, F, :], scalar=-1.0, in1=rows[:, F, :], op0=ALU.mult, op1=ALU.max))
                dve.sem_inc(s["abs_ready"], 1)
                step(nc.vector.tensor_scalar(rows[:, F, :], rows[:, F, :], 0.0, None, ALU.min))
                dve.wait_ge(s["ln_ready"], 1)
                step(nc.vector.tensor_tensor(rows[:, LF, :], rows[:, F, :], rows[:, LN, :], ALU.subtract))
                step(nc.vector.tensor_tensor_scan(rows[:, B, :], rows[:, LF, :], zeros[:], 0.0, ALU.add, ALU.add))
                step(nc.vector.tensor_tensor_scan(rows[:, M, :], rows[:, LF, :], gates[0:4, :], 0.0, ALU.add, ALU.max))
                step(nc.vector.tensor_tensor(rows[:, C, :], rows[:, B, :], rows[:, M, :], ALU.subtract))
                step(nc.vector.tensor_tensor(rows[:, A, :], gates[0:4, :], rows[:, B, :], ALU.subtract))
                step(nc.vector.tensor_scalar(neg_m[:], rows[:, M, :], -1.0, None, ALU.mult))

            @block.scalar
            def _(act):
                act.wait_ge(s["abs_ready"], 1)
                nc.scalar.activation(rows[:, LN, :], rows[:, ABS, :], ACT.Exp, scale=-1.0).then_inc(s["exp_ready"], 1)
                act.wait_ge(s["exp_ready"], 1)
                nc.scalar.activation(rows[:, LN, :], rows[:, LN, :], ACT.Ln, bias=m.one[:, 0:1][0:4]).then_inc(s["ln_ready"], 1)

        transpose_tiles(nc, "mlstm_v", m, y[:, MV:MV + 2, :], v_tok)

        with stage(nc, "mlstm_a", "turned", "copied") as (block, s):
            @block.tensor
            def _(pe):
                for j in range(NT):
                    nc.tensor.transpose(m.ps[:, 0, 4 * j:4 * j + 4], rows[:, A, j * P:(j + 1) * P], m.ident[0:4, 0:4]).then_inc(s["turned"], 1)

            @block.vector
            def _(dve):
                dve.wait_ge(s["turned"], NT)
                nc.vector.tensor_copy(a_col[:].rearrange("p a b -> p (a b)"), m.ps[:, 0, 0:4 * NT]).then_inc(s["copied"], 1)

        units = [(h, j) for h in range(4) for j in range(NT)]
        with stage(nc, "mlstm", "rows_spread", "scores_ready", "args_ready", "exp_ready", "weighted", "masked", "summed") as (block, s):
            @block.tensor
            def _(pe):
                def outputs(n):
                    h, j = units[n]
                    pe.wait_ge(s["masked"], n + 1)
                    for bank, lhsT in ((4, v_tok[:, j, h * HD:(h + 1) * HD]), (6, m.ones[:, 0:HD])):
                        mm = nc.tensor.matmul(m.ps[(h % 2) * HD:(h % 2 + 1) * HD, bank + h // 2, j * P:], lhsT, w[:, n % 4, j * P:],
                                              start=(j == 0), stop=(j == NT - 1))
                    mm.then_inc(s["summed"], 1)

                for n, (h, j) in enumerate(units):
                    lo = (h % 2) * HD
                    if j == 0:
                        if h >= 2:
                            pe.wait_ge(s["args_ready"], (h - 1) * NT)
                        nc.tensor.matmul(m.ps[:, h % 2, :], m.pick[0:4, h * P:(h + 1) * P], rows[:, C, :], start=True, stop=True).then_inc(s["rows_spread"], 1)
                    if n >= 2:
                        pe.wait_ge(s["weighted"], n - 1)
                    nc.tensor.matmul(m.ps[:, 2 + n % 2, j * P:], y[lo:lo + HD, MK + h // 2, j * P:(j + 1) * P],
                                     y[lo:lo + HD, MQ + h // 2, j * P:], start=True, stop=True).then_inc(s["scores_ready"], 1)
                    if n >= 1:
                        outputs(n - 1)
                outputs(len(units) - 1)

            @block.vector
            def _(dve):
                def args(n):
                    h, j = units[n]
                    dve.wait_ge(s["rows_spread"], h + 1)
                    if n >= 4:
                        dve.wait_ge(s["summed"], n - 3)
                    nc.vector.tensor_scalar(w[:, n % 4, j * P:], m.ps[:, h % 2, j * P:], a_col[:, j, h:h + 1], 0.0, ALU.add, ALU.min).then_inc(s["args_ready"], 1)

                args(0)
                for n, (h, j) in enumerate(units):
                    if n + 1 < len(units):
                        args(n + 1)
                    dve.wait_ge(s["exp_ready"], n + 1)
                    dve.wait_ge(s["scores_ready"], n + 1)
                    nc.vector.scalar_tensor_tensor(out=w[:, n % 4, j * P:], in0=m.ps[:, 2 + n % 2, j * P:], scalar=HD ** -0.5,
                                                   in1=w[:, n % 4, j * P:], op0=ALU.mult, op1=ALU.mult).then_inc(s["weighted"], 1)
                    dve.wait_ge(s["weighted"], n + 1)
                    nc.vector.tensor_tensor(w[:, n % 4, j * P:(j + 1) * P], w[:, n % 4, j * P:(j + 1) * P], m.masks[:, 0:P], ALU.mult).then_inc(s["masked"], 1)

            @block.scalar
            def _(act):
                for n, (h, j) in enumerate(units):
                    act.wait_ge(s["args_ready"], n + 1)
                    nc.scalar.activation(w[:, n % 4, j * P:], w[:, n % 4, j * P:], ACT.Exp).then_inc(s["exp_ready"], 1)

        with stage(nc, "mlstm_out", "floor_spread", "floor_ready", "abs_ready", "steps") as (block, s):
            @block.tensor
            def _(pe):
                for k in range(2):
                    nc.tensor.matmul(m.ps[:, k, :], m.pick_pair[0:4, k * P:(k + 1) * P], neg_m[:], start=True, stop=True).then_inc(s["floor_spread"], 1)

            @block.scalar
            def _(act):
                nc.scalar.activation(den[:], m.ps[:, 6:8, :], ACT.Abs).then_inc(s["abs_ready"], 1)
                act.wait_ge(s["floor_spread"], 2)
                nc.scalar.activation(em[:], m.ps[:, 0:2, :], ACT.Exp).then_inc(s["floor_ready"], 1)

            @block.vector
            def _(dve):
                dve.wait_ge(s["abs_ready"], 1)
                dve.wait_ge(s["floor_ready"], 1)
                nc.vector.tensor_tensor(den[:], den[:], em[:], ALU.max).then_inc(s["steps"], 1)
                dve.wait_ge(s["steps"], 1)
                nc.vector.reciprocal(den[:], den[:]).then_inc(s["steps"], 1)
                dve.wait_ge(s["steps"], 2)
                nc.vector.tensor_tensor(den[:], den[:], m.ps[:, 4:6, :], ALU.mult).then_inc(s["steps"], 1)

        heads_norm_gate(nc, "mlstm_norm", m, den[:], vec[:, V1["m_g"]:V1["m_g"] + 2], y[:, MO:MO + 2, :], ACT.Sigmoid, dst)


def hgrn(nc, m, vec, y, dst):
    with ExitStack() as tmp:
        def sb(name, shape):
            return tmp.enter_context(nc.sbuf_tensor(f"hgrn_{name}", shape, F32))

        lb = sb("lb", [P, 8, 2])
        zeros = sb("zeros", [P, S])
        G = sb("G", [P, 2, S])
        a = sb("a", [P, 2, S])
        b = sb("b", [P, 2, S])
        q_dec = sb("q_dec", [P, 2, S])
        k_dec = sb("k_dec", [P, 2, S])
        v_tok = sb("v_tok", [P, NT, 2 * P])
        A = sb("A", [P, 10, 2, 2, P])
        part = sb("part", [P, 2, 2, 2, P])
        q, f, key = y[:, HQ:HQ + 2, :], y[:, HF:HF + 2, :], y[:, HF:HF + 2, :]
        D_, ABS, LN, MIN, LP1, LP0, LOG_LB, LOG_1M = range(8)
        z0, z1 = vec[:, V1["lb"]:V1["lb"] + 2], vec[:, V1["lb"] + 2:V1["lb"] + 4]
        first = vec[:, V1["is_first"]:V1["is_first"] + 1]

        with stage(nc, "hgrn_gates", "steps", "acts", "to_act") as (block, s):
            @block.vector
            def _(dve):
                done = [0]

                def step(ins):
                    done[0] += 1
                    ins.then_inc(s["steps"], 1)
                    dve.wait_ge(s["steps"], done[0])

                step(nc.vector.tensor_tensor(lb[:, D_, :], z1, z0, ALU.subtract))
                step(nc.vector.scalar_tensor_tensor(out=lb[:, ABS, :], in0=lb[:, D_, :], scalar=-1.0, in1=lb[:, D_, :], op0=ALU.mult, op1=ALU.max))
                step(nc.vector.scalar_tensor_tensor(out=a[:], in0=f, scalar=-1.0, in1=f, op0=ALU.mult, op1=ALU.max))
                dve.sem_inc(s["to_act"], 1)
                step(nc.vector.memset(zeros[:], 0.0))
                dve.wait_ge(s["acts"], 4)
                step(nc.vector.tensor_scalar(lb[:, MIN, :], lb[:, D_, :], 0.0, None, ALU.min))
                step(nc.vector.tensor_tensor(lb[:, LP1, :], lb[:, MIN, :], lb[:, LN, :], ALU.subtract))
                step(nc.vector.tensor_tensor(lb[:, LP0, :], lb[:, LP1, :], lb[:, D_, :], ALU.subtract))
                step(nc.vector.tensor_scalar(lb[:, MIN, :], first.broadcast_to([P, 2]), -1.0, 1.0, ALU.mult, ALU.add))
                step(nc.vector.tensor_tensor(lb[:, LOG_1M, :], lb[:, LP0, :], lb[:, MIN, :], ALU.mult))
                step(nc.vector.tensor_tensor(lb[:, LP1, :], lb[:, LP1, :], lb[:, MIN, :], ALU.mult))
                step(nc.vector.scalar_tensor_tensor(out=lb[:, LOG_LB, :], in0=first.broadcast_to([P, 2]), scalar=NEG, in1=lb[:, LP1, :], op0=ALU.mult, op1=ALU.add))
                step(nc.vector.scalar_tensor_tensor(out=b[:], in0=f, scalar=0.0, in1=a[:], op0=ALU.min, op1=ALU.subtract))
                for k in range(2):
                    step(nc.vector.tensor_scalar(b[:, k, :], b[:, k, :], lb[:, LOG_1M, k:k + 1], None, ALU.add))
                for k in range(2):
                    step(nc.vector.tensor_scalar(a[:, k, :], b[:, k, :], lb[:, LOG_LB, k:k + 1], None, ALU.min))
                    step(nc.vector.tensor_scalar(G[:, k, :], b[:, k, :], lb[:, LOG_LB, k:k + 1], None, ALU.max))
                step(nc.vector.tensor_tensor(a[:], a[:], G[:], ALU.subtract))
                dve.sem_inc(s["to_act"], 1)
                dve.wait_ge(s["acts"], 9)
                step(nc.vector.tensor_tensor(b[:], G[:], a[:], ALU.add))
                for k in range(2):
                    step(nc.vector.tensor_tensor_scan(G[:, k, :], b[:, k, :], zeros[:], 0.0, ALU.add, ALU.add))
                    step(nc.vector.tensor_scalar(key[:, k, :], key[:, k, :], lb[:, MIN, k:k + 1], None, ALU.mult))

            @block.scalar
            def _(act):
                done = [0]

                def step(ins):
                    done[0] += 1
                    ins.then_inc(s["acts"], 1)
                    act.wait_ge(s["acts"], done[0])

                act.wait_ge(s["to_act"], 1)
                step(nc.scalar.activation(lb[:, LN, :], lb[:, ABS, :], ACT.Exp, scale=-1.0))
                step(nc.scalar.activation(a[:], a[:], ACT.Exp, scale=-1.0))
                step(nc.scalar.activation(lb[:, LN, :], lb[:, LN, :], ACT.Ln, bias=m.one[:, 0:1]))
                step(nc.scalar.activation(a[:], a[:], ACT.Ln, bias=m.one[:, 0:1]))
                act.wait_ge(s["to_act"], 2)
                step(nc.scalar.activation(a[:], a[:], ACT.Exp))
                step(nc.scalar.activation(lb[:, MIN, :], lb[:, LOG_1M, :], ACT.Exp))
                step(nc.scalar.activation(a[:], a[:], ACT.Ln, bias=m.one[:, 0:1]))
                step(nc.scalar.activation(key, f, ACT.Sigmoid, scale=-1.0))
                step(nc.scalar.activation(q, q, ACT.Silu))

        transpose_tiles(nc, "hgrn_v", m, y[:, HI:HI + 2, :], v_tok)

        diagonal = [(j, j) for j in range(NT)]
        across = [[(0, 1), (2, 3)], [(0, 2), (0, 3), (1, 2), (1, 3)]]
        place = {pair: n for n, pair in enumerate(diagonal + across[0] + across[1])}
        levels = [(0, diagonal)] + [(1 << n, diagonal) for n in range(HG_LEVELS)] + [(P, across[0]), (2 * P, across[1])]
        with stage(nc, "hgrn", "diffs_ready", "exp_ready", "q_ready", "k_ready", "scored", "level_scored", "masked", "added") as (block, s):
            def halves(ap, w, which):
                return ap.rearrange("p t (n two w) -> p (t n) two w", two=2, w=w)[:, :, which, :]

            def bank_of(block, parity):
                return block // 2 % 4 * 2 + parity

            def scores_of(block):
                at = bank_of(block, 0)
                return m.ps[:, at:at + 2, block % 2 * 2 * P:(block % 2 + 1) * 2 * P].rearrange("p a (b t) -> p a b t", b=2)

            def spread4(mask):
                return mask.unsqueeze(1).unsqueeze(1).broadcast_to([P, 2, 2, P])

            def middle(w):
                g = halves(G[:], w, 0)[:, :, w - 1:w]
                return g.broadcast_to([P, S // w, w])

            @block.vector
            def _(dve):
                blocks = 0
                for n, (w, pairs) in enumerate(levels):
                    if n >= 1:
                        if n >= 2:
                            dve.wait_ge(s["k_ready"], n - 1)
                            dve.wait_ge(s["q_ready"], n - 1)
                        nc.vector.tensor_tensor(halves(b[:], w, 0), middle(w), halves(G[:], w, 0), ALU.subtract).then_inc(s["diffs_ready"], 1)
                        nc.vector.tensor_tensor(halves(b[:], w, 1), halves(G[:], w, 1), middle(w), ALU.subtract).then_inc(s["diffs_ready"], 1)
                        dve.wait_ge(s["exp_ready"], n)
                        if n >= 2:
                            dve.wait_ge(s["level_scored"], n)
                        nc.vector.tensor_tensor(q_dec[:], q, b[:], ALU.mult).then_inc(s["q_ready"], 1)
                    for x, pair in enumerate(pairs):
                        dve.wait_ge(s["scored"], blocks // 2 * 2 + 2)
                        scores = scores_of(blocks)
                        into = A[:, place[pair], :, :, :]
                        if w == 0:
                            ins = nc.vector.tensor_tensor(into, scores, spread4(m.ident), ALU.mult)
                        elif w >= P:
                            ins = nc.vector.tensor_copy(into, scores)
                        else:
                            if blocks >= 6:
                                dve.wait_ge(s["added"], blocks - 5)
                            mask = m.masks[:, MASKS["levels"] + (n - 1) * P:MASKS["levels"] + n * P]
                            ins = nc.vector.tensor_tensor(part[:, blocks % 2, :, :, :], scores, spread4(mask), ALU.mult)
                        ins.then_inc(s["masked"], 1)
                        blocks += 1

            @block.gpsimd
            def _(pool):
                blocks = 4
                for n, (w, pairs) in enumerate(levels):
                    if n >= 1:
                        pool.wait_ge(s["exp_ready"], n)
                        if n >= 2:
                            pool.wait_ge(s["level_scored"], n)
                        nc.gpsimd.tensor_tensor(k_dec[:], key, b[:], ALU.mult).then_inc(s["k_ready"], 1)
                    if 1 <= n <= HG_LEVELS:
                        for x, pair in enumerate(pairs):
                            pool.wait_ge(s["masked"], blocks + 1)
                            if blocks >= 8:
                                pool.wait_ge(s["added"], blocks - 7)
                            into = A[:, place[pair], :, :, :].rearrange("p a b t -> p (a b t)")
                            more = part[:, blocks % 2, :, :, :].rearrange("p a b t -> p (a b t)")
                            nc.gpsimd.tensor_tensor(into, into, more, ALU.add).then_inc(s["added"], 1)
                            blocks += 1

            @block.scalar
            def _(act):
                for n in range(1, len(levels)):
                    act.wait_ge(s["diffs_ready"], 2 * n)
                    nc.scalar.activation(b[:], b[:], ACT.Exp).then_inc(s["exp_ready"], 1)

            @block.tensor
            def _(pe):
                blocks = 0
                for n, (w, pairs) in enumerate(levels):
                    kk, qq = (k_dec, q_dec) if n else (key, q)
                    if n >= 1:
                        pe.wait_ge(s["q_ready"], n)
                        pe.wait_ge(s["k_ready"], n)
                    for sT, lT in pairs:
                        if blocks >= 8 and blocks % 2 == 0:
                            pe.wait_ge(s["masked"], blocks - 6)
                        for h in range(4):
                            lo = (h % 2) * HD
                            at = (blocks % 2 * 2 + h // 2) * P
                            mm = nc.tensor.matmul(m.ps[:, bank_of(blocks, h % 2), at:at + P], kk[lo:lo + HD, h // 2, sT * P:(sT + 1) * P],
                                                  qq[lo:lo + HD, h // 2, lT * P:(lT + 1) * P], start=True, stop=True)
                        mm.then_inc(s["scored"], 1)
                        blocks += 1
                    pe.wait_ge(s["scored"], blocks)
                    pe.sem_inc(s["level_scored"], 1)

        with stage(nc, "hgrn_out", "summed", "copied") as (block, s):
            @block.tensor
            def _(pe):
                for h in range(4):
                    for lT in range(NT):
                        for sT in range(lT + 1):
                            mm = nc.tensor.matmul(m.ps[(h % 2) * HD:(h % 2 + 1) * HD, h // 2, lT * P:(lT + 1) * P],
                                                  v_tok[:, sT, h * HD:(h + 1) * HD], A[:, place[sT, lT], h % 2, h // 2, :],
                                                  start=(sT == 0), stop=(sT == lT))
                mm.then_inc(s["summed"], 1)

            @block.vector
            def _(dve):
                dve.wait_ge(s["summed"], 1)
                nc.vector.tensor_copy(a[:], m.ps[:, 0:2, :]).then_inc(s["copied"], 1)

        heads_norm_gate(nc, "hgrn_norm", m, a[:], vec[:, V1["h_g"]:V1["h_g"] + 2], y[:, HG:HG + 2, :], ACT.Silu, dst)


def band_attention(nc, name, m, q, k, v, sinks, bands, reach, dst):
    pairs = k.shape[1]
    nr = len(reach)
    with ExitStack() as tmp:
        def sb(name_, shape):
            return tmp.enter_context(nc.sbuf_tensor(f"{name}_{name_}", shape, F32))

        qs = sb("qs", [P, 4, S])
        k_dup = sb("k_dup", [P, 2, S])
        vs = sb("vs", [P, S])
        v_tok = sb("v_tok", [P, NT, P])
        p = sb("p", [P, 3, nr * P])
        pt = sb("pt", [P, 2, nr * P])
        stat = sb("stat", [P, 8, 8])
        sink = sb("sink", [P, 8])
        MAX, NEG_MAX, SUM, SINK, DEN, REC = range(6)
        units = [(h, b) for h in range(8) for b in range(NT)]
        N = len(units)

        def tiles_of(b):
            return [b + r for r in reach if 0 <= b + r < NT]

        def width(b):
            return len(tiles_of(b)) * P

        def bands_of(b):
            at = next(x for x, r in enumerate(reach) if 0 <= b + r)
            return bands[:, at * P:at * P + width(b)]

        with stage(nc, name, "copied", "v_turned", "v_ready", "scored", "biased", "max_ready", "neg_ready",
                   "exp_ready", "sink_ready", "den_ready", "rec_ready", "normed", "turned", "pt_ready", "summed", "out") as (block, s):
            @block.vector
            def _(dve):
                with dve.Fori(0, pairs) as g:
                    nc.vector.tensor_copy(qs[:], q[:, bass.ds(g * 4, 4), :]).then_inc(s["copied"], 1)
                    for half in range(2):
                        for to in range(2):
                            nc.vector.tensor_copy(k_dup[to * HD:(to + 1) * HD, half:half + 1, :],
                                                  k[half * HD:(half + 1) * HD, bass.ds(g, 1), :]).then_inc(s["copied"], 1)
                    nc.vector.tensor_copy(vs[:], tile_of(v, g)).then_inc(s["copied"], 1)
                    nc.vector.tensor_copy(sink[:], sinks[:, bass.ds(g * 8, 8)]).then_inc(s["copied"], 1)
                    dve.wait_ge(s["v_turned"], g * NT + NT)
                    for b in range(NT):
                        nc.vector.tensor_copy(v_tok[:, b, :], m.ps[:, 7, b * P:(b + 1) * P]).then_inc(s["v_ready"], 1)

                    def finish(n):
                        h, b = units[n]
                        st = stat[:, n % 8, :]
                        dve.wait_ge(s["exp_ready"], g * N + (n + 1))
                        dve.wait_ge(s["sink_ready"], g * N + (n + 1))
                        nc.vector.tensor_tensor(st[:, DEN:DEN + 1], st[:, SUM:SUM + 1], st[:, SINK:SINK + 1], ALU.add).then_inc(s["den_ready"], 1)
                        dve.wait_ge(s["den_ready"], g * N + (n + 1))
                        nc.vector.reciprocal(st[:, REC:REC + 1], st[:, DEN:DEN + 1]).then_inc(s["rec_ready"], 1)
                        dve.wait_ge(s["rec_ready"], g * N + (n + 1))
                        nc.vector.tensor_scalar(p[:, n % 3, 0:width(b)], p[:, n % 3, 0:width(b)], st[:, REC:REC + 1], None, ALU.mult).then_inc(s["normed"], 1)

                    for n, (h, b) in enumerate(units):
                        st = stat[:, n % 8, :]
                        dve.wait_ge(s["scored"], g * N + (n + 1))
                        if n >= 3:
                            dve.wait_ge(s["turned"], g * N + (n - 2))
                        nc.vector.scalar_tensor_tensor(out=p[:, n % 3, 0:width(b)], in0=m.ps[:, n % 2, 0:width(b)], scalar=HD ** -0.5,
                                                       in1=bands_of(b), op0=ALU.mult, op1=ALU.add).then_inc(s["biased"], 1)
                        dve.wait_ge(s["biased"], g * N + (n + 1))
                        nc.vector.tensor_reduce(st[:, MAX:MAX + 1], p[:, n % 3, 0:width(b)], AX_X, ALU.max).then_inc(s["max_ready"], 1)
                        dve.wait_ge(s["max_ready"], g * N + (n + 1))
                        if n == 0:
                            dve.wait_ge(s["copied"], g * 7 + 7)
                        nc.vector.tensor_scalar(st[:, NEG_MAX:NEG_MAX + 1], st[:, MAX:MAX + 1], sink[:, h:h + 1], -1.0, ALU.max, ALU.mult).then_inc(s["neg_ready"], 1)
                        if n >= 1:
                            finish(n - 1)
                    finish(N - 1)
                    dve.wait_ge(s["out"], g * 4 + 4)

            @block.scalar
            def _(act):
                with act.Fori(0, pairs) as g:
                    def take(n):
                        h, b = units[n]
                        act.wait_ge(s["turned"], g * N + (n + 1))
                        if n >= 2:
                            act.wait_ge(s["summed"], g * N + (n - 1))
                        nc.scalar.activation(pt[:, n % 2, 0:width(b)], m.ps[:, 2 + n % 2, 0:width(b)], ACT.Copy).then_inc(s["pt_ready"], 1)
                        if b == NT - 1 and h % 2 == 1 and h >= 3:
                            out(h // 2 - 1)

                    def out(pair):
                        act.wait_ge(s["summed"], g * N + (pair + 1) * 2 * NT)
                        nc.scalar.activation(tile_of(dst, g * 4 + pair), m.ps[:, 4 + pair % 2, :], ACT.Copy).then_inc(s["out"], 1)

                    for n, (h, b) in enumerate(units):
                        st = stat[:, n % 8, :]
                        act.wait_ge(s["neg_ready"], g * N + (n + 1))
                        nc.scalar.activation(p[:, n % 3, 0:width(b)], p[:, n % 3, 0:width(b)], ACT.Exp, bias=st[:, NEG_MAX:NEG_MAX + 1],
                                             accum_out=st[:, SUM:SUM + 1]).then_inc(s["exp_ready"], 1)
                        nc.scalar.activation(st[:, SINK:SINK + 1], sink[:, h:h + 1], ACT.Exp, bias=st[:, NEG_MAX:NEG_MAX + 1]).then_inc(s["sink_ready"], 1)
                        if n >= 2:
                            take(n - 2)
                    take(N - 2)
                    take(N - 1)
                    out(3)

            @block.tensor
            def _(pe):
                with pe.Fori(0, pairs) as g:
                    pe.wait_ge(s["copied"], g * 7 + 7)
                    for b in range(NT):
                        nc.tensor.transpose(m.ps[:, 7, b * P:(b + 1) * P], vs[:, b * P:(b + 1) * P], m.ident).then_inc(s["v_turned"], 1)

                    def turn(n):
                        h, b = units[n]
                        pe.wait_ge(s["normed"], g * N + (n + 1))
                        if n >= 2:
                            pe.wait_ge(s["pt_ready"], g * N + (n - 1))
                        for x in range(len(tiles_of(b))):
                            mm = nc.tensor.transpose(m.ps[:, 2 + n % 2, x * P:(x + 1) * P], p[:, n % 3, x * P:(x + 1) * P], m.ident)
                        mm.then_inc(s["turned"], 1)

                    def outputs(n):
                        h, b = units[n]
                        pe.wait_ge(s["pt_ready"], g * N + (n + 1))
                        if n == 0:
                            pe.wait_ge(s["v_ready"], g * NT + NT)
                        if h % 2 == 0 and b == 0 and h >= 4:
                            pe.wait_ge(s["out"], g * 4 + (h // 2 - 1))
                        head = (h // 4) * HD
                        for x, t in enumerate(tiles_of(b)):
                            mm = nc.tensor.matmul(m.ps[(h % 2) * HD:(h % 2 + 1) * HD, 4 + h // 2 % 2, b * P:(b + 1) * P],
                                                  v_tok[:, t, head:head + HD], pt[:, n % 2, x * P:(x + 1) * P],
                                                  start=(x == 0), stop=(x == len(tiles_of(b)) - 1))
                        mm.then_inc(s["summed"], 1)

                    for n, (h, b) in enumerate(units):
                        lo = (h % 2) * HD
                        if n >= 2:
                            pe.wait_ge(s["biased"], g * N + (n - 1))
                        t = tiles_of(b)
                        nc.tensor.matmul(m.ps[:, n % 2, 0:width(b)], qs[lo:lo + HD, h // 2, b * P:(b + 1) * P],
                                         k_dup[lo:lo + HD, h // 4, t[0] * P:(t[-1] + 1) * P], start=True, stop=True).then_inc(s["scored"], 1)
                        if n >= 2:
                            turn(n - 2)
                        if n >= 3:
                            outputs(n - 3)
                    turn(N - 2)
                    outputs(N - 3)
                    turn(N - 1)
                    outputs(N - 2)
                    outputs(N - 1)


def first_block(nc, m, a):
    with ExitStack() as held:
        def sb(name, shape):
            return held.enter_context(nc.sbuf_tensor(f"first_{name}", shape, F32))

        vec = sb("vec", [P, V1_W])
        m.sin = sb("sin", [P, S])
        m.cos = sb("cos", [P, S])
        m.masks = sb("masks", [P, MASKS_W])
        bands = sb("bands", [P, BANDS1_W])
        gates = sb("gates", [P, S])
        load(nc, "first_tables", [(m.masks[:], a["masks"]), (bands[:], a["bands1"])])
        rope_table(nc, "rope1", m, a["positions"])
        with nc.Fori(0, DEPTH) as layer:
            load(nc, "layer_vec", [(vec[:], row_of(a["vec1"], layer))])

            def column(name, n):
                return vec[:, V1[name]:V1[name] + n]

            with nc.sbuf_tensor("y", [P, NIN, S], F32) as y:
                with product_memory(nc, m):
                    linear(nc, "in_gates", m, a["w_gates"], layer, 1, DT, 1, first=norm_first(nc, m, m.x, column("in_g", DT)),
                           on_act=to_tiles(nc, m, gates[:].unsqueeze(1), ACT.Identity, column("b_i", 1)))
                    linear(nc, "in_proj", m, a["w_in"], layer * NIN, NIN, DT, 2, on_act=to_tiles(nc, m, y, ACT.Identity, column("b_in", NIN)))
                conv_silu(nc, m, y[:, MQ:MQ + 4, :], vec)
                mlstm(nc, m, vec, y, gates, m.h[:, 0:2, :])
                hgrn(nc, m, vec, y, m.h[:, 2:4, :])
                heads_norm_rope(nc, "q1", m, y[:, SQ:SQ + 4, :], column("q_g", 1))
                heads_norm_rope(nc, "k1", m, y[:, SK:SK + 1, :], column("k_g", 1))
                band_attention(nc, "swa1", m, y[:, SQ:SQ + 4, :], y[:, SK:SK + 1, :], y[:, SV:SV + 1, :], column("sinks", 8),
                               bands, (-1, 0), m.h[:, 4:8, :])
            with product_memory(nc, m):
                linear(nc, "out1", m, a["w_out"], layer * DT, DT, DT, 4, first=split_first(nc, m, m.h[:]), on_dve=add_to_x(nc, m))
                squared_relu_mlp(nc, m, a, layer, column("mlp_g", DT))
                gated_embedding(nc, m, a, layer, column("ple_g", DT), column("post_g", DT))


def squared_relu_mlp(nc, m, a, layer, gain):
    half = FFT // 2
    with ExitStack() as tmp:
        hid_hi = tmp.enter_context(nc.sbuf_tensor("hidden_hi", [P, half, S], F32R))
        hid_lo = tmp.enter_context(nc.sbuf_tensor("hidden_lo", [P, half, S], F32R))

        def on_act(act, t, u, s, used):
            act.wait_ge(s["squared"], t + 1)
            nc.scalar.activation(tile_of(hid_hi, t), m.sq[:, 4 + u, :], ACT.Copy).then_inc(s["hidden_hi"], 1)

        def on_dve(dve, t, u, s, used):
            dve.wait_ge(s["slots_used"], used)
            nc.vector.tensor_scalar(m.sq[:, u, :], m.ps[:, u, :], 0.0, None, ALU.max).then_inc(s["banks_free"], 1)
            dve.wait_ge(s["banks_free"], t + 5)
            dve.wait_ge(s["hidden_lo"], t + 1)
            nc.vector.tensor_tensor(m.sq[:, 4 + u, :], m.sq[:, u, :], m.sq[:, u, :], ALU.mult).then_inc(s["squared"], 1)

        def on_pool(pool, t, u, s, used):
            pool.wait_ge(s["hidden_hi"], t + 1)
            nc.gpsimd.tensor_tensor(tile_of(hid_lo, t), m.sq[:, 4 + u, :], tile_of(hid_hi, t).bitcast(F32), ALU.subtract).then_inc(s["hidden_lo"], 1)

        for n in range(2):
            linear(nc, f"up1_{n}", m, a["w_up"], layer * FFT + n * half, half, DT, 4, signals=("squared", "hidden_hi", "hidden_lo"),
                   first=norm_first(nc, m, m.x, gain) if n == 0 else None,
                   on_act=on_act, on_dve=on_dve, on_pool=on_pool, at_start=lambda pe, s: pe.sem_inc(s["hidden_lo"], 4))
            linear(nc, f"down1_{n}", m, a["w_down"], layer * (DT * 4) + n * (DT * 2), DT, DT, 2, parts=2,
                   rhs=lambda k: (hid_hi[:, k, :], hid_lo[:, k, :]), on_dve=add_to_x(nc, m))


def gated_embedding(nc, m, a, layer, gain, post_gain):
    with ExitStack() as tmp:
        gate = tmp.enter_context(nc.sbuf_tensor("ple_gate", [P, DT, S], F32))
        e = tmp.enter_context(nc.sbuf_tensor("ple_e", [P, DT, S], F32))
        pt = tmp.enter_context(nc.sbuf_tensor("ple_pt", [P, PLE // P, S], F32))
        load(nc, "ple_in", [(pt[:], a["p_t"][bass.ds(layer, 1)].rearrange("a p k n -> p (a k) n"))])
        linear(nc, "ple_gate", m, a["w_gate"], layer * DT, DT, DT, 4, first=norm_first(nc, m, m.x, gain), on_act=to_tiles(nc, m, gate, ACT.Sigmoid))
        linear(nc, "ple_proj", m, a["w_ple"], layer * DT, DT, PLE // P, 4, first=split_first(nc, m, pt[:]), on_act=to_tiles(nc, m, e))
        norm(nc, "post_norm", m, e, post_gain, e)
        with stage(nc, "ple_add", "gated", "added") as (block, s):
            @block.vector
            def _(dve):
                nc.vector.tensor_tensor(e[:], e[:], gate[:], ALU.mult).then_inc(s["gated"], 1)
                dve.wait_ge(s["gated"], 1)
                nc.vector.tensor_tensor(m.x[:], m.x[:], e[:], ALU.add).then_inc(s["added"], 1)


FFN_PARTS = (12, 10)


def conv_ffn(nc, m, a, vec, layer):
    with product_memory(nc, m, max(FFN_PARTS)), ExitStack() as tmp:
        hid_hi = tmp.enter_context(nc.sbuf_tensor(f"ffn{layer}_hi", [P, max(FFN_PARTS), S], F32R))
        hid_lo = tmp.enter_context(nc.sbuf_tensor(f"ffn{layer}_lo", [P, max(FFN_PARTS), S], F32R))
        acc = tmp.enter_context(nc.sbuf_tensor(f"ffn{layer}_acc", [P, 4, S], F32))
        at = 0
        for n, tiles in enumerate(FFN_PARTS):
            def weight(tap, t):
                return vec[:, bass.ds(t + (V2["conv_w"] + tap * 2 * GT + 2 * at), 1)]

            def on_act(act, t, u, s, used):
                act.wait_ge(s["slots_used"], used)
                act.wait_ge(s["acc_free"], t + 1)
                bias = vec[:, bass.ds(t + (V2["conv_b"] + 2 * at), 1)]
                nc.scalar.activation(acc[:, u, :], m.ps[:, u, :], ACT.Identity, scale=weight(1, t), bias=bias).then_inc(s["centred"], 1)
                if u % 2 == 1:
                    act.wait_ge(s["banks_free"], t + 4)
                    nc.scalar.activation(acc[:, u - 1, :], acc[:, u - 1, :], ACT.Silu).then_inc(s["gate_ready"], 2)
                    act.wait_ge(s["multiplied"], t + 1)
                    hi = hid_hi[:, bass.ds(half_of(t), 1), :].rearrange("p a n -> p (a n)")
                    nc.scalar.activation(hi, m.sq[:, u, :], ACT.Copy).then_inc(s["hidden_hi"], 2)

            def on_dve(dve, t, u, s, used):
                dve.wait_ge(s["centred"], t + 1)
                nc.vector.scalar_tensor_tensor(out=acc[:, u, 1:S], in0=m.ps[:, u, 0:S - 1], scalar=weight(0, t), in1=acc[:, u, 1:S],
                                               op0=ALU.mult, op1=ALU.add).then_inc(s["first_tap"], 1)
                dve.wait_ge(s["first_tap"], t + 1)
                nc.vector.scalar_tensor_tensor(out=acc[:, u, 0:S - 1], in0=m.ps[:, u, 1:S], scalar=weight(2, t), in1=acc[:, u, 0:S - 1],
                                               op0=ALU.mult, op1=ALU.add).then_inc(s["banks_free"], 1)
                if u % 2 == 1:
                    dve.wait_ge(s["banks_free"], t + 5)
                    dve.wait_ge(s["gate_ready"], t + 1)
                    dve.wait_ge(s["hidden_lo"], t + 1)
                    nc.vector.tensor_tensor(m.sq[:, u, :], acc[:, u - 1, :], acc[:, u, :], ALU.mult).then_inc(s["multiplied"], 2)
                    dve.wait_ge(s["multiplied"], t + 1)
                    dve.sem_inc(s["acc_free"], 2)

            def half_of(t):
                return (t - 1) // 2

            def on_pool(pool, t, u, s, used):
                if u % 2 == 1:
                    pool.wait_ge(s["hidden_hi"], t + 1)
                    hi, lo = (h[:, bass.ds(half_of(t), 1), :].rearrange("p a n -> p (a n)") for h in (hid_hi, hid_lo))
                    nc.gpsimd.tensor_tensor(lo, m.sq[:, u, :], hi.bitcast(F32), ALU.subtract).then_inc(s["hidden_lo"], 2)

            def at_start(pe, s):
                pe.sem_inc(s["acc_free"], 4)
                pe.sem_inc(s["hidden_lo"], 4)

            linear(nc, f"ffn{layer}_up{n}", m, a["w_ffn_up"], layer * (2 * GT) + 2 * at, 2 * tiles, DT, 4,
                   signals=("acc_free", "centred", "first_tap", "gate_ready", "multiplied", "hidden_hi", "hidden_lo"), at_start=at_start,
                   first=norm_first(nc, m, m.x, vec[:, V2["ch_g"]:V2["ch_g"] + DT]) if n == 0 else None,
                   on_act=on_act, on_dve=on_dve, on_pool=on_pool)
            linear(nc, f"ffn{layer}_down{n}", m, a[f"w_ffn_down{n}"], layer * DT, DT, tiles, 4,
                   rhs=lambda k: (hid_hi[:, k, :], hid_lo[:, k, :]), on_dve=add_to_x(nc, m))
            at += tiles


R_, K_, V_, SW, AA, G_ = 0, 1, 2, 3, 5, 7


def rwkv_inputs(nc, m, a, vec, keep):
    with product_memory(nc, m), ExitStack() as tmp:
        def sb(name, shape):
            return tmp.enter_context(nc.sbuf_tensor(f"rwkv_{name}", shape, F32))

        xx = m.sq
        mixed = sb("mixed", [P, DT, S])
        buf = sb("buf", [P, DT, S])
        low = sb("low", [P, 2, S])
        wide = sb("wide", [P, D])
        with stage(nc, "rwkv_xx", "steps") as (block, s):
            @block.vector
            def _(dve):
                nc.vector.tensor_tensor(xx[:, :, 1:S - 1], m.h[:, :, 0:S - 2], m.h[:, :, 2:S], ALU.add).then_inc(s["steps"], 1)
                nc.vector.tensor_copy(xx[:, :, 0:1], m.h[:, :, 1:2]).then_inc(s["steps"], 1)
                nc.vector.tensor_copy(xx[:, :, S - 1:S], m.h[:, :, S - 2:S - 1]).then_inc(s["steps"], 1)
                dve.wait_ge(s["steps"], 3)
                nc.vector.scalar_tensor_tensor(out=xx[:], in0=xx[:], scalar=0.5, in1=m.h[:], op0=ALU.mult, op1=ALU.subtract).then_inc(s["steps"], 1)

        def mix(i):
            mu = vec[:, VR["mu"] + i * DT:VR["mu"] + (i + 1) * DT]
            return mix_first(nc, m, xx, mu, mixed)

        def stored(what):
            def at_end(sp, s, used):
                sp.wait_ge(s["banks_free"], DT + 4)
                sp.dma_start(keep[what].rearrange("k p n -> p k n"), buf[:]).then_inc(s["stored"], 16)
                sp.wait_ge(s["stored"], 16)
            return {"signals": ("stored",), "at_end": at_end}

        for what, i, w in ((R_, 0, a["w_r"]), (K_, 2, a["w_k"]), (V_, 3, a["w_v"])):
            linear(nc, f"rwkv_p{what}", m, w, 0, DT, DT, 4, first=mix(i), on_act=to_tiles(nc, m, buf), **stored(what))

        for what, i, w1, w2, bias, func in ((SW, 1, a["w_w1"], a["w_w2"], VR["w0"], ACT.Tanh), (AA, 4, a["w_a1"], a["w_a2"], VR["a0"], ACT.Copy)):
            linear(nc, f"rwkv_low{what}", m, w1, 0, 1, DT, 1, first=mix(i), on_act=to_tiles(nc, m, low, func))
            load(nc, f"rwkv_wide{what}", [(wide[:], w2)])
            for d in range(2):
                lo = d * HD
                with stage(nc, f"rwkv_back{what}{d}", "product_ready", "taken", "stored") as (block, s):
                    @block.tensor
                    def _(pe):
                        for k in range(DT):
                            nc.tensor.matmul(m.ps[:, k, :], wide[lo:lo + HD, k * P:(k + 1) * P], low[lo:lo + HD, 0, :], start=True, stop=True).then_inc(s["product_ready"], 1)

                    @block.scalar
                    def _(act):
                        for k in range(DT):
                            act.wait_ge(s["product_ready"], k + 1)
                            at = bias + d * DT + k
                            nc.scalar.activation(buf[:, k, :], m.ps[:, k, :], ACT.Sigmoid, bias=vec[:, at:at + 1]).then_inc(s["taken"], 1)

                    @block.sync
                    def _(sp):
                        for k in range(DT):
                            sp.wait_ge(s["taken"], k + 1)
                            sp.dma_start(keep[what + d][k], buf[:, k, :]).then_inc(s["stored"], 16)
                        sp.wait_ge(s["stored"], DT * 16)

        linear(nc, "rwkv_g1", m, a["w_g1"], 0, 2, DT, 2, first=mix(5), on_act=to_tiles(nc, m, low, ACT.Sigmoid))
        linear(nc, "rwkv_g2", m, a["w_g2"], 0, DT, 2, 4, first=split_first(nc, m, low), on_act=to_tiles(nc, m, buf), **stored(G_))


def rwkv_heads(nc, m, a, vec, keep):
    with ExitStack() as tmp:
        def sb(name, shape):
            return tmp.enter_context(nc.sbuf_tensor(f"heads_{name}", shape, F32))

        L = m.sq
        masks = sb("masks", [P, RMASKS_W])
        mask4 = sb("mask4", [P, 4, P])
        restart = sb("restart", [P, S])
        par = sb("par", [P, 5, 1])
        k_a_rest = sb("k_a_rest", [P, 1])
        AR = sb("AR", [P, 2, NT, 2, P])
        BK = sb("BK", [P, 2, 2, S])
        V2_ = sb("V2", [P, S])
        bonus = sb("bonus", [P, S])
        tok = sb("tok", [P, 2, NT, 3, P])
        M = sb("M", [P, NT, 4, 4, P])
        X = sb("X", [P, NT, 4, P])
        XT = sb("XT", [P, NT, 4, P])
        T1 = sb("T1", [P, 2, 4, P])
        NM = sb("NM", [P, 2, 4, P])
        p_end = sb("p_end", [P, 2, NT, 2])
        b_own = sb("b_own", [P, 2, NT, 2, P])
        state = sb("state", [P, 2, P])
        grown = sb("grown", [P, 2, P])
        gn_eps = sb("gn_eps", [P, 1])
        t16 = M[:].rearrange("p t i k n -> p (t i) (k n)")
        KR, KK, KD, B_, GS, PM, EG, EN, EP = 0, 1, 2, 4, 6, 8, 10, 12, 14
        WT = X
        ZV = T1[:].rearrange("p a i n -> p (a i n)").rearrange("p (t i e) -> p t i e", t=NT, i=4)
        U0 = NM[:].rearrange("p a i n -> p (a i n)").rearrange("p (t i e) -> p t i e", t=NT, i=4)
        U = sb("U", [P, NT, 2, P])
        KV = sb("KV", [P, 2, NT, 2, P])

        load(nc, "heads_tables", [(masks[:], a["rmasks"]), (restart[:], a["restart"])])
        with stage(nc, "heads_mask4", "copied") as (block, s):
            @block.vector
            def _(dve):
                for k in range(4):
                    nc.vector.tensor_copy(mask4[:, k, :], masks[:, RMASKS["before"] + (k % 2) * P:RMASKS["before"] + (k % 2 + 1) * P]).then_inc(s["copied"], 1)
                nc.vector.memset(gn_eps[:], 64e-5).then_inc(s["copied"], 1)
                nc.vector.memset(b_own[:], 0.0).then_inc(s["copied"], 1)
                nc.vector.memset(KV[:], 0.0).then_inc(s["copied"], 1)

        def turned(ap, d):
            return ap if d == 0 else ap[:, ::-1]

        with nc.Fori(0, DT) as c:
            with stage(nc, "heads_scale", "loaded*8", "steps", "par_ready", "factor_ready", "kd_ready", "v_turned", "squares_ready", "kk_sums", "root_ready", "sums_ready", "exps_ready", "bonus_in", "bonus_sums", "to_square") as (block, s):
                @block.sync
                def _(sp):
                    for w in (K_, SW, AA, SW + 1, AA + 1, R_, V_, G_):
                        sp.dma_start(L[:, w, :], row_of(keep[w], c)).then_inc(s["loaded"][w], 16)
                    sp.wait_ge(s["loaded"][G_], 16)

                @block.vector
                def _(dve):
                    done = [0]

                    def step(ins):
                        done[0] += 1
                        ins.then_inc(s["steps"], 1)
                        dve.wait_ge(s["steps"], done[0])

                    def step_on(ins):
                        done[0] += 1
                        ins.then_inc(s["steps"], 1)

                    def arrived(w):
                        dve.wait_ge(s["loaded"][w], 16)

                    params = vec[:, VR["k_k"]:VR["k_k"] + 5 * DT].rearrange("p (w c) -> p w c", c=DT)
                    step(nc.vector.tensor_copy(par[:], params[:, :, bass.ds(c, 1)]))
                    step(nc.vector.tensor_scalar(k_a_rest[:], par[:, 1, :], -1.0, 1.0, ALU.mult, ALU.add))
                    dve.sem_inc(s["par_ready"], 1)
                    arrived(K_)
                    step(nc.vector.tensor_scalar(t16[:, KR, :], L[:, K_, :], par[:, 0, :], None, ALU.mult))
                    dve.sem_inc(s["to_square"], 1)
                    for d in range(2):
                        sw = turned(L[:, SW + d, :], d)
                        arrived(SW + d)
                        step(nc.vector.tensor_tensor_scan(t16[:, GS + d, :], restart[:], sw, 0.0, ALU.mult, ALU.add))
                        step(nc.vector.tensor_tensor(t16[:, PM + d, :], t16[:, GS + d, :], sw, ALU.subtract))
                        dve.sem_inc(s["sums_ready"], 1)
                    dve.wait_ge(s["root_ready"], 1)
                    step(nc.vector.tensor_scalar(t16[:, KK, :], t16[:, KK, :], 1e-12, None, ALU.max))
                    step(nc.vector.reciprocal(t16[:, KK, :], t16[:, KK, :]))
                    step(nc.vector.tensor_tensor(t16[:, KK, :], t16[:, KK, :], t16[:, KR, :], ALU.mult))
                    arrived(AA)
                    arrived(AA + 1)
                    arrived(R_)
                    arrived(V_)
                    for d in range(2):
                        step(nc.vector.tensor_tensor(t16[:, B_ + d, :], t16[:, KK, :], L[:, AA + d, :], ALU.mult))
                        dve.wait_ge(s["exps_ready"], 3 * d + 3)
                        def by_tile(ap):
                            return ap.rearrange("p (t n) -> p t n", n=P)
                        step_on(nc.vector.tensor_tensor(AR[:, d, :, 1, :], by_tile(turned(L[:, R_, :], d)), by_tile(t16[:, EG + d, :]), ALU.mult))
                        step_on(nc.vector.scalar_tensor_tensor(out=AR[:, d, :, 0, :], in0=by_tile(turned(t16[:, KK, :], d)), scalar=-1.0,
                                                            in1=by_tile(t16[:, EP + d, :]), op0=ALU.mult, op1=ALU.mult))
                        step_on(nc.vector.tensor_tensor(BK[:, 0, d, :], turned(t16[:, B_ + d, :], d), t16[:, EN + d, :], ALU.mult))
                        dve.wait_ge(s["kd_ready"], 3)
                        step_on(nc.vector.tensor_tensor(BK[:, 1, d, :], turned(t16[:, KD + d, :], d), t16[:, EN + d, :], ALU.mult))
                        ends = t16[:, EG + d, RW_CHUNK - 1::RW_CHUNK].rearrange("p (t u) -> p u t", u=2)
                        step(nc.vector.tensor_copy(p_end[:, :, :, d], ends))
                        if d == 0:
                            step(nc.vector.scalar_tensor_tensor(out=bonus[:], in0=bonus[:], scalar=par[:, 2, :], in1=L[:, R_, :], op0=ALU.mult, op1=ALU.mult))
                            dve.sem_inc(s["bonus_in"], 1)
                    dve.wait_ge(s["bonus_sums"], 1)
                    step(nc.vector.tensor_tensor(bonus[:], m.ps[:, 1, :], L[:, V_, :], ALU.mult))

                @block.gpsimd
                def _(pool):
                    for d in range(2):
                        pool.wait_ge(s["loaded"][K_], 16)
                        pool.wait_ge(s["factor_ready"], d + 1)
                        nc.gpsimd.tensor_tensor(t16[:, KD + d, :], t16[:, KD + d, :], L[:, K_, :], ALU.mult).then_inc(s["kd_ready"], 1)
                    pool.wait_ge(s["kd_ready"], 2)
                    nc.gpsimd.tensor_tensor(bonus[:], t16[:, KD, :], t16[:, KD + 1, :], ALU.add).then_inc(s["kd_ready"], 1)

                @block.scalar
                def _(act):
                    act.wait_ge(s["to_square"], 1)
                    nc.scalar.activation(t16[:, KK, :], t16[:, KR, :], ACT.Square).then_inc(s["squares_ready"], 1)
                    act.wait_ge(s["par_ready"], 1)
                    for d in range(2):
                        act.wait_ge(s["loaded"][AA + d], 16)
                        nc.scalar.activation(t16[:, KD + d, :], L[:, AA + d, :], ACT.Identity, scale=par[:, 1, :], bias=k_a_rest[:, 0:1]).then_inc(s["factor_ready"], 1)
                    act.wait_ge(s["kk_sums"], 1)
                    nc.scalar.activation(t16[:, KK, :], m.ps[:, 0, :], ACT.Sqrt).then_inc(s["root_ready"], 1)
                    for d in range(2):
                        act.wait_ge(s["sums_ready"], d + 1)
                        nc.scalar.activation(t16[:, EG + d, :], t16[:, GS + d, :], ACT.Exp, scale=-DECAY_SCALE).then_inc(s["exps_ready"], 1)
                        nc.scalar.activation(t16[:, EN + d, :], t16[:, GS + d, :], ACT.Exp, scale=DECAY_SCALE).then_inc(s["exps_ready"], 1)
                        nc.scalar.activation(t16[:, EP + d, :], t16[:, PM + d, :], ACT.Exp, scale=-DECAY_SCALE).then_inc(s["exps_ready"], 1)
                    act.wait_ge(s["loaded"][V_], 16)
                    nc.scalar.activation(V2_[:], L[:, V_, ::-1], ACT.Copy).then_inc(s["v_turned"], 1)

                @block.tensor
                def _(pe):
                    pe.wait_ge(s["squares_ready"], 1)
                    nc.tensor.matmul(m.ps[:, 0, :], m.head_ones, t16[:, KK, :], start=True, stop=True).then_inc(s["kk_sums"], 1)
                    pe.wait_ge(s["bonus_in"], 1)
                    nc.tensor.matmul(m.ps[:, 1, :], m.head_ones, bonus[:], start=True, stop=True).then_inc(s["bonus_sums"], 1)

            with stage(nc, "heads_grams", "products", "masked", "x_masked", "started", "steps", "turned", "turned_taken") as (block, s):
                @block.tensor
                def _(pe):
                    def turn(n):
                        d, t = n // NT, n % NT
                        at = slice(t * P, (t + 1) * P)
                        vv = L[:, V_, at] if d == 0 else V2_[:, at]
                        if n >= 2:
                            pe.wait_ge(s["turned_taken"], 2 * (n - 1))
                        for kind, src in enumerate((AR[:, d, t, 0, :], BK[:, 1, d, at], vv, BK[:, 0, d, at])):
                            mm = nc.tensor.transpose(m.ps[:, 6 + n % 2, kind * P:(kind + 1) * P], src, m.ident)
                        mm.then_inc(s["turned"], 1)

                    for n in range(8):
                        turn(n)
                    for t in range(NT):
                        at = slice(t * P, (t + 1) * P)
                        for inst in range(4):
                            hh, d = inst // 2, inst % 2
                            lo = slice(hh * HD, (hh + 1) * HD)
                            ar = AR[lo, d, t, :, :].rearrange("p a n -> p (a n)")
                            if t >= 1:
                                pe.wait_ge(s["masked"], 4 * t - 3 + inst)
                                if d == 0:
                                    pe.wait_ge(s["x_masked"], 2 * t - 1 + hh)
                            nc.tensor.matmul(m.ps[:, inst, 0:2 * P], BK[lo, 0, d, at], ar, start=True, stop=True)
                            nc.tensor.matmul(m.ps[:, inst, 2 * P:4 * P], BK[lo, 1, d, at], ar, start=True, stop=True)
                            nc.tensor.matmul(m.ps[:, 4 + hh, d * P:(d + 1) * P], AR[lo, d, t, 0, :], BK[lo, 0, d, at], start=True, stop=True).then_inc(s["products"], 1)

                @block.scalar
                def _(act):
                    for n in range(8):
                        d, t = n // NT, n % NT
                        act.wait_ge(s["turned"], n + 1)
                        own = b_own[:, d, t, :, :].rearrange("p a n -> p (a n)").rearrange("p (q e) -> p q e", e=HD)[:, 0::3, :]
                        nc.scalar.activation(tok[:, d, t, :, :].rearrange("p k n -> p (k n)"), m.ps[:, 6 + n % 2, 0:3 * P], ACT.Copy).then_inc(s["turned_taken"], 1)
                        nc.scalar.activation(own, m.ps[:, 6 + n % 2, 3 * P:4 * P].rearrange("p (q e) -> p q e", e=HD), ACT.Copy).then_inc(s["turned_taken"], 1)

                @block.vector
                def _(dve):
                    for t in range(NT):
                        for inst in range(4):
                            dve.wait_ge(s["products"], 4 * t + inst + 1)
                            nc.vector.tensor_tensor(M[:, t, inst, :, :], m.ps[:, inst, :].rearrange("p (k n) -> p k n", k=4), mask4[:], ALU.mult).then_inc(s["masked"], 1)
                            if inst % 2 == 1:
                                hh = inst // 2
                                nc.vector.tensor_tensor(X[:, t, 2 * hh:2 * hh + 2, :], m.ps[:, 4 + hh, 0:2 * P].rearrange("p (d n) -> p d n", d=2),
                                                        spread(masks[:, RMASKS["pair"]:RMASKS["pair"] + P], 2), ALU.mult).then_inc(s["x_masked"], 1)

                @block.gpsimd
                def _(pool):
                    for t in range(NT):
                        pool.wait_ge(s["masked"], 4 * t + 4)
                        nc.gpsimd.tensor_tensor(XT[:, t, :, :], M[:, t, :, 0, :], spread(masks[:, RMASKS["pair_t"]:RMASKS["pair_t"] + P], 4), ALU.mult).then_inc(s["started"], 1)
                        pool.wait_ge(s["x_masked"], 2 * t + 2)
                        nc.gpsimd.tensor_tensor(X[:, t, :, :], X[:, t, :, :], spread(m.ident, 4), ALU.add).then_inc(s["steps"], 1)
                        pool.wait_ge(s["started"], t + 1)
                        nc.gpsimd.tensor_tensor(XT[:, t, :, :], XT[:, t, :, :], spread(m.ident, 4), ALU.add).then_inc(s["steps"], 1)

            units = [(level, t) for level in range(RW_LEVELS) for t in range(NT)]
            with stage(nc, "heads_merge", "part_ready", "inner_ready", "inner_taken", "outer_ready", "x_added", "added") as (block, s):
                @block.gpsimd
                def _(pool):
                    for n, (level, t) in enumerate(units):
                        if n >= 2:
                            pool.wait_ge(s["inner_ready"], n - 1)
                        mask = masks[:, RMASKS["merge"] + level * P:RMASKS["merge"] + (level + 1) * P]
                        nc.gpsimd.tensor_tensor(NM[:, n % 2, :, :], M[:, t, :, 0, :], spread(mask, 4), ALU.mult).then_inc(s["part_ready"], 1)

                @block.tensor
                def _(pe):
                    def outer(n):
                        level, t = units[n]
                        pe.wait_ge(s["inner_taken"], n + 1)
                        if n >= 2:
                            pe.wait_ge(s["added"], n - 1)
                        for i in range(4):
                            if level < RW_LEVELS - 1:
                                nc.tensor.matmul(m.ps[:, 2 + n % 2, i * P:(i + 1) * P], XT[:, t, i, :], T1[:, n % 2, i, :], start=True, stop=True)
                            mm = nc.tensor.matmul(m.ps[:, 4 + n % 2, i * P:(i + 1) * P], T1[:, n % 2, i, :], XT[:, t, i, :], start=True, stop=True)
                        mm.then_inc(s["outer_ready"], 1)

                    for n, (level, t) in enumerate(units):
                        pe.wait_ge(s["part_ready"], n + 1)
                        if n >= NT:
                            pe.wait_ge(s["added"], n - NT + 1)
                        if n >= 2:
                            pe.wait_ge(s["inner_taken"], n - 1)
                        for i in range(4):
                            mm = nc.tensor.matmul(m.ps[:, n % 2, i * P:(i + 1) * P], NM[:, n % 2, i, :], X[:, t, i, :], start=True, stop=True)
                        mm.then_inc(s["inner_ready"], 1)
                        if n >= 1:
                            outer(n - 1)
                    outer(len(units) - 1)

                @block.scalar
                def _(act):
                    for n, (level, t) in enumerate(units):
                        act.wait_ge(s["inner_ready"], n + 1)
                        if n >= 2:
                            act.wait_ge(s["outer_ready"], n - 1)
                        nc.scalar.activation(T1[:, n % 2, :, :].rearrange("p i n -> p (i n)"), m.ps[:, n % 2, :], ACT.Copy).then_inc(s["inner_taken"], 1)

                @block.vector
                def _(dve):
                    for n, (level, t) in enumerate(units):
                        dve.wait_ge(s["outer_ready"], n + 1)
                        x, xt = (ap[:, t, :, :].rearrange("p i n -> p (i n)") for ap in (X, XT))
                        if level < RW_LEVELS - 1:
                            nc.vector.tensor_tensor(x, x, m.ps[:, 2 + n % 2, :], ALU.add).then_inc(s["x_added"], 1)
                            dve.wait_ge(s["x_added"], n + 1)
                        nc.vector.tensor_tensor(xt, xt, m.ps[:, 4 + n % 2, :], ALU.add).then_inc(s["added"], 1)

            with stage(nc, "heads_scan", "v_summed", "kv_ready", "wt_ready", "u0_ready", "cleared", "zv_taken", "kv_taken", "wt_taken", "u0_taken",
                       "from_state*2", "u_ready*2", "update_ready*2", "grown*2", "state_ready*2", "out_ready", "inter_taken", "steps",
                       "centred", "sums", "squared", "root_ready") as (block, s):
                @block.tensor
                def _(pe):
                    def each():
                        for t in range(NT):
                            for inst in range(4):
                                hh, d = inst // 2, inst % 2
                                yield t, inst, d, slice(hh * HD, (hh + 1) * HD), slice((t % 2 * 4 + d * 2 + hh) * HD, (t % 2 * 4 + d * 2 + hh + 1) * HD)

                    for t, inst, d, e, at in each():
                        mm = nc.tensor.matmul(m.ps[:, 2 + t // 2, at], M[:, t, inst, 2, :], tok[:, d, t, 2, e], start=True, stop=True)
                    mm.then_inc(s["v_summed"], 1)
                    for u in range(2):
                        on = slice(u * RW_CHUNK, (u + 1) * RW_CHUNK)
                        for t in range(NT):
                            for d in range(2):
                                at = (t % 2 * 2 + d) * P
                                mm = nc.tensor.matmul(m.ps[:, 4 + 2 * u + t // 2, at:at + P], tok[on, d, t, 1, :], tok[on, d, t, 2, :], start=True, stop=True)
                    mm.then_inc(s["kv_ready"], 1)
                    for t, inst, d, e, _ in each():
                        at = (t % 2 * 2 + d) * P
                        mm = nc.tensor.matmul(m.ps[e, t // 2, at:at + P], tok[:, d, t, 0, e], XT[:, t, inst, :], start=True, stop=True)
                    mm.then_inc(s["wt_ready"], 1)
                    pe.wait_ge(s["zv_taken"], 1)
                    for t, inst, d, e, at in each():
                        mm = nc.tensor.matmul(m.ps[:, 2 + t // 2, at], XT[:, t, inst, :], ZV[:, t, at.start // HD % 4, :], start=True, stop=True)
                    mm.then_inc(s["u0_ready"], 1)

                    def outputs(t, d):
                        for hh in range(2):
                            inst = hh * 2 + d
                            e = slice(hh * HD, (hh + 1) * HD)
                            into = m.ps[e, 6 + d, t * P:(t + 1) * P]
                            nc.tensor.matmul(into, U[:, t, d, e], M[:, t, inst, 1, :], start=True, stop=False)
                            mm = nc.tensor.matmul(into, tok[:, d, t, 2, e], M[:, t, inst, 3, :], start=False, stop=True)
                        mm.then_inc(s["out_ready"], 1)

                    pe.wait_ge(s["cleared"], 1)
                    pe.wait_ge(s["wt_taken"], 1)
                    pe.wait_ge(s["kv_taken"], 4)
                    for n in range(2 * NT):
                        t, u = n // 2, n % 2
                        on = slice(u * RW_CHUNK, (u + 1) * RW_CHUNK)
                        for d in range(2):
                            if n >= 1:
                                pe.wait_ge(s["state_ready"][d], n)
                            nc.tensor.matmul(m.ps[on, d, 0:P], WT[:, t, d, on], state[:, d, :], start=True, stop=True).then_inc(s["from_state"][d], 1)
                            nc.tensor.matmul(m.ps[:, 4 + d, n * RW_CHUNK:(n + 1) * RW_CHUNK], state[:, d, :], AR[:, d, t, 1, on], start=True, stop=True)
                        for d in range(2):
                            pe.wait_ge(s["u_ready"][d], n + 1)
                            for hh in range(2):
                                e = slice(hh * HD, (hh + 1) * HD)
                                mm = nc.tensor.matmul(m.ps[:, 2 + d, e], b_own[on, d, t, hh, :], U[on, t, d, e], start=True, stop=True)
                            mm.then_inc(s["update_ready"][d], 1)
                        if n >= 2:
                            outputs(t - 1, u)
                    for d in range(2):
                        outputs(NT - 1, d)
                    pe.wait_ge(s["centred"], 1)
                    nc.tensor.matmul(m.ps[:, 0, :], m.head_ones, XT[:, 0, :, :].rearrange("p i n -> p (i n)"), start=True, stop=True).then_inc(s["sums"], 1)
                    pe.wait_ge(s["squared"], 1)
                    nc.tensor.matmul(m.ps[:, 1, :], m.head_ones, XT[:, 1, :, :].rearrange("p i n -> p (i n)"), start=True, stop=True).then_inc(s["sums"], 1)

                @block.vector
                def _(dve):
                    nc.vector.memset(state[:], 0.0).then_inc(s["cleared"], 1)
                    dve.wait_ge(s["v_summed"], 1)
                    nc.vector.tensor_copy(ZV.rearrange("p (a t) i e -> p a (t i e)", a=2), m.ps[:, 2:4, :]).then_inc(s["zv_taken"], 1)
                    dve.wait_ge(s["kv_ready"], 1)
                    for u in range(2):
                        for hh in range(2):
                            e = slice(hh * HD, (hh + 1) * HD)
                            ends = p_end[e, u, :, :].rearrange("p t d -> p (t d)").unsqueeze(2).broadcast_to([HD, 2 * NT, HD])
                            products = m.ps[e, 4 + 2 * u:6 + 2 * u, :].rearrange("p a (x n) -> p (a x) n", n=P)
                            nc.vector.tensor_tensor(KV[e, u, :, :, e].rearrange("p t d n -> p (t d) n"), products[:, :, e], ends, ALU.mult).then_inc(s["kv_taken"], 1)
                    dve.wait_ge(s["cleared"], 1)
                    dve.wait_ge(s["kv_taken"], 4)
                    dve.wait_ge(s["u0_taken"], 1)
                    for n in range(2 * NT):
                        t, u = n // 2, n % 2
                        on = slice(u * RW_CHUNK, (u + 1) * RW_CHUNK)
                        for d in range(2):
                            dve.wait_ge(s["from_state"][d], n + 1)
                            nc.vector.tensor_tensor(U[on, t, d, :], m.ps[on, d, 0:P], U0[on, t, 2 * d:2 * d + 2, :].rearrange("p i e -> p (i e)"),
                                                    ALU.add).then_inc(s["u_ready"][d], 1)
                        for d in range(2):
                            if n >= 1:
                                dve.wait_ge(s["state_ready"][d], n)
                            nc.vector.scalar_tensor_tensor(out=grown[:, d, :], in0=state[:, d, :], scalar=p_end[:, u, t, d:d + 1], in1=KV[:, u, t, d, :],
                                                           op0=ALU.mult, op1=ALU.add).then_inc(s["grown"][d], 1)
                        for d in range(2):
                            dve.wait_ge(s["update_ready"][d], n + 1)
                            dve.wait_ge(s["grown"][d], n + 1)
                            nc.vector.scalar_tensor_tensor(out=state[:, d, :], in0=m.ps[:, 2 + d, 0:P], scalar=p_end[:, u, t, d:d + 1], in1=grown[:, d, :],
                                                           op0=ALU.mult, op1=ALU.add).then_inc(s["state_ready"][d], 1)
                    done = [0]

                    def step(ins):
                        done[0] += 1
                        ins.then_inc(s["steps"], 1)
                        dve.wait_ge(s["steps"], done[0])

                    y, sq, fw, bw = (XT[:, k, :, :].rearrange("p i n -> p (i n)") for k in range(NT))
                    dve.wait_ge(s["inter_taken"], 2)
                    dve.wait_ge(s["out_ready"], 2 * NT)
                    step(nc.vector.tensor_tensor(fw, fw, m.ps[:, 6, :], ALU.add))
                    step(nc.vector.tensor_tensor(bw, bw, m.ps[:, 7, :], ALU.add))
                    step(nc.vector.tensor_tensor(y, fw, bw[:, ::-1], ALU.add))
                    dve.sem_inc(s["centred"], 1)
                    dve.wait_ge(s["sums"], 1)
                    step(nc.vector.scalar_tensor_tensor(out=y, in0=m.ps[:, 0, :], scalar=-1.0 / HD, in1=y, op0=ALU.mult, op1=ALU.add))
                    dve.sem_inc(s["centred"], 1)
                    dve.wait_ge(s["root_ready"], 1)
                    step(nc.vector.reciprocal(fw, fw))
                    step(nc.vector.tensor_tensor(y, y, fw, ALU.mult))
                    step(nc.vector.tensor_scalar(y, y, par[:, 3, :], par[:, 4, :], ALU.mult, ALU.add))
                    step(nc.vector.tensor_tensor(y, y, bonus[:], ALU.add))
                    step(nc.vector.tensor_tensor(tile_of(m.h, c), y, L[:, G_, :], ALU.mult))

                @block.scalar
                def _(act):
                    act.wait_ge(s["wt_ready"], 1)
                    nc.scalar.activation(WT[:, :, 0:2, :].rearrange("p (a t) d n -> p a t (d n)", a=2), m.ps[:, 0:2, :].rearrange("p a (t n) -> p a t n", t=2),
                                         ACT.Copy).then_inc(s["wt_taken"], 1)
                    act.wait_ge(s["u0_ready"], 1)
                    nc.scalar.activation(U0.rearrange("p (a t) i e -> p a (t i e)", a=2), m.ps[:, 2:4, :], ACT.Copy).then_inc(s["u0_taken"], 1)
                    y, sq, fw, bw = (XT[:, k, :, :].rearrange("p i n -> p (i n)") for k in range(NT))
                    act.wait_ge(s["out_ready"], 2 * NT)
                    nc.scalar.activation(fw, m.ps[:, 4, :], ACT.Copy).then_inc(s["inter_taken"], 1)
                    nc.scalar.activation(bw, m.ps[:, 5, :], ACT.Copy).then_inc(s["inter_taken"], 1)
                    act.wait_ge(s["centred"], 2)
                    nc.scalar.activation(sq, y, ACT.Square).then_inc(s["squared"], 1)
                    act.wait_ge(s["sums"], 2)
                    nc.scalar.activation(fw, m.ps[:, 1, :], ACT.Sqrt, scale=1.0 / HD, bias=gn_eps[:, 0:1]).then_inc(s["root_ready"], 1)


def second_block(nc, m, a):
    with ExitStack() as held:
        def sb(name, shape):
            return held.enter_context(nc.sbuf_tensor(f"second_{name}", shape, F32))

        vec = sb("vec", [P, V2_W])
        own = sb("own", [P, VR_W])
        assert VS_W <= VR_W
        token_gain = vec[:, V2["tok_g"]:V2["tok_g"] + DT]
        load(nc, "vec2_0", [(vec[:], a["vec2"][0]), (own[:, 0:VS_W], a["vec_swa"])])
        with ExitStack() as tmp:
            y = tmp.enter_context(nc.sbuf_tensor("swa2_y", [P, 12, S], F32))
            m.sin = tmp.enter_context(nc.sbuf_tensor("swa2_sin", [P, S], F32))
            m.cos = tmp.enter_context(nc.sbuf_tensor("swa2_cos", [P, S], F32))
            bands = tmp.enter_context(nc.sbuf_tensor("swa2_bands", [P, BANDS2_W], F32))
            load(nc, "bands2", [(bands[:], a["bands2"])])
            rope_table(nc, "rope2", m, a["positions2"])
            with product_memory(nc, m):
                linear(nc, "qkv", m, a["w_qkv"], 0, 12, DT, 4, first=norm_first(nc, m, m.x, token_gain), on_act=to_tiles(nc, m, y))
            for half in range(2):
                heads_norm_rope(nc, f"q2_{half}", m, y[:, 4 * half:4 * half + 4, :], own[:, VS["q_g"]:VS["q_g"] + 1])
            heads_norm_rope(nc, "k2", m, y[:, 8:10, :], own[:, VS["k_g"]:VS["k_g"] + 1])
            band_attention(nc, "swa2", m, y[:, 0:8, :], y[:, 8:10, :], y[:, 10:12, :], own[:, VS["sinks"]:VS["sinks"] + 16], bands, (-1, 0, 1), m.h)
        with product_memory(nc, m):
            linear(nc, "out2", m, a["w_o_swa"], 0, DT, DT, 4, first=split_first(nc, m, m.h[:]), on_dve=add_to_x(nc, m))
        conv_ffn(nc, m, a, vec, 0)

        load(nc, "vec2_1", [(vec[:], a["vec2"][1]), (own[:], a["vec_rwkv"])])
        norm(nc, "tok_norm1", m, m.x, token_gain, m.h)
        keep = [nc.dram_tensor(f"rwkv_keep{w}", (DT, P, S), F32).ap() for w in range(8)]
        rwkv_inputs(nc, m, a, own, keep)
        rwkv_heads(nc, m, a, own, keep)
        with product_memory(nc, m):
            linear(nc, "out3", m, a["w_o_rwkv"], 0, DT, DT, 4, first=split_first(nc, m, m.h[:]), on_dve=add_to_x(nc, m))
        conv_ffn(nc, m, a, vec, 1)


def lay_out_second(q):
    q = {k[:-2]: np.asarray(v) for k, v in q.items() if k.endswith("_2")}
    a = {}
    up = q["ffn_w_up"].reshape(DEPTH, D, 2, GT, P).transpose(0, 1, 3, 2, 4).reshape(DEPTH, D, 2 * FFN)

    def paired(v):
        return v.reshape(-1, 2, GT, P).transpose(0, 2, 1, 3).reshape(-1, 2 * FFN)

    def each(w, ks):
        return np.concatenate([weight_slots(w[l], ks) for l in range(w.shape[0])])

    a["w_ffn_up"] = each(up, DT)
    at = 0
    for n, tiles in enumerate(FFN_PARTS):
        a[f"w_ffn_down{n}"] = each(q["ffn_w_down"][:, at * P:(at + tiles) * P], tiles)
        at += tiles
    a["w_qkv"] = weight_slots(q["swa_w_qkv"][0], DT)
    a["w_o_swa"] = weight_slots(q["swa_w_o"][0], DT)
    for name in ("r", "k", "v"):
        a[f"w_{name}"] = weight_slots(q[f"rwkv_w_{name}"][0], DT)
    a["w_o_rwkv"] = weight_slots(q["rwkv_w_o"][0], DT)
    for name in ("w", "a"):
        a[f"w_{name}1"] = weight_slots(np.concatenate(list(q[f"rwkv_{name}1"][0]), 1), DT)
        a[f"w_{name}2"] = np.concatenate(list(q[f"rwkv_{name}2"][0]), 0)
    g1 = np.zeros((D, 2 * P), np.float32)
    g1[:, :q["rwkv_g1"].shape[2]] = q["rwkv_g1"][0]
    g2 = np.zeros((2 * P, D), np.float32)
    g2[:q["rwkv_g2"].shape[1]] = q["rwkv_g2"][0]
    a["w_g1"] = weight_slots(g1, DT)
    a["w_g2"] = weight_slots(g2, 2)
    vec = np.zeros((DEPTH, P, V2_W), np.float32)
    for l in range(DEPTH):
        for at, what in ((V2["tok_g"], q["norm_tok"][l]), (V2["ch_g"], q["norm_ch"][l]), (V2["conv_w"], paired(q["ffn_conv_w"][l])),
                         (V2["conv_b"], paired(q["ffn_conv_b"][l]))):
            c = as_columns(what)
            vec[l, :, at:at + c.shape[1]] = c
    a["vec2"] = vec
    swa = np.zeros((P, VS_W), np.float32)
    swa[:, VS["q_g"]:VS["q_g"] + 1] = both_heads(q["swa_q_gain"][0])
    swa[:, VS["k_g"]:VS["k_g"] + 1] = both_heads(q["swa_k_gain"][0])
    swa[:, VS["sinks"]:VS["sinks"] + 16] = everywhere(q["swa_sinks"][0])
    a["vec_swa"] = swa
    rwkv = np.zeros((P, VR_W), np.float32)
    for at, what in ((VR["mu"], q["rwkv_mu"][0]), (VR["w0"], q["rwkv_w0"][0]), (VR["a0"], q["rwkv_a0"][0]), (VR["k_k"], q["rwkv_k_k"][0]),
                     (VR["k_a"], q["rwkv_k_a"][0]), (VR["r_k"], q["rwkv_r_k"][0]), (VR["ln_w"], q["rwkv_lnx_w"][0]), (VR["ln_b"], q["rwkv_lnx_b"][0])):
        c = as_columns(what)
        rwkv[:, at:at + c.shape[1]] = c
    a["vec_rwkv"] = rwkv
    a["positions2"] = np.ascontiguousarray(np.broadcast_to(np.arange(S, dtype=np.int32), (P, S)))
    restart = np.ones((P, S), np.float32)
    restart[:, ::RW_CHUNK] = 0.0
    a["restart"] = restart
    return a


class Memory:
    pass


def build(nc, a, out_t):
    with ExitStack() as held:
        def sb(name, shape):
            return held.enter_context(nc.sbuf_tensor(name, shape, F32))

        m = Memory()
        m.count = 0
        m.x = sb("x", [P, DT, S])
        m.h = sb("h", [P, DT, S])
        m.sq = sb("sq", [P, DT, S])
        m.rstd = sb("rstd", [P, S])
        m.c = sb("c", [P, CONSTS_W])
        m.eps = sb("eps", [P, 1])
        m.one = sb("one", [P, 1])
        m.ps = held.enter_context(nc.psum_tensor("ps", [P, 8, S], F32))
        m.ident = m.c[:, CONSTS["ident"]:CONSTS["ident"] + P]
        m.ones = m.c[:, CONSTS["ones"]:CONSTS["ones"] + P]
        m.head_ones = m.c[:, CONSTS["head_ones"]:CONSTS["head_ones"] + P]
        m.rot = m.c[:, CONSTS["rot"]:CONSTS["rot"] + P]
        m.pick = m.c[:, CONSTS["pick"]:CONSTS["pick"] + 4 * P]
        m.pick_pair = m.c[:, CONSTS["pick_pair"]:CONSTS["pick_pair"] + 2 * P]

        with stage(nc, "start", "set") as (block, s):
            @block.vector
            def _(dve):
                nc.vector.memset(m.eps[:], EPS).then_inc(s["set"], 1)
                nc.vector.memset(m.one[:], 1.0).then_inc(s["set"], 1)
        load(nc, "start_load", [(m.x[:], a["x_t"]), (m.c[:], a["consts"])])
        first_block(nc, m, a)
        second_block(nc, m, a)
        with stage(nc, "end", "stored") as (block, s):
            @block.sync
            def _(sp):
                sp.dma_start(out_t, m.x[:]).then_inc(s["stored"], 16)
                sp.wait_ge(s["stored"], 16)


def feature_tiles(a):
    a = np.asarray(a)
    return np.ascontiguousarray(a.T.reshape(a.shape[1] // P, P, a.shape[0]).transpose(1, 0, 2))


def weight_slots(w, ks):
    w = np.asarray(w)
    k, n = w.shape
    w = w.reshape(k // (ks * P), ks, P, n // P, P).transpose(3, 0, 2, 1, 4)
    return np.ascontiguousarray(w).reshape(-1, P, ks * P)


def as_columns(v):
    v = np.asarray(v)
    return v.reshape(-1, P).T


def everywhere(v):
    v = np.asarray(v)
    return np.broadcast_to(v[None, :], (P, v.shape[0]))


def both_heads(v):
    v = np.asarray(v)
    return np.concatenate([v, v])[:, None]


def lay_out(q):
    a = dict(constants())
    a["x_t"] = feature_tiles(q["x"][0])
    a["p_t"] = np.stack([feature_tiles(q["p"][l, 0]) for l in range(DEPTH)])
    a["positions"] = np.ascontiguousarray(np.broadcast_to(np.asarray(q["positions"]), (P, S)))
    w_in = np.asarray(q["w_in"])
    b_in = np.asarray(q["b_in"])
    g0 = 4 * 256
    keep = np.r_[0:g0, g0 + 8:w_in.shape[2]]
    pad = np.zeros((DEPTH, D, P), np.float32)
    pad[:, :, 0:4] = w_in[:, :, g0:g0 + 4]
    pad[:, :, 32:36] = w_in[:, :, g0 + 4:g0 + 8]
    def each(w, ks):
        return np.concatenate([weight_slots(w[l], ks) for l in range(w.shape[0])])
    a["w_gates"] = each(pad, DT)
    a["w_in"] = each(w_in[:, :, keep], DT)
    a["w_out"] = each(np.asarray(q["w_out"]), DT)
    a["w_up"] = each(np.asarray(q["w_up"]), DT)
    w_down = np.asarray(q["w_down"]).reshape(DEPTH * 2, D_FF // 2, D)
    a["w_down"] = each(w_down, DT)
    a["w_gate"] = each(np.asarray(q["w_ple_gate"]), DT)
    a["w_ple"] = each(np.asarray(q["w_ple_proj"]), PLE // P)
    vec = np.zeros((DEPTH, P, V1_W), np.float32)
    for l in range(DEPTH):
        v = vec[l]
        for at, what in ((V1["in_g"], q["in_norm_g"][l]), (V1["b_in"], b_in[l][keep]), (V1["m_g"], q["mlstm_norm_g"][l]),
                         (V1["h_g"], q["hgrn_norm_g"][l]), (V1["conv_w"], q["mlstm_conv_w"][l]), (V1["conv_b"], q["mlstm_conv_b"][l]),
                         (V1["mlp_g"], q["mlp_norm_g"][l]), (V1["ple_g"], q["ple_norm_g"][l]), (V1["post_g"], q["ple_post_norm_g"][l]),
                         (V1["lb"], q["hgrn_lb_logits"])):
            c = as_columns(what)
            v[:, at:at + c.shape[1]] = c
        v[:, V1["q_g"]:V1["q_g"] + 1] = both_heads(q["swa_q_norm_g"][l])
        v[:, V1["k_g"]:V1["k_g"] + 1] = both_heads(q["swa_k_norm_g"][l])
        v[:, V1["sinks"]:V1["sinks"] + 8] = everywhere(q["swa_sinks"][l])
        v[0:4, V1["b_i"]] = b_in[l][g0:g0 + 4]
        v[32:36, V1["b_i"]] = b_in[l][g0 + 4:g0 + 8]
        v[32:36, V1["f_bias"]] = np.asarray(q["mlstm_f_bias"])[l]
        v[:, V1["is_first"]] = 1.0 if l == 0 else 0.0
    a["vec1"] = vec
    a.update(lay_out_second(q))
    return a


def kernel(**inputs):
    import concourse.bacc as _bacc
    from concourse.bass_utils import run_bass_kernel_spmd as _run

    nc = _bacc.Bacc("TRN2", target_bir_lowering=False, num_devices=1)
    arrays, args = {}, {}
    for name, value in lay_out(inputs).items():
        value = np.ascontiguousarray(value)
        arrays[f"in_{name}"] = value
        args[name] = nc.dram_tensor(f"in_{name}", value.shape, mybir.dt.from_np(value.dtype), kind="ExternalInput").ap()
    out_t = nc.dram_tensor("out_t", (P, DT, S), F32, kind="ExternalOutput").ap()
    build(nc, args, out_t)
    r = _run(nc, [arrays], core_ids=[0])
    got = np.asarray(r.results[0]["out_t"])
    return np.ascontiguousarray(got.transpose(1, 0, 2).reshape(D, S).T)[None]
```
